# Optimizing a Trainium2 kernel written in Bass

```python
import math
import jax, jax.numpy as jnp
from jax import lax
import numpy as np

D_MODEL = 1024
BATCH = 1
SEQ = 256
DEPTH = 2

GRID_W = 64
ROPE_THETA = 10000.0
NORM_EPS = 1e-6
Q_BLOCK = 128

GDN_HEADS = 4
GDN_DK = 128
GDN_DV = 128
GDN_CONV = 5
GDN_CHUNK = 64
DIFF_HEADS = 4
DIFF_DQK = 64
DIFF_DV = 2 * DIFF_DQK
GQA_HEADS = 8
GQA_KV = 2
GQA_DH = 64

N_BRANCH = 3
GDN_W = GDN_HEADS * GDN_DV
DIFF_W = DIFF_HEADS * DIFF_DV
GQA_W = GQA_HEADS * GQA_DH
GDN_QKV = GDN_HEADS * (2 * GDN_DK + GDN_DV)

IN_SIZES = (
    GDN_QKV,
    GDN_W,
    2 * GDN_HEADS,
    2 * GDN_HEADS,
    DIFF_HEADS * 2 * DIFF_DQK,
    DIFF_HEADS * 2 * DIFF_DQK,
    DIFF_W,
    GQA_HEADS * GQA_DH,
    GQA_KV * GQA_DH,
    GQA_KV * GQA_DH,
    N_BRANCH * D_MODEL,
)
IN_COLS = sum(IN_SIZES)

N_GROUPS = 4
EXPERTS_PER_GROUP = 8
N_EXPERTS = N_GROUPS * EXPERTS_PER_GROUP
TOPK = 2
EXPERT_FF = 512
MOE_BLOCK = 256

kernel_name = 'hybrid_gdn_diff_axialgqa_hiermoe_encoder'

def _rmsnorm(x, w):
    xf = x.astype(jnp.float32)
    y = xf * lax.rsqrt(jnp.mean(xf * xf, axis=-1, keepdims=True) + NORM_EPS)
    return (y * w.astype(jnp.float32)).astype(x.dtype)

def _l2norm(x):
    return x * lax.rsqrt(jnp.sum(x * x, axis=-1, keepdims=True) + NORM_EPS)

def _split_cols(p):
    idx = []
    acc = 0
    for s in IN_SIZES[:-1]:
        acc += s
        idx.append(acc)
    return jnp.split(p, idx, axis=-1)

def _rope_tables(pos, dim):
    inv = 1.0 / (ROPE_THETA ** (jnp.arange(0, dim, 2, dtype=jnp.float32) / dim))
    ang = pos.astype(jnp.float32)[:, None] * inv[None, :]
    ang = jnp.concatenate([ang, ang], axis=-1)
    return (jnp.cos(ang), jnp.sin(ang))

def _apply_rope(x, cos, sin):
    c = cos[:, None, :].astype(x.dtype)
    s = sin[:, None, :].astype(x.dtype)
    half = x.shape[-1] // 2
    rot = jnp.concatenate([-x[..., half:], x[..., :half]], axis=-1)
    return x * c + rot * s

def _axial_rope(x, cos_r, sin_r, cos_c, sin_c):
    half = x.shape[-1] // 2
    return jnp.concatenate([_apply_rope(x[..., :half], cos_r, sin_r),
                            _apply_rope(x[..., half:], cos_c, sin_c)], axis=-1)

def _to_qblocks(x):
    b, s = x.shape[:2]
    x = x.reshape((b, s // Q_BLOCK, Q_BLOCK) + x.shape[2:])
    return jnp.moveaxis(x, 1, 0)

def _from_qblocks(y):
    nb, b, qb = y.shape[:3]
    return jnp.moveaxis(y, 0, 1).reshape((b, nb * qb) + y.shape[3:])

def _short_conv(x, w):
    c = x.shape[-1]
    pad = GDN_CONV // 2
    return lax.conv_general_dilated(x, w[:, None, :].astype(x.dtype), window_strides=(1,),
                                    padding=[(pad, pad)], dimension_numbers=('NWC', 'WIO', 'NWC'),
                                    feature_group_count=c)

def _gated_delta_chunked(q, k, v, beta, g):
    bsz, nh, s, dk = q.shape
    dv = v.shape[-1]
    c = GDN_CHUNK
    n = s // c
    q = q.reshape(bsz, nh, n, c, dk) * (dk ** -0.5)
    k = k.reshape(bsz, nh, n, c, dk)
    v = v.reshape(bsz, nh, n, c, dv)
    beta = beta.reshape(bsz, nh, n, c)
    gc = jnp.cumsum(g.reshape(bsz, nh, n, c), axis=-1)
    idx = jnp.arange(c)
    incl = idx[:, None] >= idx[None, :]
    strict = idx[:, None] > idx[None, :]
    decay = jnp.exp(jnp.where(incl, gc[..., :, None] - gc[..., None, :], -jnp.inf))
    kb = k * beta[..., None]
    lmat = jnp.where(strict, jnp.einsum('bhnid,bhnjd->bhnij', kb, k) * decay, 0.0)
    tmat = lmat + jnp.eye(c, dtype=jnp.float32)
    rhs = jnp.concatenate([v * beta[..., None], kb * jnp.exp(gc)[..., None]], axis=-1)
    sol = lax.linalg.triangular_solve(tmat, rhs, left_side=True, lower=True, unit_diagonal=True)
    u, w = sol[..., :dv], sol[..., dv:]
    intra = jnp.einsum('bhnid,bhnjd->bhnij', q, k) * decay
    q_dec = q * jnp.exp(gc)[..., None]
    k_dec = k * jnp.exp(gc[..., -1:] - gc)[..., None]
    g_last = jnp.exp(gc[..., -1])
    xs = (jnp.moveaxis(u, 2, 0), jnp.moveaxis(w, 2, 0), jnp.moveaxis(intra, 2, 0),
          jnp.moveaxis(q_dec, 2, 0), jnp.moveaxis(k_dec, 2, 0), jnp.moveaxis(g_last, 2, 0))

    def step(state, inp):
        u_n, w_n, intra_n, qd_n, kd_n, gl_n = inp
        v_new = u_n - jnp.einsum('bhck,bhkv->bhcv', w_n, state)
        o_n = jnp.einsum('bhck,bhkv->bhcv', qd_n, state) + jnp.einsum('bhij,bhjv->bhiv', intra_n, v_new)
        state = state * gl_n[..., None, None] + jnp.einsum('bhck,bhcv->bhkv', kd_n, v_new)
        return state, o_n

    s0 = jnp.zeros((bsz, nh, dk, dv), jnp.float32)
    _, o = lax.scan(step, s0, xs)
    return jnp.moveaxis(o, 0, 2).reshape(bsz, nh, s, dv)

def _gdn_mixer(qkv, z, b_raw, a_raw, conv_w, a_log, dt_bias, norm_w):
    bsz, s, _ = qkv.shape
    qkv = jax.nn.silu(_short_conv(qkv, conv_w))
    q, k, v = jnp.split(qkv, [GDN_HEADS * GDN_DK, 2 * GDN_HEADS * GDN_DK], axis=-1)

    def heads(t, d):
        return jnp.transpose(t.reshape(bsz, s, GDN_HEADS, d).astype(jnp.float32), (0, 2, 1, 3))

    q = _l2norm(heads(q, GDN_DK))
    k = _l2norm(heads(k, GDN_DK))
    v = heads(v, GDN_DV)
    beta = jax.nn.sigmoid(b_raw.astype(jnp.float32)).reshape(bsz, s, 2, GDN_HEADS)
    g = -jnp.exp(a_log.astype(jnp.float32)) * jax.nn.softplus(
        a_raw.astype(jnp.float32).reshape(bsz, s, 2, GDN_HEADS) + dt_bias.astype(jnp.float32))
    beta = jnp.transpose(beta, (2, 0, 3, 1))
    g = jnp.transpose(g, (2, 0, 3, 1))
    o_fwd = _gated_delta_chunked(q, k, v, beta[0], g[0])
    fl = lambda t: jnp.flip(t, axis=2)
    o_bwd = fl(_gated_delta_chunked(fl(q), fl(k), fl(v), fl(beta[1]), fl(g[1])))
    o = jnp.transpose(o_fwd + o_bwd, (0, 2, 1, 3))
    o = _rmsnorm(o, norm_w) * jax.nn.silu(z.astype(jnp.float32).reshape(bsz, s, GDN_HEADS, GDN_DV))
    return o.reshape(bsz, s, GDN_W).astype(qkv.dtype)

def _diff_mixer(q, k, v, lam_vecs, norm_w, lambda_init, cos, sin):
    bsz, s, _ = q.shape
    q = _apply_rope(q.reshape(bsz, s, 2 * DIFF_HEADS, DIFF_DQK), cos, sin)
    q = q.reshape(bsz, s, DIFF_HEADS, 2, DIFF_DQK) * (DIFF_DQK ** -0.5)
    k = _apply_rope(k.reshape(bsz, s, 2 * DIFF_HEADS, DIFF_DQK), cos, sin)
    k = k.reshape(bsz, s, DIFF_HEADS, 2, DIFF_DQK)
    v = v.reshape(bsz, s, DIFF_HEADS, DIFF_DV)
    lv = lam_vecs.astype(jnp.float32)
    lam = jnp.exp(jnp.sum(lv[0] * lv[1])) - jnp.exp(jnp.sum(lv[2] * lv[3])) + lambda_init

    def block(qb):
        sc = jnp.einsum('bqhmd,bshmd->bhmqs', qb, k).astype(jnp.float32)
        p = jax.nn.softmax(sc, axis=-1)
        pd = (p[:, :, 0] - lam * p[:, :, 1]).astype(v.dtype)
        return jnp.einsum('bhqs,bshe->bqhe', pd, v)

    o = _from_qblocks(lax.map(block, _to_qblocks(q)))
    o = _rmsnorm(o, norm_w) * (1.0 - lambda_init)
    return o.reshape(bsz, s, DIFF_W)

def _gqa_mixer(q, k, v, qn_w, kn_w, cos_r, sin_r, cos_c, sin_c):
    bsz, s, _ = q.shape
    q = _rmsnorm(q.reshape(bsz, s, GQA_HEADS, GQA_DH), qn_w)
    k = _rmsnorm(k.reshape(bsz, s, GQA_KV, GQA_DH), kn_w)
    v = v.reshape(bsz, s, GQA_KV, GQA_DH)
    q = _axial_rope(q, cos_r, sin_r, cos_c, sin_c) * (GQA_DH ** -0.5)
    k = _axial_rope(k, cos_r, sin_r, cos_c, sin_c)
    q = q.reshape(bsz, s, GQA_KV, GQA_HEADS // GQA_KV, GQA_DH)

    def block(qb):
        sc = jnp.einsum('bqkgd,bskd->bkgqs', qb, k).astype(jnp.float32)
        p = jax.nn.softmax(sc, axis=-1).astype(v.dtype)
        return jnp.einsum('bkgqs,bskd->bqkgd', p, v)

    o = _from_qblocks(lax.map(block, _to_qblocks(q)))
    return o.reshape(bsz, s, GQA_W)

def _hier_moe(h, wg, bg, we, be, w1, w3, w2):
    bsz, s, d = h.shape
    t = bsz * s
    ht = h.reshape(t, d)
    gprob = jax.nn.softmax((ht @ wg).astype(jnp.float32) + bg.astype(jnp.float32), axis=-1)
    gp, gidx = lax.top_k(gprob, 1)
    elog = ((ht @ we).astype(jnp.float32) + be.astype(jnp.float32)).reshape(t, N_GROUPS, EXPERTS_PER_GROUP)
    elog = jnp.take_along_axis(elog, gidx[:, :, None], axis=1)[:, 0]
    ep, eidx = lax.top_k(jax.nn.softmax(elog, axis=-1), TOPK)
    ep = ep / jnp.sum(ep, axis=-1, keepdims=True)
    weights = (gp * ep).astype(h.dtype)
    expert_id = (gidx * EXPERTS_PER_GROUP + eidx).astype(jnp.int32)
    a = t * TOPK
    p_len = ((a + N_EXPERTS * (MOE_BLOCK - 1) + MOE_BLOCK - 1) // MOE_BLOCK) * MOE_BLOCK
    n_blocks = p_len // MOE_BLOCK
    flat_e = expert_id.reshape(-1)
    flat_w = weights.reshape(-1)
    flat_t = jnp.repeat(jnp.arange(t, dtype=jnp.int32), TOPK)
    order = jnp.argsort(flat_e)
    se = flat_e[order]
    counts = jnp.bincount(flat_e, length=N_EXPERTS).astype(jnp.int32)
    start = jnp.cumsum(counts) - counts
    pcounts = ((counts + MOE_BLOCK - 1) // MOE_BLOCK) * MOE_BLOCK
    pend = jnp.cumsum(pcounts)
    pstart = pend - pcounts
    dest = pstart[se] + (jnp.arange(a, dtype=jnp.int32) - start[se])
    tok_buf = jnp.full((p_len,), t, jnp.int32).at[dest].set(flat_t[order])
    w_buf = jnp.zeros((p_len,), h.dtype).at[dest].set(flat_w[order])
    blk_e = jnp.minimum(jnp.searchsorted(pend, jnp.arange(n_blocks, dtype=jnp.int32) * MOE_BLOCK, side='right'),
                        N_EXPERTS - 1)
    x_pad = jnp.concatenate([ht, jnp.zeros((1, d), h.dtype)], axis=0)
    xb = x_pad[tok_buf].reshape(n_blocks, MOE_BLOCK, d)

    def expert_block(args):
        xblk, e = args
        return (jax.nn.silu(xblk @ w1[e]) * (xblk @ w3[e])) @ w2[e]

    yb = lax.map(expert_block, (xb, blk_e)).reshape(p_len, d) * w_buf[:, None]
    out = jnp.zeros((t + 1, d), h.dtype).at[tok_buf].add(yb)[:t]
    return out.reshape(bsz, s, d)

def setup_inputs(seed: int = 0) -> dict:
    key = jax.random.key(seed)
    ks = jax.random.split(key, 32)
    f32 = jnp.float32
    nrm = lambda k, shape, scale: jax.random.normal(k, shape, f32) * scale
    gain = lambda k, shape: 1.0 + 0.02 * jax.random.normal(k, shape, f32)
    lo, hi = math.log(0.001), math.log(0.1)
    dt = jnp.exp(jax.random.uniform(ks[5], (DEPTH, 2, GDN_HEADS), f32) * (hi - lo) + lo)
    return {
        'x': jax.random.normal(ks[0], (BATCH, SEQ, D_MODEL), f32),
        'attn_norm_w': gain(ks[1], (DEPTH, D_MODEL)),
        'w_in': nrm(ks[2], (DEPTH, D_MODEL, IN_COLS), D_MODEL ** -0.5),
        'gdn_conv_w': nrm(ks[3], (DEPTH, GDN_CONV, GDN_QKV), GDN_CONV ** -0.5),
        'gdn_a_log': jnp.log(jax.random.uniform(ks[4], (DEPTH, 2, GDN_HEADS), f32, 1.0, 16.0)),
        'gdn_dt_bias': dt + jnp.log(-jnp.expm1(-dt)),
        'gdn_norm_w': gain(ks[6], (DEPTH, GDN_DV)),
        'diff_lambda': nrm(ks[7], (DEPTH, 4, DIFF_DQK), 0.1),
        'diff_norm_w': gain(ks[8], (DEPTH, DIFF_DV)),
        'gqa_q_norm_w': gain(ks[9], (DEPTH, GQA_DH)),
        'gqa_k_norm_w': gain(ks[10], (DEPTH, GQA_DH)),
        'w_branch_a': nrm(ks[11], (DEPTH, GDN_W, D_MODEL), GDN_W ** -0.5),
        'w_branch_b': nrm(ks[12], (DEPTH, DIFF_W, D_MODEL), DIFF_W ** -0.5),
        'w_branch_c': nrm(ks[13], (DEPTH, GQA_W, D_MODEL), GQA_W ** -0.5),
        'w_out': nrm(ks[14], (DEPTH, D_MODEL, D_MODEL), D_MODEL ** -0.5),
        'ffn_norm_w': gain(ks[15], (DEPTH, D_MODEL)),
        'router_group_w': nrm(ks[16], (DEPTH, D_MODEL, N_GROUPS), D_MODEL ** -0.5),
        'router_group_b': nrm(ks[17], (DEPTH, N_GROUPS), 0.01),
        'router_expert_w': nrm(ks[18], (DEPTH, D_MODEL, N_EXPERTS), D_MODEL ** -0.5),
        'router_expert_b': nrm(ks[19], (DEPTH, N_EXPERTS), 0.01),
        'expert_w_gate': nrm(ks[20], (DEPTH, N_EXPERTS, D_MODEL, EXPERT_FF), D_MODEL ** -0.5),
        'expert_w_up': nrm(ks[21], (DEPTH, N_EXPERTS, D_MODEL, EXPERT_FF), D_MODEL ** -0.5),
        'expert_w_down': nrm(ks[22], (DEPTH, N_EXPERTS, EXPERT_FF, D_MODEL), EXPERT_FF ** -0.5),
        'final_norm_w': gain(ks[23], (D_MODEL,)),
    }

def reference(x, attn_norm_w, w_in, gdn_conv_w, gdn_a_log, gdn_dt_bias, gdn_norm_w, diff_lambda,
              diff_norm_w, gqa_q_norm_w, gqa_k_norm_w, w_branch_a, w_branch_b, w_branch_c, w_out,
              ffn_norm_w, router_group_w, router_group_b, router_expert_w, router_expert_b,
              expert_w_gate, expert_w_up, expert_w_down, final_norm_w):
    bsz, s, _ = x.shape
    rows = s // GRID_W
    row = jnp.broadcast_to(jnp.arange(rows)[:, None], (rows, GRID_W)).reshape(s)
    col = jnp.broadcast_to(jnp.arange(GRID_W)[None, :], (rows, GRID_W)).reshape(s)
    cos1, sin1 = _rope_tables(jnp.arange(s), DIFF_DQK)
    cos_r, sin_r = _rope_tables(row, GQA_DH // 2)
    cos_c, sin_c = _rope_tables(col, GQA_DH // 2)
    for l in range(DEPTH):
        lambda_init = 0.8 - 0.6 * math.exp(-0.3 * l)
        h = _rmsnorm(x, attn_norm_w[l])
        (g_qkv, g_z, g_b, g_a, d_q, d_k, d_v, c_q, c_k, c_v, gate_raw) = _split_cols(h @ w_in[l])
        y_a = _gdn_mixer(g_qkv, g_z, g_b, g_a, gdn_conv_w[l], gdn_a_log[l], gdn_dt_bias[l], gdn_norm_w[l])
        y_b = _diff_mixer(d_q, d_k, d_v, diff_lambda[l], diff_norm_w[l], lambda_init, cos1, sin1)
        y_c = _gqa_mixer(c_q, c_k, c_v, gqa_q_norm_w[l], gqa_k_norm_w[l], cos_r, sin_r, cos_c, sin_c)
        gates = jax.nn.sigmoid(gate_raw.astype(jnp.float32)).astype(x.dtype).reshape(bsz, s, N_BRANCH, D_MODEL)
        merged = (gates[:, :, 0] * (y_a @ w_branch_a[l]) + gates[:, :, 1] * (y_b @ w_branch_b[l])
                  + gates[:, :, 2] * (y_c @ w_branch_c[l]))
        x = x + merged @ w_out[l]
        x = x + _hier_moe(_rmsnorm(x, ffn_norm_w[l]), router_group_w[l], router_group_b[l],
                          router_expert_w[l], router_expert_b[l], expert_w_gate[l], expert_w_up[l],
                          expert_w_down[l])
    return _rmsnorm(x, final_norm_w)


_drawn_inputs = setup_inputs


def setup_inputs(seed=0):
    import zlib

    import numpy as np

    out = dict(_drawn_inputs(seed))
    spreads = {}
    factors = {'gqa_q_norm_w': 6.479,
     'gqa_k_norm_w': 8.0,
     'router_group_b': 4.273,
     'router_expert_b': 3.296,
     'final_norm_w': 2.905}
    for name, (base, spread) in spreads.items():
        noise = np.random.default_rng([zlib.crc32(name.encode()), seed]).standard_normal(out[name].shape)
        drawn = base * np.exp(spread * noise) if base else spread * noise
        out[name] = __import__('jax').numpy.asarray(drawn.astype(out[name].dtype))
    for name, factor in factors.items():
        out[name] = (out[name] * factor).astype(out[name].dtype)
    return out
```

```python
import concourse.bass as bass
from concourse import mybir
from contextlib import ExitStack
import math

F32 = mybir.dt.float32
I32 = mybir.dt.int32
ALU = mybir.AluOpType
ACT = mybir.ActivationFunctionType
AX = mybir.AxisListType

P = 128
D_MODEL = 1024
SEQ = 256
NT = SEQ // P
KC = D_MODEL // P
EPS = 1e-6
HEADS = 4
DH = 128
TAPS = 5
N_EXPERTS = 32
N_GROUPS = 4
PER_GROUP = 8
FF = 512
CAP = 32
ROUNDS = SEQ // CAP
JOBS = 48
LEVELS = 7
SCALE = 64 ** -0.5

C_Q, C_Z, C_BA, C_DQ, C_DK, C_DV, C_CQ, C_CKV, C_GATE = 0, 1536, 2048, 2064, 2576, 3088, 3600, 4112, 4368

RING = 6
U_DQ, U_DK, U_DV, U_CQ, U_CKV, U_GQ, U_GK, U_GV, U_Z = range(9)
ORDER = (2, 1, 0)
U_GATE0, U_BRANCH, U_GATE1 = (9, 12, 15), (10, 13, 16), (11, 14, 17)
U_OUT = 18
N_FIXED = 20

K_IDENT, K_ONES, K_UF, K_UB, K_SF, K_SB = (128 * n for n in range(6))
K_LEVEL0 = 768
K_LEVEL = K_LEVEL0 + 2 * 128
K_COSD = K_LEVEL + 2 * LEVELS * 64
K_SIND, K_COSG, K_SING = K_COSD + 128, K_COSD + 256, K_COSD + 384
K_IOTA = K_COSD + 512
K_LAM = K_IOTA + SEQ
K_THR = K_LAM + 4
K_FOLD = K_THR + 8
K_HALF = K_FOLD + 64
K_INDEX = K_HALF + 8
K_ALL = K_INDEX + 1


def shape_constants():
    import numpy as np
    c = np.zeros((P, K_ALL), np.float32)
    r, j = np.arange(P)[:, None], np.arange(P)[None, :]
    c[:, K_IDENT:K_IDENT + P] = r == j
    c[:, K_ONES:K_ONES + P] = 1
    c[:, K_UF:K_UF + P] = r <= j
    c[:, K_UB:K_UB + P] = r >= j
    c[:, K_SF:K_SF + P] = r < j
    c[:, K_SB:K_SB + P] = r > j
    for n in range(LEVELS):
        s = 1 << n
        m = (r // (2 * s) == j // (2 * s)) & (r % (2 * s) >= s) & (j % (2 * s) < s)
        for d, mask in enumerate((m, m.T)):
            cols = (np.arange(P) >> n & 1) == d
            c[:, K_LEVEL + (d * LEVELS + n) * 64:K_LEVEL + (d * LEVELS + n + 1) * 64] = mask[:, cols]
            if n == 0:
                c[:, K_LEVEL0 + d * P:K_LEVEL0 + (d + 1) * P] = mask

    def rope(pos, dim):
        inv = np.float32(1.0) / np.power(np.float32(10000.0), np.arange(0, dim, 2, dtype=np.float32) / np.float32(dim))
        ang = pos.astype(np.float32)[:, None] * inv[None, :].astype(np.float32)
        cos, sin = np.cos(ang), np.sin(ang)
        return np.concatenate([cos, cos], 1), np.concatenate([-sin, sin], 1)

    pos = np.arange(SEQ)
    cd, sd = rope(pos, 64)
    cr, sr = rope(pos // 64, 32)
    cc, sc = rope(pos % 64, 32)
    for at, t in ((K_COSD, cd), (K_SIND, sd), (K_COSG, np.concatenate([cr, cc], 1)), (K_SING, np.concatenate([sr, sc], 1))):
        c[:, at:at + 128] = t.reshape(NT, P, 64).transpose(1, 0, 2).reshape(P, 128)
    c[:, K_IOTA:K_IOTA + SEQ] = np.arange(SEQ)
    for l in range(2):
        init = 0.8 - 0.6 * math.exp(-0.3 * l)
        c[:, K_LAM + 2 * l] = init
        c[:, K_LAM + 2 * l + 1] = 1.0 - init
    c[:, K_THR:K_THR + ROUNDS - 1] = CAP * np.arange(1, ROUNDS)
    c[:, K_THR + ROUNDS - 1] = 1e9
    m = np.arange(64)[None, :]
    c[:, K_FOLD:K_FOLD + 64] = (r % 32 == m % 32) & ((r >= 64) == (m >= 32))
    c[:, K_HALF:K_HALF + 8] = -0.5
    c[:, K_INDEX] = np.arange(P)
    return c


def encoder_trunk(nc, x, attn_norm_w, w_in, gdn_conv_w, gdn_a_log, gdn_dt_bias, gdn_norm_w, diff_lambda, diff_norm_w,
                  gqa_q_norm_w, gqa_k_norm_w, w_branch_a, w_branch_b, w_branch_c, w_out, ffn_norm_w, router_group_w,
                  router_group_b, router_expert_w, router_expert_b, expert_w_gate, expert_w_up, expert_w_down,
                  final_norm_w, consts, out):
    depth = w_in.shape[0]
    top = ExitStack()

    def sb(name, cols, dt=F32):
        return top.enter_context(nc.sbuf_tensor(name, [P, cols], dt))

    ring = sb("ring", RING * 4096)
    x_sb = sb("x_sb", NT * D_MODEL)
    hT = sb("hT", KC * SEQ)
    xn = sb("xn", NT * D_MODEL)
    cst = sb("cst", K_ALL)
    arena = sb("arena", 16160)
    par = sb("par", 1064)
    small = sb("small", 768)
    nbi = sb("nbi", N_EXPERTS, I32)
    ps = [top.enter_context(nc.psum_tensor(f"ps{i}", [P, 512], F32)) for i in range(8)]

    def view(t, at, *dims):
        n = math.prod(dims)
        v = t[:, at:at + n]
        if len(dims) == 1:
            return v
        names = "abcd"[:len(dims)]
        return v.rearrange(f"p ({' '.join(names)}) -> p {' '.join(names)}", **dict(zip(names, dims)))

    ident = cst[:, K_IDENT:K_IDENT + P]
    ones = cst[:, K_ONES:K_ONES + P]
    cum = [cst[:, K_UF:K_UF + P], cst[:, K_UB:K_UB + P]]
    strict = [cst[:, K_SF:K_SF + P], cst[:, K_SB:K_SB + P]]

    def level0(direction):
        return cst[:, K_LEVEL0 + direction * P:K_LEVEL0 + (direction + 1) * P]

    def level(direction, n):
        return cst[:, K_LEVEL + (direction * LEVELS + n) * 64:K_LEVEL + (direction * LEVELS + n + 1) * 64]

    X = view(x_sb, 0, NT, D_MODEL)
    HT = view(hT, 0, KC, SEQ)
    XN = view(xn, 0, NT, D_MODEL)

    p_at = [0]

    def param(*dims):
        v = view(par, p_at[0], *dims)
        p_at[0] += math.prod(dims)
        return v

    g_attn, g_ffn = param(KC), param(KC)
    convw = param(TAPS * 12)
    dt_bias, a_log = param(8), param(8)
    n_gdn, n_diff = param(1), param(1)
    lamv_flat = param(256)
    lamv = lamv_flat.rearrange("p (a b d) -> p a b d", a=2, b=2)
    qn_w, kn_w = param(64), param(64)
    rgw, rew = param(KC, N_GROUPS), param(KC, N_EXPERTS)
    rb = param(N_GROUPS + N_EXPERTS)
    wba = param(KC, 16)
    convrows = param(128)
    assert p_at[0] <= 1064

    s_at = [0]

    def tiny(*dims):
        v = view(small, s_at[0], *dims)
        s_at[0] += math.prod(dims)
        return v

    ss, rstd = tiny(NT), tiny(NT)
    beta, gg = tiny(2, NT, HEADS), tiny(2, NT, HEADS)
    sp_a, sp_b, sp_c = tiny(2, NT, HEADS), tiny(2, NT, HEADS), tiny(2, NT, HEADS)
    aexp = tiny(8)
    bar = tiny(NT, 16)
    gc, gtot, egc, kdec = tiny(16), tiny(16), tiny(16), tiny(16)
    lprod, lsum, lexp = tiny(2, 64), tiny(2), tiny(2)
    nlam, ndl = tiny(1), tiny(1)
    hss, hrs = tiny(16), tiny(16)
    qss, qrs = tiny(NT, HEADS), tiny(NT, HEADS)
    mx, nmx, rsum, rinv = tiny(2, 4), tiny(2, 4), tiny(2, 4), tiny(2, 4)
    rl = tiny(2, 2)
    yss, yrs = tiny(16), tiny(16)
    logit = tiny(NT, 36)
    gpad, gmax8 = tiny(NT, 8), tiny(NT, 8)
    gexp, gsum, gprob, ngm = tiny(NT, 4), tiny(NT), tiny(NT), tiny(NT)
    goh = tiny(NT, 8)
    emask, etop = tiny(NT, N_EXPERTS), tiny(NT, 8)
    e1, esum, w01 = tiny(NT), tiny(NT), tiny(NT, 2)
    idxf = tiny(NT, 8)
    assert s_at[0] <= 768, s_at[0]
    idx = top.enter_context(nc.sbuf_tensor("idx", [P, NT * 8], mybir.dt.uint32))
    idx3 = idx[:, :].rearrange("p (t k) -> p t k", t=NT)
    hot = view(arena, 4096, 6, NT, N_EXPERTS)
    assigned, weight, posn, hot0, hot1, hotw = (hot[:, n] for n in range(6))
    cnt, nbf = view(arena, 4480, N_EXPERTS), view(arena, 4512, N_EXPERTS)
    over = view(arena, 4544, N_EXPERTS, 8)
    jend, jstart = view(arena, 4800, N_EXPERTS), view(arena, 4832, N_EXPERTS)
    jf = view(arena, 4864, 2)
    jcmp = view(arena, 4868, 2, N_EXPERTS)
    jobtab = top.enter_context(nc.sbuf_tensor("jobtab", [P, 2 * JOBS], I32))[:, :].rearrange("p (a j) -> p a j", a=2)

    dqT, dkT = view(arena, 0, HEADS, SEQ), view(arena, 1024, HEADS, SEQ)
    dv = view(arena, 2048, NT, 512)
    cqT = view(arena, 3072, HEADS, SEQ)
    ckT = view(arena, 4096, 2, SEQ)
    cv = view(arena, 4608, NT, 128)
    squares, gqa_tmp = view(arena, 6912, 2, 512), view(arena, 7936, 512)
    rope_a, rope_b = view(arena, 4864, 2, 512), view(arena, 5888, 2, 512)
    probs = view(arena, 6912, 2, 2, NT, SEQ)
    probsT = view(arena, 5888, 2, 2, SEQ)
    gqn = view(arena, 4864, 2, 512)
    pad = view(arena, 8960, 2, HEADS, SEQ + 4)
    conv = view(arena, 11040, 2, HEADS, SEQ)
    conv_flat = view(arena, 11040, 2, HEADS * SEQ)
    qtok = view(arena, 13088, NT, HEADS, DH)
    ktok = view(arena, 14112, NT, HEADS, DH)
    vtok = view(arena, 15136, NT, HEADS, DH)
    QT, KT = view(arena, 8960, HEADS, SEQ), view(arena, 9984, HEADS, SEQ)
    yb, yc = view(xn, 0, NT, 512), view(xn, 1024, NT, 512)
    LT = view(arena, 0, 4, HEADS, P)
    INT = view(arena, 2048, 4, HEADS, P)
    DI = view(arena, 4096, 4, HEADS, P)
    DT = view(arena, 6144, 4, HEADS, P)
    E = view(arena, 11040, 4, HEADS, P)
    YM = view(arena, 11040, 4, HEADS, 64)
    kd = view(arena, 13088, 2, HEADS, DH)
    vn1, S1 = view(arena, 0, 2, HEADS, DH), view(arena, 1024, 2, HEADS, DH)
    R2 = view(arena, 4096, 2, HEADS, DH)
    vn2, qs = view(arena, 5120, 2, HEADS, DH), view(arena, 11040, 2, HEADS, DH)
    oa = view(arena, 12064, NT, HEADS, DH)
    yT = [view(arena, 1024 * n, HEADS, SEQ) for n in range(3)]
    zs = view(arena, 3072, NT, 512)
    sig = view(arena, 4096, 3, 512)
    part = view(arena, 5632, 2, 512)
    merged = view(arena, 13088, NT, D_MODEL)
    ysq = view(arena, 11040, NT, 512)
    sel = view(arena, 0, NT, CAP)
    selw = view(arena, 64, NT, 4, CAP)
    selwT = view(arena, 320, NT, P)
    xg = view(arena, 576, KC, CAP)
    gu = view(arena, 832, FF)
    sg = view(arena, 1344, 4, CAP)
    hid = view(arena, 1472, 4, CAP)
    ymoe = view(arena, 1600, D_MODEL)
    rows = view(arena, 2624, 256)
    junk = view(arena, 9000, NT, D_MODEL)
    fin = view(arena, 0, NT, D_MODEL)
    fw = view(arena, 2048, D_MODEL)

    def slot(u):
        return ring[:, (u % RING) * 4096:(u % RING + 1) * 4096]

    def unit8(u):
        return slot(u).rearrange("p (c n) -> p c n", c=8)

    def bcast(ap, shape):
        return ap.broadcast_to(shape)

    names = []

    def sem(name):
        s = top.enter_context(nc.semaphore(name))
        names.append(s)
        return s

    landed = [sem(f"unit_landed{n}") for n in range(RING)]
    used_at = {}
    m_land = [sem(f"expert_landed{n}") for n in range(RING)]

    def unit_landed(eng, u):
        eng.wait_ge(landed[u % RING], 16 * (u // RING + 1))

    def load_unit(sp, l, u):
        if u >= RING:
            sp.wait_ge(*used_at[u - RING])
        cols = {U_DQ: C_DQ, U_DK: C_DK, U_DV: C_DV, U_CQ: C_CQ, U_GQ: C_Q, U_GK: C_Q + 512, U_GV: C_Q + 1024, U_Z: C_Z}
        for k, b in enumerate(ORDER):
            cols[U_GATE0[k]] = C_GATE + b * D_MODEL
            cols[U_GATE1[k]] = C_GATE + b * D_MODEL + 512
        if u in U_BRANCH:
            w = (w_branch_a, w_branch_b, w_branch_c)[ORDER[U_BRANCH.index(u)]]
            src = w[bass.ds(l, 1)].rearrange("o (c p) n -> p (o c) n", p=P)
            dst = slot(u).rearrange("p (c n) -> p c n", c=4)
        elif u == U_CKV:
            src = w_in[bass.ds(l, 1), :, C_CKV:C_CKV + 256].rearrange("o (p c) n -> p (o c) n", c=KC)
            dst = unit8(u)[:, :, 0:256]
        elif u >= U_OUT:
            n = u - U_OUT
            src = w_out[bass.ds(l, 1), :, n * 512:(n + 1) * 512].rearrange("o (p c) n -> p (o c) n", c=KC)
            dst = unit8(u)
        else:
            src = w_in[bass.ds(l, 1), :, cols[u]:cols[u] + 512].rearrange("o (p c) n -> p (o c) n", c=KC)
            dst = unit8(u)
        sp.dma_start(dst, src).then_inc(landed[u % RING], 16)

    def load_expert(sp, l, e, n):
        if n % 3 < 2:
            w = (expert_w_gate, expert_w_up)[n % 3].rearrange("l e (p c) f -> (l e) p c f", c=KC)
            dst = slot(n).rearrange("p (o c f) -> p o c f", o=1, c=KC)
        else:
            w = expert_w_down.rearrange("l e (p c) d -> (l e) p c d", c=4)
            dst = slot(n).rearrange("p (o c d) -> p o c d", o=1, c=4)
        src = w[bass.ds(l * N_EXPERTS + e, 1)].rearrange("o p c f -> p o c f")
        sp.dma_start(dst, src).then_inc(m_land[n], 16)

    def chain(eng, s):
        count = [0]

        def link(ins):
            count[0] += 1
            ins.then_inc(s, 1)
            eng.wait_ge(s, count[0])
        return link

    def root_asker(v, asked, given):
        count = [0]

        def ask(ins):
            count[0] += 1
            ins.then_inc(asked, 1)

        def got():
            v.wait_ge(given, count[0])
        return ask, got

    def roots(pool, asked, given, args):
        for n, a in enumerate(args):
            pool.wait_ge(asked, n + 1)
            half = cst[:, K_HALF:K_HALF + math.prod(a.shape[1:])]
            if len(a.shape) == 3:
                half = half.rearrange("p (t h) -> p t h", t=a.shape[1])
            pool.tensor_tensor(a, a, half, ALU.pow).then_inc(given, 1)

    def norm_act(act, done):
        for t in range(NT):
            act.activation(junk[:, t], X[:, t], ACT.Square, accum_out=ss[:, t:t + 1]).then_inc(done, 1)

    def norm_dve(v, squares, root, xn_ready):
        ask, got = root
        v.wait_ge(squares, NT)
        ask(v.tensor_scalar(rstd, ss, 1.0 / D_MODEL, EPS, ALU.mult, ALU.add))
        got()
        for t in range(NT):
            v.tensor_scalar(XN[:, t], X[:, t], rstd[:, t:t + 1], None, ALU.mult).then_inc(xn_ready, 1)

    def transpose_pe(pe, src, ready, turned):
        pe.wait_ge(ready, NT)
        for c in range(KC):
            for t in range(NT):
                ins = pe.transpose(ps[c // 2][:, (c % 2) * SEQ + t * P:(c % 2) * SEQ + (t + 1) * P],
                                   src[:, t].rearrange("p (f c) -> p c f", c=KC)[:, c], ident)
            if c % 2:
                ins.then_inc(turned, 1)

    def scaled_act(act, turned, gain, done):
        for j in (0, 2):
            act.wait_ge(turned, j + 1)
            for c in (2 * j, 2 * j + 1):
                ins = act.activation(HT[:, c], ps[j][:, (c % 2) * SEQ:(c % 2 + 1) * SEQ], ACT.Copy,
                                     scale=1.0 if gain is None else gain[:, c:c + 1])
            ins.then_inc(done, 1)

    def scaled_dve(v, turned, gain, done):
        for j in (1, 3):
            v.wait_ge(turned, j + 1)
            for c in (2 * j, 2 * j + 1):
                src = ps[j][:, (c % 2) * SEQ:(c % 2 + 1) * SEQ]
                if gain is None:
                    ins = v.tensor_copy(HT[:, c], src)
                else:
                    ins = v.tensor_scalar(HT[:, c], src, gain[:, c:c + 1], None, ALU.mult)
            ins.then_inc(done, 1)

    s_in = top.enter_context(nc.semaphore("inputs_landed"))
    with nc.Block() as block:
        @block.sync
        def _(sp):
            sp.dma_start(X, x.rearrange("b (t p) d -> p (b t) d", p=P)).then_inc(s_in, 16)
            sp.dma_start(cst[:, :], consts).then_inc(s_in, 16)
            sp.wait_ge(s_in, 32)

    with nc.Fori(0, depth) as l:
        a_squares, a_asked, a_root, a_xn, a_turned, a_done = sem("a_squares"), sem("a_root_asked"), sem("a_root"), sem("a_xn"), sem("a_turned"), sem("a_done")
        a_par, a_conv, a_convt = sem("a_params"), sem("a_convrows"), sem("a_convT")
        with nc.Block() as block:
            @block.sync
            def _(sp):
                one = bass.ds(l, 1)
                loads = [
                    (g_attn, attn_norm_w[one].rearrange("o (p c) -> p (o c)", c=KC)),
                    (g_ffn, ffn_norm_w[one].rearrange("o (p c) -> p (o c)", c=KC)),
                    (convrows[0:60], gdn_conv_w[one].rearrange("o k (c p) -> (o k c) p", p=P)),
                    (dt_bias, gdn_dt_bias[one].rearrange("o d h -> o (d h)").broadcast_to([P, 8])),
                    (a_log, gdn_a_log[one].rearrange("o d h -> o (d h)").broadcast_to([P, 8])),
                    (n_gdn, gdn_norm_w[one].rearrange("o p -> p o")),
                    (n_diff, diff_norm_w[one].rearrange("o p -> p o")),
                    (lamv_flat, diff_lambda[one].rearrange("o k d -> o (k d)").broadcast_to([P, 256])),
                    (qn_w, gqa_q_norm_w[one].broadcast_to([P, 64])),
                    (kn_w, gqa_k_norm_w[one].broadcast_to([P, 64])),
                    (rgw, router_group_w[one].rearrange("o (p c) n -> p (o c) n", c=KC)),
                    (rew, router_expert_w[one].rearrange("o (p c) n -> p (o c) n", c=KC)),
                    (rb[:, 0:N_GROUPS], router_group_b[one].broadcast_to([P, N_GROUPS])),
                    (rb[:, N_GROUPS:], router_expert_b[one].broadcast_to([P, N_EXPERTS])),
                    (wba, w_in[one, :, C_BA:C_BA + 16].rearrange("o (p c) n -> p (o c) n", c=KC)),
                ]
                for dst, src in loads:
                    sp.dma_start(dst, src).then_inc(a_par, 16)
                for u in range(RING):
                    load_unit(sp, l, u)
                sp.wait_ge(a_par, 16 * len(loads))

            @block.scalar
            def _(act):
                norm_act(act, a_squares)
                act.wait_ge(a_par, 16 * 15)
                scaled_act(act, a_turned, g_attn, a_done)

            @block.vector
            def _(v):
                norm_dve(v, a_squares, root_asker(v, a_asked, a_root), a_xn)
                v.wait_ge(a_par, 16 * 15)
                scaled_dve(v, a_turned, g_attn, a_done)
                v.wait_ge(a_convt, 1)
                v.tensor_copy(convw, ps[4][:, 0:60])

            @block.gpsimd
            def _(pool):
                roots(pool, a_asked, a_root, [rstd])

            @block.tensor
            def _(pe):
                transpose_pe(pe, XN, a_xn, a_turned)
                pe.wait_ge(a_par, 16 * 15)
                pe.transpose(ps[4][:, 0:60], convrows[0:60], ident[0:60, 0:60]).then_inc(a_convt, 1)

        b_proj, b_free, b_rope, b_turned, b_out = sem("b_proj"), sem("b_free"), sem("b_rope"), sem("b_turned"), sem("b_out")
        b_chain, b_sq, b_ba, b_dvc, b_asked, b_root = sem("b_chain"), sem("b_squares"), sem("b_ba"), sem("b_dv_copied"), sem("b_root_asked"), sem("b_root")
        items = [(u, t) for u in (U_DQ, U_DK, U_DV, U_CQ, U_CKV) for t in range(NT)]
        roped = [i for i, (u, t) in enumerate(items) if u != U_DV]
        width = {U_CKV: 256}
        used_at.update({u: (b_proj, NT * (n + 1)) for n, u in enumerate((U_DQ, U_DK, U_DV, U_CQ, U_CKV))})
        with nc.Block() as block:
            @block.sync
            def _(sp):
                for u in range(RING, RING + 5):
                    load_unit(sp, l, u)

            @block.tensor
            def _(pe):
                def heads(i):
                    n = roped.index(i)
                    u, t = items[i]
                    pe.wait_ge(b_rope, n + 1)
                    if n >= 2:
                        pe.wait_ge(b_out, n - 1)
                    for j in range(2 if u == U_CKV else HEADS):
                        ins = pe.transpose(ps[4 + n % 2][:, j * P:(j + 1) * P],
                                           rope_b[:, n % 2, j * P:(j + 1) * P], ident)
                    ins.then_inc(b_turned, 1)

                for i, (u, t) in enumerate(items):
                    if t == 0:
                        unit_landed(pe, u)
                    if i >= 4:
                        pe.wait_ge(b_free, i - 3)
                    n = width.get(u, 512)
                    for c in range(KC):
                        ins = pe.matmul(ps[i % 4][:, 0:n], HT[:, c, t * P:(t + 1) * P], unit8(u)[:, c, 0:n],
                                        start=(c == 0), stop=(c == KC - 1))
                    ins.then_inc(b_proj, 1)
                    if i == 0:
                        for tt in range(NT):
                            for c in range(KC):
                                ins2 = pe.matmul(ps[6][:, tt * 16:(tt + 1) * 16], HT[:, c, tt * P:(tt + 1) * P], wba[:, c],
                                                 start=(c == 0), stop=(c == KC - 1))
                        ins2.then_inc(b_ba, 1)
                    if i - 1 in roped:
                        heads(i - 1)
                heads(len(items) - 1)

            @block.scalar
            def _(act):
                def heads_out(i):
                    n = roped.index(i)
                    u, t = items[i]
                    dst = {U_DQ: dqT, U_DK: dkT, U_CQ: cqT, U_CKV: ckT}[u]
                    nh = 2 if u == U_CKV else HEADS
                    act.wait_ge(b_turned, n + 1)
                    act.activation(dst[:, :, t * P:(t + 1) * P],
                                   ps[4 + n % 2][:, 0:nh * P].rearrange("p (j q) -> p j q", j=nh), ACT.Copy).then_inc(b_out, 1)

                for i, (u, t) in enumerate(items):
                    if u in (U_CQ, U_CKV):
                        act.wait_ge(b_proj, i + 1)
                        n = 512 if u == U_CQ else 128
                        m = i - items.index((U_CQ, 0))
                        if m >= 2:
                            act.wait_ge(b_rope, roped.index(i) - 1)
                        act.activation(squares[:, m % 2, 0:n], ps[i % 4][:, 0:n], ACT.Square).then_inc(b_sq, 1)
                    if u == U_DV:
                        act.wait_ge(b_proj, i + 1)
                        act.activation(dv[:, t], ps[i % 4][:, :], ACT.Copy).then_inc(b_dvc, 1)
                    if i - 1 in roped and i >= 1:
                        heads_out(i - 1)
                heads_out(len(items) - 1)

            @block.vector
            def _(v):
                link = chain(v, b_chain)
                ask, got = root_asker(v, b_asked, b_root)
                n_sq = 0
                for i, (u, t) in enumerate(items):
                    src = ps[i % 4]
                    v.wait_ge(b_proj, i + 1)
                    if u == U_DV:
                        v.wait_ge(b_dvc, t + 1)
                        v.sem_inc(b_free, 1)
                        continue
                    n = roped.index(i)
                    if n >= 2:
                        v.wait_ge(b_turned, n - 1)
                    ra, rb_ = rope_a[:, n % 2], rope_b[:, n % 2]
                    if u in (U_DQ, U_DK):
                        cos = cst[:, K_COSD + t * 64:K_COSD + (t + 1) * 64]
                        sin = cst[:, K_SIND + t * 64:K_SIND + (t + 1) * 64]
                        s4 = src[:, :].rearrange("p (h a d) -> p h a d", a=2, d=32)
                        r4 = rb_.rearrange("p (h a d) -> p h a d", a=2, d=32)
                        for a in range(2):
                            v.tensor_tensor(r4[:, :, a], s4[:, :, 1 - a],
                                            bcast(sin[:, a * 32:(a + 1) * 32].unsqueeze(1), [P, 8, 32]), ALU.mult)
                        v.tensor_tensor(ra.rearrange("p (h d) -> p h d", d=64), src[:, :].rearrange("p (h d) -> p h d", d=64),
                                        bcast(cos.unsqueeze(1), [P, 8, 64]), ALU.mult).then_inc(b_free, 1)
                        v.wait_ge(b_free, i + 1)
                        v.tensor_tensor(rb_, rb_, ra, ALU.add).then_inc(b_rope, 1)
                    else:
                        nh = 8 if u == U_CQ else 2
                        w = qn_w if u == U_CQ else kn_w
                        cos = cst[:, K_COSG + t * 64:K_COSG + (t + 1) * 64]
                        sin = cst[:, K_SING + t * 64:K_SING + (t + 1) * 64]
                        n_sq += 1
                        qw = gqn[:, n % 2, 0:nh * 64]
                        v.wait_ge(b_sq, n_sq)
                        v.tensor_tensor(qw.rearrange("p (h d) -> p h d", d=64), src[:, 0:nh * 64].rearrange("p (h d) -> p h d", d=64),
                                        bcast(w.unsqueeze(1), [P, nh, 64]), ALU.mult)
                        if u == U_CKV:
                            v.tensor_copy(cv[:, t], src[:, 128:256])
                        link(v.tensor_reduce(hss[:, 0:nh], squares[:, (n_sq - 1) % 2, 0:nh * 64].rearrange("p (h d) -> p h d", d=64), AX.X, ALU.add))
                        v.sem_inc(b_free, 1)
                        ask(v.tensor_scalar(hrs[:, 0:nh], hss[:, 0:nh], 1.0 / 64, EPS, ALU.mult, ALU.add))
                        tmp = gqa_tmp[:, 0:nh * 64]
                        sin4 = sin.rearrange("p (g a d) -> p g a d", a=2, d=16)
                        for a in range(2):
                            for g in range(2):
                                ins = v.tensor_tensor(tmp.rearrange("p (h g a d) -> p h g a d", g=2, a=2, d=16)[:, :, g, a],
                                                qw.rearrange("p (h g a d) -> p h g a d", g=2, a=2, d=16)[:, :, g, 1 - a],
                                                bcast(sin4[:, g, a].unsqueeze(1), [P, nh, 16]), ALU.mult)
                        link(ins)
                        link(v.tensor_tensor(qw.rearrange("p (h d) -> p h d", d=64), qw.rearrange("p (h d) -> p h d", d=64),
                                             bcast(cos.unsqueeze(1), [P, nh, 64]), ALU.mult))
                        link(v.tensor_tensor(tmp, tmp, qw, ALU.add))
                        got()
                        if u == U_CQ:
                            v.tensor_tensor(rb_.rearrange("p (h d) -> p h d", d=64), tmp.rearrange("p (h d) -> p h d", d=64),
                                            bcast(hrs[:, 0:8].unsqueeze(2), [P, 8, 64]), ALU.mult).then_inc(b_rope, 1)
                        else:
                            for a in range(2):
                                ins = v.tensor_tensor(rb_[:, 0:256].rearrange("p (h a d) -> p h a d", a=2, d=64)[:, :, a],
                                                      tmp.rearrange("p (h d) -> p h d", d=64),
                                                      bcast(hrs[:, 0:2].unsqueeze(2), [P, 2, 64]), ALU.mult)
                            ins.then_inc(b_rope, 1)
                v.wait_ge(b_ba, 1)
                v.tensor_copy(bar, ps[6][:, 0:32].rearrange("p (t n) -> p t n", t=NT))

            @block.gpsimd
            def _(pool):
                roots(pool, b_asked, b_root, [hrs[:, 0:8], hrs[:, 0:8], hrs[:, 0:2], hrs[:, 0:2]])

        c_score, c_max, c_exp, c_prob = sem("c_scores"), sem("c_max"), sem("c_exp"), sem("c_probs")
        c_turned, c_pT, c_pv, c_y, c_chain, c_achain = (sem("c_" + n) for n in ("turned", "probsT", "pv", "y", "chain", "act_chain"))
        d_fill, d_empty, d_conv, d_silu, d_sq, d_norm, d_zero = (sem("d_" + n) for n in ("fill", "empty", "conv", "silu", "squares", "norm", "zero"))
        d_asked, d_root = sem("d_root_asked"), sem("d_root")
        g_dve, g_act = sem("g_dve"), sem("g_act")
        STEPS = 8
        first_fill = [s if s < 4 else 4 + 2 * (s - 4) for s in range(STEPS + 1)]
        fills = [("proj", 0), ("proj", 1), ("tok", 0), ("proj", 2), ("tok", 1), ("back", 0), ("tok", 2), ("back", 1)]
        fills_at = {k: 2 * n for n, k in enumerate(fills)}
        pieces = [[fills[0]], [fills[1]], [fills[2]], [fills[3]], [fills[4], fills[5]], [fills[6]], [fills[7]], []]
        tok = (qtok, ktok, vtok)
        used_at.update({U_GQ + g: (d_fill, fills_at["proj", g] + 2) for g in range(3)})
        with nc.Block() as block:
            @block.sync
            def _(sp):
                for u in range(RING + 5, RING + 8):
                    load_unit(sp, l, u)

            @block.tensor
            def _(pe):
                def scores(s):
                    if s >= 2:
                        pe.wait_ge(c_exp, s - 1)
                    for m in range(2):
                        half = slice(64 * m, 64 * m + 64)
                        q, k = (dqT[half, s], dkT[half, s]) if s < 4 else (cqT[half, s - 4], ckT[half, (s - 4) // 2])
                        for t in range(NT):
                            ins = pe.matmul(ps[2 * (s % 2) + m][:, t * SEQ:(t + 1) * SEQ], q[:, t * P:(t + 1) * P], k,
                                            start=True, stop=True)
                    ins.then_inc(c_score, 1)

                def turn(s, m, f):
                    pe.wait_ge(c_prob, s + 1)
                    if f:
                        pe.wait_ge(c_pT, f)
                    for t in range(NT):
                        for kt in range(NT):
                            ins = pe.transpose(ps[4][:, kt * SEQ + t * P:kt * SEQ + (t + 1) * P],
                                               probs[:, s % 2, m, t, kt * P:(kt + 1) * P], ident)
                    ins.then_inc(c_turned, 1)

                def weighted(s, m, f):
                    pe.wait_ge(c_pT, f + 1)
                    if s:
                        pe.wait_ge(c_y, s)
                    for t in range(NT):
                        for kt in range(NT):
                            if s < 4:
                                o, val = ps[5][:, t * P:(t + 1) * P], dv[:, kt, s * P:(s + 1) * P]
                            else:
                                kv = (s - 4) // 2
                                o, val = ps[5][:, (2 * t + m) * 64:(2 * t + m + 1) * 64], cv[:, kt, kv * 64:(kv + 1) * 64]
                            ins = pe.matmul(o, probsT[:, f % 2, kt, t * P:(t + 1) * P], val, start=(kt == 0), stop=(kt == NT - 1))
                    ins.then_inc(c_pv, 1)

                def fill(kind, g):
                    for w in range(2):
                        f = fills_at[kind, g] + w
                        bank = ps[6 + f % 2]
                        if f >= 2:
                            pe.wait_ge(d_empty, f - 1)
                        if kind == "proj":
                            if w == 0:
                                unit_landed(pe, U_GQ + g)
                            for h in (2 * w, 2 * w + 1):
                                for c in range(KC):
                                    ins = pe.matmul(bank[:, (h % 2) * SEQ:(h % 2 + 1) * SEQ],
                                                    unit8(U_GQ + g)[:, c, h * DH:(h + 1) * DH], HT[:, c],
                                                    start=(c == 0), stop=(c == KC - 1))
                        elif kind == "tok":
                            pe.wait_ge(d_silu, g + 1)
                            for h in range(HEADS):
                                ins = pe.transpose(bank[:, h * DH:(h + 1) * DH], conv[:, g % 2, h, w * P:(w + 1) * P], ident)
                        else:
                            pe.wait_ge(d_norm, g + 1)
                            for h in range(HEADS):
                                ins = pe.transpose(bank[:, h * P:(h + 1) * P], tok[g][:, w, h], ident)
                        ins.then_inc(d_fill, 1)

                scores(0)
                scores(1)
                for s in range(STEPS):
                    for kind, g in pieces[s]:
                        fill(kind, g)
                    for m in range(1 if s < 4 else 2):
                        f = first_fill[s] + m
                        turn(s, m, f)
                        if m == 0 and s + 2 < STEPS:
                            scores(s + 2)
                        weighted(s, m, f)

            @block.scalar
            def _(act):
                alink = chain(act, c_achain)
                act.activation(beta.rearrange("p d t h -> p t d h"), bar[:, :, 0:8].rearrange("p t (d h) -> p t d h", d=2),
                               ACT.Sigmoid)
                act.activation(aexp, a_log, ACT.Exp).then_inc(g_act, 1)
                act.wait_ge(g_dve, 1)
                act.activation(lexp, lsum, ACT.Exp)
                act.activation(sp_b, sp_b, ACT.Exp, scale=-1.0).then_inc(g_act, 1)
                act.wait_ge(g_dve, 2)
                act.activation(sp_b, sp_b, ACT.Ln).then_inc(g_act, 1)

                def exps(s):
                    act.wait_ge(c_max, s + 1)
                    if s >= 2:
                        act.wait_ge(c_turned, first_fill[s - 1])
                    for m in range(2):
                        for t in range(NT):
                            ins = act.activation(probs[:, s % 2, m, t], ps[2 * (s % 2) + m][:, t * SEQ:(t + 1) * SEQ], ACT.Exp,
                                                 bias=nmx[:, s % 2, 2 * m + t:2 * m + t + 1], scale=SCALE,
                                                 accum_out=rsum[:, s % 2, 2 * m + t:2 * m + t + 1])
                    ins.then_inc(c_exp, 1)

                def empty(kind, g):
                    for w in range(2):
                        f = fills_at[kind, g] + w
                        act.wait_ge(d_fill, f + 1)
                        bank = ps[6 + f % 2]
                        if kind == "proj":
                            if g == 2 and w == 0:
                                act.wait_ge(d_conv, 1)
                            dst, src = pad[:, g % 2, 2 * w:2 * w + 2, 2:2 + SEQ], bank[:, :].rearrange("p (h t) -> p h t", h=2)
                        elif kind == "tok":
                            dst, src = tok[g][:, w], bank[:, :].rearrange("p (h d) -> p h d", h=HEADS)
                        else:
                            if g == 0 and w == 0:
                                act.wait_ge(d_conv, 3)
                            dst, src = (QT, KT)[g][:, :, w * P:(w + 1) * P], bank[:, :].rearrange("p (h t) -> p h t", h=HEADS)
                        act.activation(dst, src, ACT.Copy).then_inc(d_empty, 1)

                def silu(g):
                    act.wait_ge(d_conv, g + 1)
                    act.activation(conv[:, g % 2], conv[:, g % 2], ACT.Silu).then_inc(d_silu, 1)

                def square(g):
                    act.wait_ge(d_empty, fills_at["tok", g] + 2)
                    act.activation(conv_flat[:, g % 2], tok[g].rearrange("p t h d -> p (t h d)"),
                                   ACT.Square).then_inc(d_sq, 1)

                exps(0)
                for s in range(STEPS):
                    if s + 1 < STEPS:
                        exps(s + 1)
                    if s == 5:
                        silu(2)
                    for kind, g in pieces[s]:
                        empty(kind, g)
                        if (kind, g) in (("tok", 0), ("tok", 1)):
                            square(g)
                    if s in (1, 3):
                        silu(s // 2)
                    for m in range(1 if s < 4 else 2):
                        f = first_fill[s] + m
                        act.wait_ge(c_turned, f + 1)
                        if f >= 2:
                            act.wait_ge(c_pv, f - 1)
                        act.activation(probsT[:, f % 2].rearrange("p k q -> p (k q)"), ps[4][:, :], ACT.Copy).then_inc(c_pT, 1)

            @block.vector
            def _(v):
                link = chain(v, c_chain)
                ask, got = root_asker(v, d_asked, d_root)
                for b in range(2):
                    v.memset(pad[:, b, :, 0:2], 0.0)
                    v.memset(pad[:, b, :, SEQ + 2:SEQ + 4], 0.0)
                link(v.tensor_tensor(lprod, lamv[:, :, 0], lamv[:, :, 1], ALU.mult))
                v.tensor_reduce(lsum, lprod, AX.X, ALU.add)
                link(v.tensor_tensor(sp_a.rearrange("p d t h -> p t d h"), bar[:, :, 8:16].rearrange("p t (d h) -> p t d h", d=2),
                                     bcast(dt_bias.rearrange("p (d h) -> p d h", d=2).unsqueeze(1), [P, NT, 2, HEADS]), ALU.add))
                v.scalar_tensor_tensor(sp_b, sp_a, -1.0, sp_a, ALU.mult, ALU.max).then_inc(g_dve, 1)

                def maxima(s):
                    v.wait_ge(c_score, s + 1)
                    for m in range(2):
                        ins = v.tensor_reduce(mx[:, s % 2, 2 * m:2 * m + 2],
                                              ps[2 * (s % 2) + m][:, :].rearrange("p (t k) -> p t k", t=NT), AX.X, ALU.max)
                    link(ins)
                    v.tensor_scalar(nmx[:, s % 2], mx[:, s % 2], -SCALE, None, ALU.mult).then_inc(c_max, 1)

                maxima(0)
                maxima(1)
                v.wait_ge(g_act, 2)
                link(v.tensor_scalar(sp_b, sp_b, 1.0, None, ALU.add))
                v.sem_inc(g_dve, 1)
                link(v.tensor_tensor(nlam, lexp[:, 1:2], lexp[:, 0:1], ALU.subtract))
                link(v.tensor_tensor(nlam, nlam, cst[:, bass.ds(l * 2 + K_LAM, 1)], ALU.subtract))
                v.wait_ge(g_act, 3)
                link(v.scalar_tensor_tensor(sp_a, sp_a, 0.0, sp_b, ALU.max, ALU.add))
                for t in range(NT):
                    ins = v.tensor_tensor(gg[:, :, t], sp_a[:, :, t], aexp.rearrange("p (d h) -> p d h", d=2), ALU.mult)
                link(ins)
                v.tensor_scalar(gg, gg, -1.0, None, ALU.mult)

                def convolve(g):
                    v.wait_ge(d_empty, fills_at["proj", g] + 2)
                    if g == 2:
                        v.wait_ge(d_fill, fills_at["tok", 0] + 2)
                    for k in range(TAPS):
                        for h in range(HEADS):
                            w = convw[:, k * 12 + g * HEADS + h:k * 12 + g * HEADS + h + 1]
                            src = pad[:, g % 2, h, k:k + SEQ]
                            if k == 0:
                                ins = v.tensor_scalar(conv[:, g % 2, h], src, w, None, ALU.mult)
                            else:
                                ins = v.scalar_tensor_tensor(conv[:, g % 2, h], src, w, conv[:, g % 2, h], ALU.mult, ALU.add)
                        if k < TAPS - 1:
                            link(ins)
                    ins.then_inc(d_conv, 1)

                def l2norm(g):
                    v.wait_ge(d_sq, g + 1)
                    link(v.tensor_reduce(qss, conv_flat[:, g % 2].rearrange("p (t h d) -> p t h d", t=NT, h=HEADS), AX.X, ALU.add))
                    ask(v.tensor_scalar(qrs, qss, EPS, None, ALU.add))
                    got()
                    if g == 0:
                        link(v.tensor_scalar(qrs, qrs, DH ** -0.5, None, ALU.mult))
                    v.tensor_tensor(tok[g], tok[g], bcast(qrs.unsqueeze(3), [P, NT, HEADS, DH]), ALU.mult).then_inc(d_norm, 1)

                work = {0: lambda: convolve(0), 1: lambda: convolve(1), 2: lambda: l2norm(0), 3: lambda: convolve(2), 4: lambda: l2norm(1)}
                for s in range(STEPS):
                    b = s % 2
                    v.wait_ge(c_exp, s + 1)
                    if s < 4:
                        link(v.reciprocal(rinv[:, b], rsum[:, b]))
                        link(v.tensor_scalar(rl[:, b], rinv[:, b, 2:4], nlam, None, ALU.mult))
                        for t in range(NT):
                            ins = v.tensor_scalar(probs[:, b, 1, t], probs[:, b, 1, t], rl[:, b, t:t + 1], None, ALU.mult)
                        link(ins)
                        for t in range(NT):
                            ins = v.scalar_tensor_tensor(probs[:, b, 0, t], probs[:, b, 0, t], rinv[:, b, t:t + 1], probs[:, b, 1, t],
                                                         ALU.mult, ALU.add)
                        ins.then_inc(c_prob, 1)
                    else:
                        v.reciprocal(rinv[:, b], rsum[:, b]).then_inc(c_prob, 1)
                    if s in work:
                        work[s]()
                    v.wait_ge(c_pv, first_fill[s + 1])
                    if s < 4:
                        v.tensor_copy(yb[:, :, s * P:(s + 1) * P], ps[5][:, 0:SEQ].rearrange("p (t e) -> p t e", t=NT)).then_inc(c_y, 1)
                    else:
                        v.wait_ge(c_prob, s + 1)
                        for m in range(2):
                            h = 2 * (s - 4) + m
                            ins = v.tensor_tensor(yc[:, :, h * 64:(h + 1) * 64],
                                                  ps[5][:, 0:256].rearrange("p (t m e) -> p t m e", t=NT, m=2)[:, :, m],
                                                  bcast(rinv[:, b, 2 * m:2 * m + 2].unsqueeze(2), [P, NT, 64]), ALU.mult)
                        ins.then_inc(c_y, 1)
                    if s + 2 < STEPS:
                        maxima(s + 2)

            @block.gpsimd
            def _(pool):
                roots(pool, d_asked, d_root, [qrs, qrs])

        e_gc, e_gcc, e_gr, e_kk, e_d, e_e, e_m = (sem("e_" + n) for n in ("gc", "gc_copied", "gc_rows", "kk", "diff", "exp", "masked"))
        e_lt, e_y, e_ym, e_z, e_upd, e_chain = (sem("e_" + n) for n in ("lt", "y", "ym", "z", "updated", "chain"))
        e_u, e_v, e_kd, e_s, e_sc, e_ks, e_r, e_o, e_oa, e_osq, e_small, e_pchain = (
            sem("e_" + n) for n in ("u", "v", "kd", "s", "s_copied", "ks", "r", "o", "oa", "osq", "small", "pool_chain"))
        e_asked, e_root = sem("e_root_asked"), sem("e_root")
        ybank = [ps[1], ps[2], ps[3], ps[4]]
        zbank, tbank = [ps[5], ps[6]], [ps[7], ps[0]]
        e_t, e_dt = sem("e_inverse_turned"), sem("e_dt")
        kkbank, qkbank = [ps[5], ps[6]], [ps[7], ps[0]]

        def heads3(bank):
            return bank[:, :].rearrange("p (h i) -> p h i", h=HEADS)

        def per_head(cols):
            return bcast(cols.unsqueeze(2), [P, HEADS, P])

        def columns(m, direction, n):
            if len(m.shape) == 2:
                return m.rearrange("p (b a s) -> p b a s", a=2, s=1 << n)[:, :, direction]
            return m.rearrange("p h (b a s) -> p h b a s", a=2, s=1 << n)[:, :, :, direction]

        def all_heads(m):
            return bcast(m.unsqueeze(1), [P, HEADS, P])

        with nc.Block() as block:
            @block.tensor
            def _(pe):
                def turn_inverse(k):
                    n, G = divmod(k, 4)
                    pe.wait_ge(e_upd, k + 1)
                    pe.wait_ge(e_dt, k - 1)
                    for h in range(HEADS):
                        ins = pe.transpose(tbank[G % 2][:, h * P:(h + 1) * P], DI[:, G, h], ident)
                    ins.then_inc(e_t, 1)

                for d in range(2):
                    pe.matmul(ps[0][:, 8 * d:8 * d + 8], cum[d], gg[:, d].rearrange("p t h -> p (t h)"), start=True, stop=True)
                pe.matmul(ps[0][:, 16:32], ones, gg.rearrange("p d t h -> p (d t h)"), start=True, stop=True).then_inc(e_gc, 1)
                for G in range(4):
                    d, t = divmod(G, 2)
                    for h in range(HEADS):
                        ins = pe.matmul(ybank[G][:, h * P:(h + 1) * P], bcast(gg[:, d, t, h:h + 1], [P, P]), cum[d],
                                        start=True, stop=True)
                    ins.then_inc(e_gr, 1)
                for t in range(NT):
                    for h in range(HEADS):
                        k = KT[:, h, t * P:(t + 1) * P]
                        ins = pe.matmul(kkbank[t][:, h * P:(h + 1) * P], k, k, start=True, stop=True)
                    ins.then_inc(e_kk, 1)
                pe.wait_ge(e_gcc, 1)
                for t in range(NT):
                    for h in range(HEADS):
                        ins = pe.matmul(qkbank[t][:, h * P:(h + 1) * P], KT[:, h, t * P:(t + 1) * P], QT[:, h, t * P:(t + 1) * P],
                                        start=True, stop=True)
                    ins.then_inc(e_kk, 1)
                for G in range(4):
                    pe.wait_ge(e_lt, G + 1)
                    for h in range(HEADS):
                        ins = pe.transpose(ybank[G][:, h * P:(h + 1) * P], LT[:, G, h], ident)
                    ins.then_inc(e_y, 1)
                for n in range(1, LEVELS):
                    for G in range(4):
                        k = 4 * n + G
                        pe.wait_ge(e_upd, k - 3)
                        pe.wait_ge(e_dt, k - 3)
                        for h in range(HEADS):
                            ins = pe.matmul(ybank[G][:, h * 64:(h + 1) * 64], LT[:, G, h], columns(DI[:, G, h], G // 2, n),
                                            start=True, stop=True)
                        ins.then_inc(e_y, 1)
                    for G in range(4):
                        k = 4 * n + G
                        pe.wait_ge(e_ym, k - 3)
                        pe.wait_ge(e_upd, k - 1)
                        for h in range(HEADS):
                            ins = pe.matmul(zbank[G % 2][:, h * 64:(h + 1) * 64], DT[:, G, h], YM[:, G, h], start=True, stop=True)
                        ins.then_inc(e_z, 1)
                        if G >= 1:
                            turn_inverse(k - 1)
                    turn_inverse(4 * n + 3)
                pe.wait_ge(e_dt, 4 * LEVELS)
                for d in range(2):
                    t = d
                    for h in range(HEADS):
                        ins = pe.matmul(ps[1 + d][:, h * P:(h + 1) * P], DT[:, 2 * d + t, h], vtok[:, t, h], start=True, stop=True)
                    ins.then_inc(e_u, 1)
                for d in range(2):
                    pe.wait_ge(e_v, d + 1)
                    pe.wait_ge(e_kd, d + 1)
                    for h in range(HEADS):
                        ins = pe.matmul(ps[3 + d][:, h * P:(h + 1) * P], kd[:, d, h], vn1[:, d, h], start=True, stop=True)
                    ins.then_inc(e_s, 1)
                for d in range(2):
                    t = 1 - d
                    pe.wait_ge(e_sc, d + 1)
                    for h in range(HEADS):
                        pe.matmul(ps[5 + d][:, h * P:(h + 1) * P], KT[:, h, t * P:(t + 1) * P], S1[:, d, h], start=True, stop=True)
                    for h in range(HEADS):
                        ins = pe.matmul(qkbank[d][:, h * P:(h + 1) * P], QT[:, h, t * P:(t + 1) * P], S1[:, d, h], start=True, stop=True)
                    ins.then_inc(e_ks, 1)
                for d in range(2):
                    t = 1 - d
                    pe.wait_ge(e_r, d + 1)
                    for h in range(HEADS):
                        ins = pe.matmul(ps[1 + d][:, h * P:(h + 1) * P], DT[:, 2 * d + t, h], R2[:, d, h], start=True, stop=True)
                    ins.then_inc(e_u, 1)
                pe.wait_ge(e_v, 4)
                for t in range(NT):
                    first, second = t, 1 - t
                    for h in range(HEADS):
                        pe.matmul(ps[3 + t][:, h * P:(h + 1) * P], INT[:, 2 * first + t, h], vn1[:, first, h], start=True, stop=False)
                        ins = pe.matmul(ps[3 + t][:, h * P:(h + 1) * P], INT[:, 2 * second + t, h], vn2[:, second, h],
                                        start=False, stop=True)
                    ins.then_inc(e_o, 1)

            @block.scalar
            def _(act):
                act.wait_ge(e_gcc, 1)
                act.activation(egc, gc, ACT.Exp)
                act.activation(kdec, kdec, ACT.Exp).then_inc(e_small, 1)
                for G in range(4):
                    act.wait_ge(e_d, G + 1)
                    act.activation(E[:, G], E[:, G], ACT.Exp).then_inc(e_e, 1)
                for k in range(4, 4 * LEVELS):
                    act.wait_ge(e_t, k - 3)
                    act.activation(DT[:, k % 4], heads3(tbank[k % 2]), ACT.Copy).then_inc(e_dt, 1)
                for d in range(2):
                    act.wait_ge(e_s, d + 1)
                    act.activation(S1[:, d], heads3(ps[3 + d]), ACT.Copy).then_inc(e_sc, 1)
                act.wait_ge(e_oa, 2)
                act.activation(ysq.rearrange("p t n -> p (t n)"), oa.rearrange("p t h e -> p (t h e)"), ACT.Square).then_inc(e_osq, 1)

            @block.gpsimd
            def _(pool):
                plink = chain(pool, e_pchain)
                pool.wait_ge(e_small, 1)
                for d in range(2):
                    pool.tensor_tensor(kd[:, d], ktok[:, d], per_head(kdec[:, 12 * d:12 * d + 4]),
                                       ALU.mult).then_inc(e_kd, 1)
                for G in range(4):
                    d, t = divmod(G, 2)
                    pool.wait_ge(e_e, G + 1)
                    pool.tensor_tensor(INT[:, G], E[:, G], all_heads(cum[d]), ALU.mult)
                    plink(pool.tensor_tensor(LT[:, G], E[:, G], all_heads(strict[d]), ALU.mult))
                    pool.tensor_tensor(LT[:, G], LT[:, G], per_head(beta[:, d, t]), ALU.mult).then_inc(e_m, 1)
                roots(pool, e_asked, e_root, [yrs[:, 0:8]])

            @block.vector
            def _(v):
                link = chain(v, e_chain)
                ask, got = root_asker(v, e_asked, e_root)
                v.wait_ge(e_gc, 1)
                v.tensor_copy(gc, ps[0][:, 0:16])
                link(v.tensor_copy(gtot, ps[0][:, 16:32]))
                v.tensor_tensor(kdec, gtot, gc, ALU.subtract).then_inc(e_gcc, 1)
                for G in range(4):
                    v.wait_ge(e_gr, G + 1)
                    for h in range(HEADS):
                        ins = v.tensor_scalar(E[:, G, h], ybank[G][:, h * P:(h + 1) * P], gc[:, 4 * G + h:4 * G + h + 1], 0.0,
                                              ALU.subtract, ALU.min)
                    ins.then_inc(e_d, 1)
                v.wait_ge(e_kk, 4)
                for G in range(4):
                    d, t = divmod(G, 2)
                    v.wait_ge(e_m, G + 1)
                    v.tensor_tensor(LT[:, G], heads3(kkbank[t]), LT[:, G], ALU.mult).then_inc(e_lt, 1)
                    v.tensor_tensor(INT[:, G], heads3(qkbank[t]), INT[:, G], ALU.mult)
                for G in range(4):
                    d, t = divmod(G, 2)
                    v.wait_ge(e_y, G + 1)
                    v.tensor_tensor(E[:, G], heads3(ybank[G]), all_heads(level0(d)), ALU.mult)
                    link(v.tensor_tensor(DT[:, G], LT[:, G], all_heads(level0(1 - d)), ALU.mult))
                    v.tensor_tensor(DI[:, G], all_heads(ident), E[:, G], ALU.subtract).then_inc(e_upd, 1)
                    v.tensor_tensor(DT[:, G], all_heads(ident), DT[:, G], ALU.subtract).then_inc(e_dt, 1)
                for n in range(1, LEVELS):
                    for G in range(4):
                        k = 4 * n + G
                        v.wait_ge(e_y, k + 1)
                        if n > 1:
                            v.wait_ge(e_z, k - 7)
                        v.tensor_tensor(YM[:, G], ybank[G][:, 0:256].rearrange("p (h i) -> p h i", h=HEADS),
                                        bcast(level(G // 2, n).unsqueeze(1), [P, HEADS, 64]), ALU.mult).then_inc(e_ym, 1)
                    for G in range(4):
                        k = 4 * n + G
                        v.wait_ge(e_z, k - 3)
                        if n > 1:
                            v.wait_ge(e_t, k - 7)
                        d = columns(DI[:, G], G // 2, n)
                        v.tensor_tensor(d, d, zbank[G % 2][:, 0:256].rearrange("p (h b s) -> p h b s", h=HEADS, s=1 << n),
                                        ALU.subtract).then_inc(e_upd, 1)
                for d in range(2):
                    v.wait_ge(e_u, d + 1)
                    v.tensor_tensor(vn1[:, d], heads3(ps[1 + d]), per_head(beta[:, d, d]), ALU.mult).then_inc(e_v, 1)
                v.wait_ge(e_small, 1)
                for d in range(2):
                    t = 1 - d
                    G = 2 * d + t
                    v.wait_ge(e_ks, d + 1)
                    link(v.tensor_tensor(R2[:, d], heads3(ps[5 + d]), per_head(egc[:, 4 * G:4 * G + 4]), ALU.mult))
                    v.tensor_tensor(R2[:, d], vtok[:, t], R2[:, d], ALU.subtract).then_inc(e_r, 1)
                    v.tensor_tensor(qs[:, d], heads3(qkbank[d]), per_head(egc[:, 4 * G:4 * G + 4]), ALU.mult)
                for d in range(2):
                    v.wait_ge(e_u, d + 3)
                    v.tensor_tensor(vn2[:, d], heads3(ps[1 + d]), per_head(beta[:, d, 1 - d]), ALU.mult).then_inc(e_v, 1)
                for t in range(NT):
                    v.wait_ge(e_o, t + 1)
                    v.wait_ge(e_v, 4)
                    v.tensor_tensor(oa[:, t], heads3(ps[3 + t]), qs[:, 1 - t], ALU.add).then_inc(e_oa, 1)
                v.wait_ge(e_osq, 1)
                link(v.tensor_reduce(yss[:, 0:8], ysq.rearrange("p t (h e) -> p (t h) e", h=HEADS), AX.X, ALU.add))
                ask(v.tensor_scalar(yrs[:, 0:8], yss[:, 0:8], 1.0 / DH, EPS, ALU.mult, ALU.add))
                got()
                v.tensor_tensor(oa.rearrange("p t h e -> p (t h) e"), oa.rearrange("p t h e -> p (t h) e"),
                                bcast(yrs[:, 0:8].unsqueeze(2), [P, 8, DH]), ALU.mult)

        f_sq, f_yn, f_z, f_zs, f_ya, f_t, f_y, f_p, f_sig, f_m, f_chain = (
            sem("f_" + n) for n in ("squares", "y_normed", "z", "z_silu", "ya", "turned", "yT", "products", "gates", "merged", "chain"))
        f_asked, f_root = sem("f_root_asked"), sem("f_root")
        used_at[U_Z] = (f_z, NT)
        for k in range(3):
            used_at.update({U_GATE0[k]: (f_p, 4 * k + 2), U_BRANCH[k]: (f_p, 4 * k + 4), U_GATE1[k]: (f_p, 4 * k + 4)})
        merges = [(k, n, t) for k in range(3) for n in range(2) for t in range(NT)]
        with nc.Block() as block:
            @block.sync
            def _(sp):
                for u in range(RING + 8, N_FIXED - 2):
                    load_unit(sp, l, u)

            @block.tensor
            def _(pe):
                def turn(src, banks):
                    for h in range(HEADS):
                        for t in range(NT):
                            ins = pe.transpose(banks[h // 2][:, (h % 2) * SEQ + t * P:(h % 2) * SEQ + (t + 1) * P],
                                               src[:, t, h * P:(h + 1) * P], ident)
                    ins.then_inc(f_t, 1)

                unit_landed(pe, U_Z)
                for t in range(NT):
                    for c in range(KC):
                        ins = pe.matmul(ps[t][:, :], HT[:, c, t * P:(t + 1) * P], unit8(U_Z)[:, c], start=(c == 0), stop=(c == KC - 1))
                    ins.then_inc(f_z, 1)
                turn(yc, ps[2:4])
                pe.wait_ge(f_yn, 1)
                turn(yb, ps[4:6])
                pe.wait_ge(f_ya, 1)
                turn(oa.rearrange("p t h e -> p t (h e)"), ps[6:8])
                pe.wait_ge(f_y, 3)
                for i, (k, n, t) in enumerate(merges):
                    pair = 2 * (i % 3)
                    gate = (U_GATE0, U_GATE1)[n][k]
                    if i >= 3:
                        pe.wait_ge(f_m, i - 2)
                    unit_landed(pe, U_BRANCH[k])
                    unit_landed(pe, gate)
                    w = slot(U_BRANCH[k]).rearrange("p (c n) -> p c n", c=HEADS)
                    for c in range(HEADS):
                        pe.matmul(ps[pair][:, :], yT[ORDER[k]][:, c, t * P:(t + 1) * P], w[:, c, n * 512:(n + 1) * 512],
                                  start=(c == 0), stop=(c == HEADS - 1))
                    for c in range(KC):
                        ins = pe.matmul(ps[pair + 1][:, :], HT[:, c, t * P:(t + 1) * P], unit8(gate)[:, c],
                                        start=(c == 0), stop=(c == KC - 1))
                    ins.then_inc(f_p, 1)

            @block.scalar
            def _(act):
                act.activation(ysq.rearrange("p t n -> p (t n)"), yb.rearrange("p t n -> p (t n)"), ACT.Square).then_inc(f_sq, 1)
                for t in range(NT):
                    act.wait_ge(f_z, t + 1)
                    act.activation(zs[:, t], ps[t][:, :], ACT.Silu).then_inc(f_zs, 1)
                for n, (b, gain) in enumerate(((2, 1.0), (1, ndl), (0, n_gdn))):
                    act.wait_ge(f_t, n + 1)
                    for j in range(2):
                        ins = act.activation(yT[b][:, 2 * j:2 * j + 2].rearrange("p h t -> p (h t)"), ps[2 + 2 * n + j][:, :],
                                             ACT.Copy, scale=gain)
                    ins.then_inc(f_y, 1)
                for i in range(len(merges)):
                    act.wait_ge(f_p, i + 1)
                    if i >= 3:
                        act.wait_ge(f_m, i - 2)
                    act.activation(sig[:, i % 3], ps[2 * (i % 3) + 1][:, :], ACT.Sigmoid).then_inc(f_sig, 1)

            @block.vector
            def _(v):
                link = chain(v, f_chain)
                ask, got = root_asker(v, f_asked, f_root)
                v.wait_ge(f_sq, 1)
                link(v.tensor_reduce(yss[:, 0:8], ysq.rearrange("p t (h e) -> p (t h) e", h=HEADS), AX.X, ALU.add))
                ask(v.tensor_scalar(yrs[:, 0:8], yss[:, 0:8], 1.0 / DH, EPS, ALU.mult, ALU.add))
                v.tensor_tensor(ndl, n_diff, cst[:, bass.ds(l * 2 + (K_LAM + 1), 1)], ALU.mult)
                got()
                v.tensor_tensor(yb.rearrange("p t (h e) -> p (t h) e", h=HEADS), yb.rearrange("p t (h e) -> p (t h) e", h=HEADS),
                                bcast(yrs[:, 0:8].unsqueeze(2), [P, 8, DH]), ALU.mult).then_inc(f_yn, 1)
                v.wait_ge(f_zs, 2)
                v.tensor_tensor(oa.rearrange("p t h e -> p (t h e)"), oa.rearrange("p t h e -> p (t h e)"),
                                zs.rearrange("p t n -> p (t n)"), ALU.mult).then_inc(f_ya, 1)
                for i, (k, n, t) in enumerate(merges):
                    v.wait_ge(f_sig, i + 1)
                    bank = ps[2 * (i % 3)]
                    dst = merged[:, t, n * 512:(n + 1) * 512]
                    if k == 0:
                        v.tensor_tensor(dst, bank[:, :], sig[:, i % 3], ALU.mult).then_inc(f_m, 1)
                    else:
                        link(v.tensor_tensor(part[:, i % 2], bank[:, :], sig[:, i % 3], ALU.mult))
                        v.tensor_tensor(dst, dst, part[:, i % 2], ALU.add).then_inc(f_m, 1)

            @block.gpsimd
            def _(pool):
                roots(pool, f_asked, f_root, [yrs[:, 0:8]])

        h_t, h_tc, h_o, h_x, h_sq, h_xn, h_turned, h_done, h_chain = (
            sem("h_" + n) for n in ("turned", "turned_copied", "out", "residual", "squares", "xn", "turned2", "hT", "chain"))
        h_asked, h_root = sem("h_root_asked"), sem("h_root")
        used_at.update({U_OUT + n: (h_o, NT * (n + 1)) for n in range(2)})
        h_r, h_gm, h_ge, h_e1, h_ev, h_a, h_pos, h_mgood = (sem("h_" + n) for n in ("router", "group_max", "group_exp", "pair", "pair_exp", "assigned", "pos", "merged_ready"))
        with nc.Block() as block:
            @block.sync
            def _(sp):
                for u in range(N_FIXED - 2, N_FIXED):
                    load_unit(sp, l, u)
                for n in range(RING):
                    last = max(u for u in range(N_FIXED) if u % RING == n)
                    sp.wait_ge(*used_at[last])
                    load_expert(sp, l, n // 3, n)

            @block.tensor
            def _(pe):
                for c in range(KC):
                    for t in range(NT):
                        ins = pe.transpose(ps[c // 2][:, (c % 2) * SEQ + t * P:(c % 2) * SEQ + (t + 1) * P],
                                           merged[:, t].rearrange("p (f c) -> p c f", c=KC)[:, c], ident)
                    if c % 2:
                        ins.then_inc(h_t, 1)
                pe.wait_ge(h_tc, 4)
                for n in range(2):
                    unit_landed(pe, U_OUT + n)
                    for t in range(NT):
                        for c in range(KC):
                            ins = pe.matmul(ps[4 + 2 * n + t][:, :], HT[:, c, t * P:(t + 1) * P], unit8(U_OUT + n)[:, c],
                                            start=(c == 0), stop=(c == KC - 1))
                        ins.then_inc(h_o, 1)
                transpose_pe(pe, XN, h_xn, h_turned)
                pe.wait_ge(h_done, 4)
                for t in range(NT):
                    for at, n, w in ((0, N_GROUPS, rgw), (N_GROUPS, N_EXPERTS, rew)):
                        for c in range(KC):
                            ins = pe.matmul(ps[4][:, t * 36 + at:t * 36 + at + n], HT[:, c, t * P:(t + 1) * P], w[:, c],
                                            start=(c == 0), stop=(c == KC - 1))
                ins.then_inc(h_r, 1)
                for t in range(NT):
                    for n in range(2):
                        pe.matmul(ps[2 * t + n][:, :], ident, X[:, t, n * 512:(n + 1) * 512], start=True, stop=True)
                pe.wait_ge(h_a, 1)
                pe.matmul(ps[5][:, 0:32], strict[0], assigned[:, 0], start=True, stop=True)
                pe.matmul(ps[5][:, 32:64], strict[0], assigned[:, 1], start=True, stop=False)
                pe.matmul(ps[5][:, 32:64], ones, assigned[:, 0], start=False, stop=True)
                pe.matmul(ps[5][:, 64:96], ones, assigned[:, 0], start=True, stop=False)
                pe.matmul(ps[5][:, 64:96], ones, assigned[:, 1], start=False, stop=True).then_inc(h_pos, 1)

            @block.scalar
            def _(act):
                scaled_act(act, h_t, None, h_tc)
                act.wait_ge(h_x, 4)
                norm_act(act, h_sq)
                scaled_act(act, h_turned, g_ffn, h_done)
                act.wait_ge(h_gm, 1)
                for t in range(NT):
                    ins = act.activation(gexp[:, t], logit[:, t, 0:4], ACT.Exp, bias=ngm[:, t:t + 1], accum_out=gsum[:, t:t + 1])
                ins.then_inc(h_ge, 1)
                act.wait_ge(h_e1, 1)
                act.activation(e1, e1, ACT.Exp).then_inc(h_ev, 1)

            @block.vector
            def _(v):
                link = chain(v, h_chain)
                v.memset(gpad, -3e38)
                scaled_dve(v, h_t, None, h_tc)
                for n in range(2):
                    for t in range(NT):
                        v.wait_ge(h_o, 2 * n + t + 1)
                        dst = X[:, t, n * 512:(n + 1) * 512]
                        v.tensor_tensor(dst, dst, ps[4 + 2 * n + t][:, :], ALU.add).then_inc(h_x, 1)
                norm_dve(v, h_sq, root_asker(v, h_asked, h_root), h_xn)
                scaled_dve(v, h_turned, g_ffn, h_done)
                v.wait_ge(h_r, 1)
                link(v.tensor_tensor(logit, ps[4][:, 0:72].rearrange("p (t n) -> p t n", t=NT), bcast(rb.unsqueeze(1), [P, NT, 36]), ALU.add))
                link(v.tensor_copy(gpad[:, :, 0:4], logit[:, :, 0:4]))
                for t in range(NT):
                    ins = v.max(gmax8[:, t], gpad[:, t])
                link(ins)
                v.tensor_scalar(ngm, gmax8[:, :, 0], -1.0, None, ALU.mult).then_inc(h_gm, 1)
                for t in range(NT):
                    ins = v.max_index(idx3[:, t], gmax8[:, t], gpad[:, t])
                link(ins)
                link(v.tensor_copy(idxf, idx3))
                for t in range(NT):
                    ins = v.tensor_scalar(goh[:, t], cst[:, K_IOTA:K_IOTA + 8], idxf[:, t, 0:1], None, ALU.is_equal)
                link(ins)
                link(v.tensor_scalar(goh, goh, -1.0, 1e30, ALU.add, ALU.mult))
                for t in range(NT):
                    ins = v.tensor_tensor(emask[:, t].rearrange("p (g e) -> p g e", g=N_GROUPS),
                                          logit[:, t, 4:36].rearrange("p (g e) -> p g e", g=N_GROUPS),
                                          bcast(goh[:, t, 0:4].unsqueeze(2), [P, N_GROUPS, PER_GROUP]), ALU.add)
                link(ins)
                for t in range(NT):
                    ins = v.max(etop[:, t], emask[:, t])
                link(ins)
                v.tensor_tensor(e1, etop[:, :, 1], etop[:, :, 0], ALU.subtract).then_inc(h_e1, 1)
                for t in range(NT):
                    ins = v.max_index(idx3[:, t], etop[:, t], emask[:, t])
                link(ins)
                link(v.tensor_copy(idxf, idx3))
                for t in range(NT):
                    v.tensor_scalar(hot0[:, t], cst[:, K_IOTA:K_IOTA + N_EXPERTS], idxf[:, t, 0:1], None, ALU.is_equal)
                    ins = v.tensor_scalar(hot1[:, t], cst[:, K_IOTA:K_IOTA + N_EXPERTS], idxf[:, t, 1:2], None, ALU.is_equal)
                link(ins)
                v.tensor_tensor(assigned, hot0, hot1, ALU.add).then_inc(h_a, 1)
                v.wait_ge(h_ge, 1)
                v.wait_ge(h_ev, 1)
                v.tensor_scalar(esum, e1, 1.0, None, ALU.add)
                link(v.reciprocal(gprob, gsum))
                link(v.reciprocal(esum, esum))
                link(v.tensor_tensor(w01[:, :, 0], gprob, esum, ALU.mult))
                link(v.tensor_tensor(w01[:, :, 1], w01[:, :, 0], e1, ALU.mult))
                for t in range(NT):
                    ins = v.tensor_scalar(hotw[:, t], hot0[:, t], w01[:, t, 0:1], None, ALU.mult)
                link(ins)
                for t in range(NT):
                    ins = v.scalar_tensor_tensor(weight[:, t], hot1[:, t], w01[:, t, 1:2], hotw[:, t], ALU.mult, ALU.add)
                link(ins)
                v.wait_ge(h_pos, 1)
                link(v.scalar_tensor_tensor(posn, ps[5][:, 0:64].rearrange("p (t e) -> p t e", t=NT), 1.0, assigned, ALU.add, ALU.mult))
                v.tensor_scalar(posn, posn, -1.0, None, ALU.add)
                link(v.tensor_copy(cnt[:, :], ps[5][:, 64:96]))
                link(v.tensor_tensor(over, bcast(cnt[:, :].unsqueeze(2), [P, N_EXPERTS, 8]),
                                     bcast(cst[:, K_THR:K_THR + 8].unsqueeze(1), [P, N_EXPERTS, 8]), ALU.is_gt))
                link(v.tensor_reduce(nbf[:, :], over, AX.X, ALU.add))
                link(v.tensor_scalar(nbf[:, :], nbf[:, :], 1.0, None, ALU.add))
                v.tensor_copy(nbi[:, :], nbf[:, :])

            @block.gpsimd
            def _(pool):
                roots(pool, h_asked, h_root, [rstd])

        (m_sel, m_gathered, m_rows, m_turned, m_xg, m_tw, m_selwT, m_gu, m_p, m_fold, m_sg, m_hid, m_d0, m_d1, m_y0, m_y1, m_end, m_scattered, m_chain, m_jobs, m_jobs_turned) = (
            sem("m_" + n) for n in ("selected", "gathered", "rows_copied", "rows_turned", "xg", "selw_turned", "selwT", "gate_up", "gate_up_copied", "folded",
                                    "silu", "hidden", "down0", "down1", "y0", "y1", "end", "scattered", "chain", "jobs", "jobs_turned"))
        bank_a, bank_b, bank_c, bank_d = ps[4:8]
        wg, wu, wd = [[slot(3 * k + n) for k in range(2)] for n in range(3)]

        def jobs(eng, body):
            J = eng.alloc_register("jobs")
            eng.reg_mov(J, 1)
            with eng.Fori(0, N_EXPERTS // 2) as i:
                for k in range(2):
                    n = eng.value_load(nbi[0:1, bass.ds(i * 2 + k, 1)], min_val=1, max_val=ROUNDS)
                    with eng.Fori(0, n) as r:
                        body(eng.snap(J), i, k, r)
                        eng.reg_add(J, J, 1)
            eng.free_register(J)

        with nc.Block() as block:
            @block.sync
            def _(sp):
                ended = sp.alloc_register("jobs_ended")
                sp.reg_mov(ended, 0)
                with sp.Fori(0, N_EXPERTS // 2 - 1) as i:
                    for k in range(2):
                        n = sp.value_load(nbi[0:1, bass.ds(i * 2 + k, 1)], min_val=1, max_val=ROUNDS)
                        sp.reg_add(ended, ended, n)
                        sp.wait_ge(m_gu, sp.snap(ended))
                        for n in range(2):
                            load_expert(sp, l, i * 2 + k + 2, 3 * k + n)
                        sp.wait_ge(m_d1, sp.snap(ended))
                        load_expert(sp, l, i * 2 + k + 2, 3 * k + 2)
                sp.free_register(ended)

            @block.tensor
            def _(pe):
                def gather(J):
                    pe.wait_ge(m_sel, J)
                    for t in range(NT):
                        for g in range(4):
                            ins = pe.matmul(bank_a[32 * g:32 * g + 32, 0:256], sel[:, t],
                                            XN[:, t].rearrange("p (f c) -> p c f", c=KC)[:, 2 * g:2 * g + 2],
                                            start=(t == 0), stop=(t == NT - 1))
                    ins.then_inc(m_gathered, 1)

                def turn(J):
                    pe.wait_ge(m_rows, J)
                    for h in range(2):
                        ins = pe.transpose(bank_a[:, 256 + h * P:256 + (h + 1) * P], rows[:, h * P:(h + 1) * P], ident)
                    ins.then_inc(m_turned, 1)

                def scatter(J):
                    pe.wait_ge(m_selwT, J)
                    for n, s in ((0, m_y0), (1, m_y1)):
                        pe.wait_ge(s, J)
                        for t in range(NT):
                            pe.matmul(ps[2 * t + n][:, :], selwT[:, t], ymoe[:, n * 512:(n + 1) * 512], start=False, stop=True,
                                      skip_group_check=True)

                def job(J, i, k, r):
                    pe.wait_ge(m_xg, J)
                    landing = pe.snap(i * 16 + 16)
                    pe.wait_ge(m_land[3 * k], landing)
                    pe.wait_ge(m_land[3 * k + 1], landing)
                    for kk in range(4):
                        for g in range(4):
                            c = 4 * (g % 2) + kk
                            w = (wg if g < 2 else wu)[k].rearrange("p (c n) -> p c n", c=KC)
                            ins = pe.matmul(bank_b[32 * g:32 * g + 32, :], xg[:, c], w[:, c], start=(kk == 0), stop=(kk == 3))
                    ins.then_inc(m_gu, 1)
                    pe.wait_ge(m_y1, J)
                    gather(pe.snap(J + 1))
                    pe.wait_ge(m_p, J)
                    pe.wait_ge(m_selwT, J)
                    for c in range(4):
                        ins = pe.matmul(bank_c[:, c * 64:(c + 1) * 64], gu.rearrange("p (f c) -> p c f", c=4)[:, c],
                                        cst[:, K_FOLD:K_FOLD + 64], start=True, stop=True)
                    ins.then_inc(m_fold, 1)
                    turn(pe.snap(J + 1))
                    scatter(J)
                    pe.wait_ge(m_hid, J)
                    pe.wait_ge(m_land[3 * k + 2], landing)
                    w = wd[k].rearrange("p (c n) -> p c n", c=4)
                    for n, bank, s in ((0, bank_d, m_d0), (1, bank_a, m_d1)):
                        for g in range(4):
                            ins = pe.matmul(bank[32 * g:32 * g + 32, :], hid[:, g], w[:, g, n * 512:(n + 1) * 512], start=True, stop=True)
                        ins.then_inc(s, 1)
                    for t in range(NT):
                        ins = pe.transpose(bank_c[:, 256 + t * P:256 + (t + 1) * P], selw[:, t].rearrange("p g s -> p (g s)"), ident)
                    ins.then_inc(m_tw, 1)

                gather(1)
                turn(1)
                pe.wait_ge(m_jobs, 1)
                for n in range(2):
                    ins = pe.transpose(bank_c[0:1, 256 + n * P:256 + (n + 1) * P], jf[:, n:n + 1], ident)
                ins.then_inc(m_jobs_turned, 1)
                jobs(pe, job)
                pe.wait_ge(m_end, 1)
                scatter_last = [(m, n) for n in range(2) for m in range(NT)]
                for t, n in scatter_last:
                    ins = pe.matmul(ps[2 * t + n][:, :], selwT[:, t], ymoe[:, n * 512:(n + 1) * 512], start=False, stop=True,
                                    skip_group_check=True)
                ins.then_inc(m_scattered, 1)

            @block.scalar
            def _(act):
                def job(J, i, k, r):
                    act.wait_ge(m_gu, J)
                    act.activation(gu, bank_b[:, :], ACT.Copy).then_inc(m_p, 1)
                    act.wait_ge(m_fold, J)
                    act.activation(sg, bank_c[:, 0:256].rearrange("p (c x s) -> p c x s", c=4, x=2)[:, :, 0], ACT.Silu).then_inc(m_sg, 1)
                    act.wait_ge(m_d0, J)
                    act.activation(ymoe[:, 0:512], bank_d[:, :], ACT.Copy).then_inc(m_y0, 1)
                jobs(act, job)

            @block.vector
            def _(v):
                def select(e, r):
                    for t in range(NT):
                        ins = v.tensor_scalar(sel[:, t], cst[:, bass.ds(r * CAP + K_IOTA, CAP)], posn[:, t, bass.ds(e, 1)], None, ALU.is_equal)
                    ins.then_inc(m_sel, 1)

                def gained(J):
                    v.wait_ge(m_gathered, J)
                    v.tensor_copy(rows, bank_a[:, 0:256]).then_inc(m_rows, 1)
                    v.wait_ge(m_turned, J)
                    v.tensor_tensor(xg.rearrange("p (g h) s -> p h g s", h=2), bank_a[:, 256:512].rearrange("p (h g s) -> p h g s", h=2, g=4),
                                    bcast(g_ffn.rearrange("p (g h) -> p h g", h=2).unsqueeze(3), [P, 2, 4, CAP]),
                                    ALU.mult).then_inc(m_xg, 1)

                v.memset(ymoe[:, 0:512], 0.0).then_inc(m_y0, 1)
                v.memset(ymoe[:, 512:1024], 0.0).then_inc(m_y1, 1)
                v.memset(selwT, 0.0).then_inc(m_selwT, 1)
                select(0, 0)
                index = cst[:, K_INDEX:K_INDEX + 1]
                link = chain(v, m_chain)
                link(v.tensor_tensor_scan(jend, cst[:, K_ONES:K_ONES + N_EXPERTS], nbf, 0.0, ALU.mult, ALU.add))
                v.tensor_scalar(jcmp[:, 0], jend, index, None, ALU.is_le)
                link(v.tensor_tensor(jstart, jend, nbf, ALU.subtract))
                gained(1)
                link(v.scalar_tensor_tensor(jcmp[:, 1], jstart, index, jstart, ALU.is_le, ALU.mult))
                link(v.tensor_reduce(jf[:, 0:1], jcmp[:, 0], AX.X, ALU.add))
                v.tensor_scalar(jf[:, 0:1], jf[:, 0:1], float(N_EXPERTS - 1), None, ALU.min)
                link(v.tensor_reduce(jf[:, 1:2], jcmp[:, 1], AX.X, ALU.max))
                link(v.tensor_tensor(jf[:, 1:2], index, jf[:, 1:2], ALU.subtract))
                v.tensor_scalar(jf[:, 1:2], jf[:, 1:2], float(ROUNDS - 1), None, ALU.min).then_inc(m_jobs, 1)
                v.wait_ge(m_jobs_turned, 1)
                link(v.tensor_copy(jobtab[0:1], bank_c[0:1, 256:512].rearrange("p (a j) -> p a j", a=2)[:, :, 0:JOBS]))

                def job(J, i, k, r):
                    e = i * 2 + k
                    for t in range(NT):
                        v.tensor_scalar(selw[:, t], bcast(cst[:, bass.ds(r * CAP + K_IOTA, CAP)].unsqueeze(1), [P, 4, CAP]),
                                        posn[:, t, bass.ds(e, 1)], weight[:, t, bass.ds(e, 1)], ALU.is_equal, ALU.mult)
                    e_next = v.value_load(jobtab[0:1, 0, bass.ds(J, 1)], min_val=0, max_val=N_EXPERTS - 1)
                    r_next = v.value_load(jobtab[0:1, 1, bass.ds(J, 1)], min_val=0, max_val=ROUNDS - 1)
                    select(e_next, r_next)
                    gained(v.snap(J + 1))
                    v.wait_ge(m_sg, J)
                    v.tensor_tensor(hid, bank_c[:, 0:256].rearrange("p (c x s) -> p c x s", c=4, x=2)[:, :, 1], sg, ALU.mult).then_inc(m_hid, 1)
                    v.wait_ge(m_d1, J)
                    v.tensor_copy(ymoe[:, 512:1024], bank_a[:, :]).then_inc(m_y1, 1)
                    v.wait_ge(m_tw, J)
                    v.tensor_copy(selwT.rearrange("p t q -> p (t q)"), bank_c[:, 256:512]).then_inc(m_selwT, 1)
                    v.wait_ge(m_y0, v.snap(J + 1))
                jobs(v, job)
                v.drain().then_inc(m_end, 1)
                v.wait_ge(m_scattered, 1)
                for t in range(NT):
                    for n in range(2):
                        v.tensor_copy(X[:, t, n * 512:(n + 1) * 512], ps[2 * t + n][:, :])

        for s in names:
            nc.gpsimd.sem_clear(s)
        nc.all_engine_barrier()

    z_sq, z_asked, z_root, z_w, z_out, z_y = (top.enter_context(nc.semaphore("z_" + n)) for n in ("squares", "root_asked", "root", "gain", "stored", "y"))
    with nc.Block() as block:
        @block.sync
        def _(sp):
            sp.dma_start(fw, final_norm_w.rearrange("(o d) -> o d", o=1).broadcast_to([P, D_MODEL])).then_inc(z_w, 16)
            for t in range(NT):
                sp.wait_ge(z_y, t + 1)
                sp.dma_start(out[0, t * P:(t + 1) * P, :], fin[:, t]).then_inc(z_out, 16)
            sp.wait_ge(z_out, 16 * NT)

        @block.gpsimd
        def _(pool):
            roots(pool, z_asked, z_root, [rstd])

        @block.scalar
        def _(act):
            norm_act(act, z_sq)

        @block.vector
        def _(v):
            ask, got = root_asker(v, z_asked, z_root)
            v.wait_ge(z_sq, NT)
            ask(v.tensor_scalar(rstd, ss, 1.0 / D_MODEL, EPS, ALU.mult, ALU.add))
            got()
            v.wait_ge(z_w, 16)
            for t in range(NT):
                v.scalar_tensor_tensor(fin[:, t], X[:, t], rstd[:, t:t + 1], fw, ALU.mult, ALU.mult).then_inc(z_y, 1)
    top.close()


_INS = ['x', 'attn_norm_w', 'w_in', 'gdn_conv_w', 'gdn_a_log', 'gdn_dt_bias', 'gdn_norm_w', 'diff_lambda', 'diff_norm_w',
        'gqa_q_norm_w', 'gqa_k_norm_w', 'w_branch_a', 'w_branch_b', 'w_branch_c', 'w_out', 'ffn_norm_w', 'router_group_w',
        'router_group_b', 'router_expert_w', 'router_expert_b', 'expert_w_gate', 'expert_w_up', 'expert_w_down',
        'final_norm_w']
_OUTS = [((1, SEQ, D_MODEL), 'float32')]


def kernel(**inputs):
    import numpy as _np
    import concourse.bacc as _bacc
    from concourse import mybir as _mybir
    from concourse.bass_utils import run_bass_kernel_spmd as _run

    nc = _bacc.Bacc("TRN2", target_bir_lowering=False, num_devices=1)
    arrays, args = {}, []
    for name in _INS:
        a = _np.ascontiguousarray(inputs[name])
        arrays[f"in_{name}_dram"] = a
        args.append(nc.dram_tensor(f"in_{name}_dram", a.shape, _mybir.dt.from_np(a.dtype), kind="ExternalInput").ap())
    c = shape_constants()
    arrays["consts_dram"] = c
    args.append(nc.dram_tensor("consts_dram", c.shape, _mybir.dt.from_np(c.dtype), kind="ExternalInput").ap())
    for i, (shape, dtype) in enumerate(_OUTS):
        dt = _mybir.dt.from_np(_np.dtype(dtype))
        args.append(nc.dram_tensor(f"out_{i}_dram", shape, dt, kind="ExternalOutput").ap())
    encoder_trunk(nc, *args)
    r = _run(nc, [arrays], core_ids=[0])
    got = tuple(r.results[0][f"out_{i}_dram"] for i in range(len(_OUTS)))
    return got[0]
```

```python
import concourse.bass as bass
from concourse import mybir
from contextlib import ExitStack
import math

F32 = mybir.dt.float32
I32 = mybir.dt.int32
ALU = mybir.AluOpType
ACT = mybir.ActivationFunctionType
AX = mybir.AxisListType

P = 128
D_MODEL = 1024
SEQ = 256
NT = SEQ // P
KC = D_MODEL // P
EPS = 1e-6
HEADS = 4
DH = 128
TAPS = 5
N_EXPERTS = 32
N_GROUPS = 4
PER_GROUP = 8
FF = 512
CAP = 32
ROUNDS = SEQ // CAP
SETS = 3
JOBS = 48
LEVELS = 7
SCALE = 64 ** -0.5

C_Q, C_Z, C_BA, C_DQ, C_DK, C_DV, C_CQ, C_CKV, C_GATE = 0, 1536, 2048, 2064, 2576, 3088, 3600, 4112, 4368

RING = 6
U_DQ, U_DK, U_DV, U_CQ, U_CKV, U_GQ, U_GK, U_GV, U_Z = range(9)
ORDER = (2, 1, 0)
U_GATE0, U_BRANCH, U_GATE1 = (9, 12, 15), (10, 13, 16), (11, 14, 17)
U_OUT = 18
N_FIXED = 20

K_IDENT, K_ONES, K_UF, K_UB, K_SF, K_SB = (128 * n for n in range(6))
K_LEVEL0 = 768
K_LEVEL = K_LEVEL0 + 2 * 128
K_COSD = K_LEVEL + 2 * LEVELS * 64
K_SIND, K_COSG, K_SING = K_COSD + 128, K_COSD + 256, K_COSD + 384
K_IOTA = K_COSD + 512
K_LAM = K_IOTA + SEQ
K_THR = K_LAM + 4
K_FOLD = K_THR + 8
K_HALF = K_FOLD + 64
K_INDEX = K_HALF + 8
K_ALL = K_INDEX + 1


def shape_constants():
    import numpy as np
    c = np.zeros((P, K_ALL), np.float32)
    r, j = np.arange(P)[:, None], np.arange(P)[None, :]
    c[:, K_IDENT:K_IDENT + P] = r == j
    c[:, K_ONES:K_ONES + P] = 1
    c[:, K_UF:K_UF + P] = r <= j
    c[:, K_UB:K_UB + P] = r >= j
    c[:, K_SF:K_SF + P] = r < j
    c[:, K_SB:K_SB + P] = r > j
    for n in range(LEVELS):
        s = 1 << n
        m = (r // (2 * s) == j // (2 * s)) & (r % (2 * s) >= s) & (j % (2 * s) < s)
        for d, mask in enumerate((m, m.T)):
            cols = (np.arange(P) >> n & 1) == d
            c[:, K_LEVEL + (d * LEVELS + n) * 64:K_LEVEL + (d * LEVELS + n + 1) * 64] = mask[:, cols]
            if n == 0:
                c[:, K_LEVEL0 + d * P:K_LEVEL0 + (d + 1) * P] = mask

    def rope(pos, dim):
        inv = np.float32(1.0) / np.power(np.float32(10000.0), np.arange(0, dim, 2, dtype=np.float32) / np.float32(dim))
        ang = pos.astype(np.float32)[:, None] * inv[None, :].astype(np.float32)
        cos, sin = np.cos(ang), np.sin(ang)
        return np.concatenate([cos, cos], 1), np.concatenate([-sin, sin], 1)

    pos = np.arange(SEQ)
    cd, sd = rope(pos, 64)
    cr, sr = rope(pos // 64, 32)
    cc, sc = rope(pos % 64, 32)
    for at, t in ((K_COSD, cd), (K_SIND, sd), (K_COSG, np.concatenate([cr, cc], 1)), (K_SING, np.concatenate([sr, sc], 1))):
        c[:, at:at + 128] = t.reshape(NT, P, 64).transpose(1, 0, 2).reshape(P, 128)
    c[:, K_IOTA:K_IOTA + SEQ] = np.arange(SEQ)
    for l in range(2):
        init = 0.8 - 0.6 * math.exp(-0.3 * l)
        c[:, K_LAM + 2 * l] = init
        c[:, K_LAM + 2 * l + 1] = 1.0 - init
    c[:, K_THR:K_THR + ROUNDS - 1] = CAP * np.arange(1, ROUNDS)
    c[:, K_THR + ROUNDS - 1] = 1e9
    m = np.arange(64)[None, :]
    c[:, K_FOLD:K_FOLD + 64] = (r % 32 == m % 32) & ((r >= 64) == (m >= 32))
    c[:, K_HALF:K_HALF + 8] = -0.5
    c[:, K_INDEX] = np.arange(P)
    return c


def encoder_trunk(nc, x, attn_norm_w, w_in, gdn_conv_w, gdn_a_log, gdn_dt_bias, gdn_norm_w, diff_lambda, diff_norm_w,
                  gqa_q_norm_w, gqa_k_norm_w, w_branch_a, w_branch_b, w_branch_c, w_out, ffn_norm_w, router_group_w,
                  router_group_b, router_expert_w, router_expert_b, expert_w_gate, expert_w_up, expert_w_down,
                  final_norm_w, consts, out):
    depth = w_in.shape[0]
    top = ExitStack()

    def sb(name, cols, dt=F32):
        return top.enter_context(nc.sbuf_tensor(name, [P, cols], dt))

    ring = sb("ring", RING * 4096)
    x_sb = sb("x_sb", NT * D_MODEL)
    hT = sb("hT", KC * SEQ)
    xn = sb("xn", NT * D_MODEL)
    cst = sb("cst", K_ALL)
    arena = sb("arena", 16160)
    par = sb("par", 1064)
    small = sb("small", 768)
    nbi = sb("nbi", N_EXPERTS, I32)
    ps = [top.enter_context(nc.psum_tensor(f"ps{i}", [P, 512], F32)) for i in range(8)]

    def view(t, at, *dims):
        n = math.prod(dims)
        v = t[:, at:at + n]
        if len(dims) == 1:
            return v
        names = "abcd"[:len(dims)]
        return v.rearrange(f"p ({' '.join(names)}) -> p {' '.join(names)}", **dict(zip(names, dims)))

    ident = cst[:, K_IDENT:K_IDENT + P]
    ones = cst[:, K_ONES:K_ONES + P]
    cum = [cst[:, K_UF:K_UF + P], cst[:, K_UB:K_UB + P]]
    strict = [cst[:, K_SF:K_SF + P], cst[:, K_SB:K_SB + P]]

    def level0(direction):
        return cst[:, K_LEVEL0 + direction * P:K_LEVEL0 + (direction + 1) * P]

    def level(direction, n):
        return cst[:, K_LEVEL + (direction * LEVELS + n) * 64:K_LEVEL + (direction * LEVELS + n + 1) * 64]

    X = view(x_sb, 0, NT, D_MODEL)
    HT = view(hT, 0, KC, SEQ)
    XN = view(xn, 0, NT, D_MODEL)

    p_at = [0]

    def param(*dims):
        v = view(par, p_at[0], *dims)
        p_at[0] += math.prod(dims)
        return v

    g_attn, g_ffn = param(KC), param(KC)
    convw = param(TAPS * 12)
    dt_bias, a_log = param(8), param(8)
    n_gdn, n_diff = param(1), param(1)
    lamv_flat = param(256)
    lamv = lamv_flat.rearrange("p (a b d) -> p a b d", a=2, b=2)
    qn_w, kn_w = param(64), param(64)
    rw = param(KC, N_GROUPS + N_EXPERTS)
    rb = param(N_GROUPS + N_EXPERTS)
    wba = param(KC, 16)
    convrows = param(128)
    assert p_at[0] <= 1064

    s_at = [0]

    def tiny(*dims):
        v = view(small, s_at[0], *dims)
        s_at[0] += math.prod(dims)
        return v

    ss, rstd = tiny(NT), tiny(NT)
    beta, gg = tiny(2, NT, HEADS), tiny(2, NT, HEADS)
    sp_a, sp_b, sp_c = tiny(2, NT, HEADS), tiny(2, NT, HEADS), tiny(2, NT, HEADS)
    aexp = tiny(8)
    bar = tiny(NT, 16)
    gc, gtot, egc, kdec = tiny(16), tiny(16), tiny(16), tiny(16)
    lprod, lsum, lexp = tiny(2, 64), tiny(2), tiny(2)
    nlam, ndl = tiny(1), tiny(1)
    hss, hrs = tiny(16), tiny(16)
    qss, qrs = tiny(NT, HEADS), tiny(NT, HEADS)
    mx, nmx, rsum, rinv = tiny(2, 4), tiny(2, 4), tiny(2, 4), tiny(2, 4)
    rl = tiny(2, 2)
    yss, yrs = tiny(16), tiny(16)
    logit = tiny(NT, 36)
    gpad, gmax8 = tiny(NT, 8), tiny(NT, 8)
    gexp, gsum, gprob, ngm = tiny(NT, 4), tiny(NT), tiny(NT), tiny(NT)
    goh = tiny(NT, 8)
    emask, etop = tiny(NT, N_EXPERTS), tiny(NT, 8)
    e1, esum, w01 = tiny(NT), tiny(NT), tiny(NT, 2)
    idxf = tiny(NT, 8)
    assert s_at[0] <= 768, s_at[0]
    idx = top.enter_context(nc.sbuf_tensor("idx", [P, NT * 8], mybir.dt.uint32))
    idx3 = idx[:, :].rearrange("p (t k) -> p t k", t=NT)
    hot = view(arena, 2880, 6, NT, N_EXPERTS)
    assigned, weight, posn, hot0, hot1, hotw = (hot[:, n] for n in range(6))
    cnt, nbf = view(arena, 3264, N_EXPERTS), view(arena, 3296, N_EXPERTS)
    over = view(arena, 3328, N_EXPERTS, 8)
    jend, jstart = view(arena, 3584, N_EXPERTS), view(arena, 3616, N_EXPERTS)
    jf = view(arena, 3648, 2)
    jcmp = view(arena, 3652, 2, N_EXPERTS)
    jobtab = top.enter_context(nc.sbuf_tensor("jobtab", [P, 2 * JOBS], I32))[:, :].rearrange("p (a j) -> p a j", a=2)

    dqT, dkT = view(arena, 0, HEADS, SEQ), view(arena, 1024, HEADS, SEQ)
    dv = view(arena, 2048, NT, 512)
    cqT = view(arena, 3072, HEADS, SEQ)
    ckT = view(arena, 4096, 2, SEQ)
    cv = view(arena, 4608, NT, 128)
    squares, gqa_tmp = view(arena, 6912, 2, 512), view(arena, 7936, 512)
    rope_a, rope_b = view(arena, 4864, 2, 512), view(arena, 5888, 2, 512)
    probs = view(arena, 6912, 2, 2, NT, SEQ)
    probsT = view(arena, 5888, 2, 2, SEQ)
    gqn = view(arena, 4864, 2, 512)
    pad = view(arena, 8960, 2, HEADS, SEQ + 4)
    conv = view(arena, 11040, 2, HEADS, SEQ)
    conv_flat = view(arena, 11040, 2, HEADS * SEQ)
    qtok = view(arena, 13088, NT, HEADS, DH)
    ktok = view(arena, 14112, NT, HEADS, DH)
    vtok = view(arena, 15136, NT, HEADS, DH)
    QT, KT = view(arena, 8960, HEADS, SEQ), view(arena, 9984, HEADS, SEQ)
    yb, yc = view(xn, 0, NT, 512), view(xn, 1024, NT, 512)
    LT = view(arena, 0, 4, HEADS, P)
    INT = view(arena, 2048, 4, HEADS, P)
    DI = view(arena, 4096, 4, HEADS, P)
    DT = view(arena, 6144, 4, HEADS, P)
    E = view(arena, 11040, 4, HEADS, P)
    YM = view(arena, 11040, 4, HEADS, 64)
    kd = view(arena, 13088, 2, HEADS, DH)
    vn1, S1 = view(arena, 0, 2, HEADS, DH), view(arena, 1024, 2, HEADS, DH)
    R2 = view(arena, 4096, 2, HEADS, DH)
    vn2, qs = view(arena, 5120, 2, HEADS, DH), view(arena, 11040, 2, HEADS, DH)
    oa = view(arena, 12064, NT, HEADS, DH)
    yT = [view(arena, 1024 * n, HEADS, SEQ) for n in range(3)]
    zs = view(arena, 3072, NT, 512)
    sig = view(arena, 4096, 3, 512)
    part = view(arena, 5632, 2, 512)
    merged = view(arena, 13088, NT, D_MODEL)
    ysq = view(arena, 11040, NT, 512)
    sel = view(arena, 0, NT, CAP)
    selw = view(arena, 64, NT, 4, CAP)
    selwT = view(arena, 320, NT, P)
    xg = view(arena, 576, KC, CAP)
    gu = view(arena, 832, FF)
    sg = view(arena, 1344, 4, CAP)
    hid = view(arena, 1472, 4, CAP)
    ymoe = view(arena, 1600, D_MODEL)
    rows = view(arena, 2624, 256)
    junk = view(arena, 0, NT, D_MODEL)
    fin = view(arena, 0, NT, D_MODEL)
    fw = view(arena, 2048, D_MODEL)

    def slot(u):
        return ring[:, (u % RING) * 4096:(u % RING + 1) * 4096]

    def expert_slot(n):
        return slot(n) if n < RING else view(arena, 3872 + (n - RING) * 4096, 4096)

    def unit8(u):
        return slot(u).rearrange("p (c n) -> p c n", c=8)

    def bcast(ap, shape):
        return ap.broadcast_to(shape)

    names = {}

    def sem(name):
        names[name] = top.enter_context(nc.semaphore(name))
        return names[name]

    landed = [sem(f"unit_landed{n}") for n in range(RING)]
    used_at = {}
    (m_sel, m_gathered, m_rows, m_turned, m_xg, m_tw, m_selwT, m_gu, m_p, m_fold, m_sg, m_hid, m_d0, m_d1, m_y0, m_y1, m_end, m_scattered, m_chain, m_jobs, m_jobs_turned) = (
        sem("m_" + n) for n in ("selected", "gathered", "rows_copied", "rows_turned", "xg", "selw_turned", "selwT", "gate_up", "gate_up_copied", "folded",
                                "silu", "hidden", "down0", "down1", "y0", "y1", "end", "scattered", "chain", "jobs", "jobs_turned"))
    m_land = [sem(f"expert_landed{n}") for n in range(3 * SETS)]
    expert_sems = [name for name in names if name.startswith(("m_", "expert_landed"))]

    def unit_landed(eng, u):
        eng.wait_ge(landed[u % RING], 16 * (u // RING + 1))

    def load_unit(sp, l, u):
        if u >= RING:
            sp.wait_ge(*used_at[u - RING])
        cols = {U_DQ: C_DQ, U_DK: C_DK, U_DV: C_DV, U_CQ: C_CQ, U_GQ: C_Q, U_GK: C_Q + 512, U_GV: C_Q + 1024, U_Z: C_Z}
        for k, b in enumerate(ORDER):
            cols[U_GATE0[k]] = C_GATE + b * D_MODEL
            cols[U_GATE1[k]] = C_GATE + b * D_MODEL + 512
        if u in U_BRANCH:
            w = (w_branch_a, w_branch_b, w_branch_c)[ORDER[U_BRANCH.index(u)]]
            src = w[bass.ds(l, 1)].rearrange("o (c p) n -> p (o c) n", p=P)
            dst = slot(u).rearrange("p (c n) -> p c n", c=4)
        elif u == U_CKV:
            src = w_in[bass.ds(l, 1), :, C_CKV:C_CKV + 256].rearrange("o (p c) n -> p (o c) n", c=KC)
            dst = unit8(u)[:, :, 0:256]
        elif u >= U_OUT:
            n = u - U_OUT
            src = w_out[bass.ds(l, 1), :, n * 512:(n + 1) * 512].rearrange("o (p c) n -> p (o c) n", c=KC)
            dst = unit8(u)
        else:
            src = w_in[bass.ds(l, 1), :, cols[u]:cols[u] + 512].rearrange("o (p c) n -> p (o c) n", c=KC)
            dst = unit8(u)
        sp.dma_start(dst, src).then_inc(landed[u % RING], 16)

    def last_unit(n):
        return max(u for u in range(N_FIXED) if u % RING == n)

    def load_expert(sp, l, e, n):
        if n % 3 < 2:
            w = (expert_w_gate, expert_w_up)[n % 3].rearrange("l e (p c) f -> (l e) p c f", c=KC)
            dst = expert_slot(n).rearrange("p (o c f) -> p o c f", o=1, c=KC)
        else:
            w = expert_w_down.rearrange("l e (p c) d -> (l e) p c d", c=4)
            dst = expert_slot(n).rearrange("p (o c d) -> p o c d", o=1, c=4)
        src = w[bass.ds(l * N_EXPERTS + e, 1)].rearrange("o p c f -> p o c f")
        sp.dma_start(dst, src).then_inc(m_land[n], 16)

    def chain(eng, s):
        count = [0]

        def link(ins):
            count[0] += 1
            ins.then_inc(s, 1)
            eng.wait_ge(s, count[0])
        return link

    def root_asker(v, asked, given):
        count = [0]

        def ask(ins):
            count[0] += 1
            ins.then_inc(asked, 1)

        def got():
            v.wait_ge(given, count[0])
        return ask, got

    def roots(pool, asked, given, args):
        for n, a in enumerate(args):
            pool.wait_ge(asked, n + 1)
            half = cst[:, K_HALF:K_HALF + math.prod(a.shape[1:])]
            if len(a.shape) == 3:
                half = half.rearrange("p (t h) -> p t h", t=a.shape[1])
            pool.tensor_tensor(a, a, half, ALU.pow).then_inc(given, 1)

    def norm_act(act, done):
        for t in range(NT):
            act.activation(junk[:, t], X[:, t], ACT.Square, accum_out=ss[:, t:t + 1]).then_inc(done, 1)

    def norm_dve(v, squares, root, xn_ready):
        ask, got = root
        v.wait_ge(squares, NT)
        ask(v.tensor_scalar(rstd, ss, 1.0 / D_MODEL, EPS, ALU.mult, ALU.add))
        got()
        for t in range(NT):
            v.tensor_scalar(XN[:, t], X[:, t], rstd[:, t:t + 1], None, ALU.mult).then_inc(xn_ready, 1)

    def transpose_pe(pe, src, ready, turned, banks):
        pe.wait_ge(ready, NT)
        for c in range(KC):
            for t in range(NT):
                ins = pe.transpose(banks[c // 2][:, (c % 2) * SEQ + t * P:(c % 2) * SEQ + (t + 1) * P],
                                   src[:, t].rearrange("p (f c) -> p c f", c=KC)[:, c], ident)
            if c % 2:
                ins.then_inc(turned, 1)

    def scaled_act(act, turned, gain, done, banks):
        for j in (0, 2):
            act.wait_ge(turned, j + 1)
            for c in (2 * j, 2 * j + 1):
                ins = act.activation(HT[:, c], banks[j][:, (c % 2) * SEQ:(c % 2 + 1) * SEQ], ACT.Copy,
                                     scale=1.0 if gain is None else gain[:, c:c + 1])
            ins.then_inc(done, 1)

    def scaled_dve(v, turned, gain, done, banks):
        for j in (1, 3):
            v.wait_ge(turned, j + 1)
            for c in (2 * j, 2 * j + 1):
                src = banks[j][:, (c % 2) * SEQ:(c % 2 + 1) * SEQ]
                if gain is None:
                    ins = v.tensor_copy(HT[:, c], src)
                else:
                    ins = v.tensor_scalar(HT[:, c], src, gain[:, c:c + 1], None, ALU.mult)
            ins.then_inc(done, 1)

    s_x, s_cst = (top.enter_context(nc.semaphore(n)) for n in ("x_landed", "constants_landed"))
    with nc.Block() as block:
        @block.sync
        def _(sp):
            sp.dma_start(X, x.rearrange("b (t p) d -> p (b t) d", p=P)).then_inc(s_x, 16)
            sp.dma_start(cst[:, :], consts).then_inc(s_cst, 16)

    with nc.Fori(0, depth) as l:
        a_squares, a_asked, a_root, a_xn, a_turned, a_done = sem("a_squares"), sem("a_root_asked"), sem("a_root"), sem("a_xn"), sem("a_turned"), sem("a_done")
        a_par, a_late, a_convt = sem("a_params"), sem("a_late_params"), sem("a_convT")
        with nc.Block() as block:
            @block.sync
            def _(sp):
                one = bass.ds(l, 1)
                early = [
                    (g_attn, attn_norm_w[one].rearrange("o (p c) -> p (o c)", c=KC)),
                    (convrows[0:60], gdn_conv_w[one].rearrange("o k (c p) -> (o k c) p", p=P)),
                    (qn_w, gqa_q_norm_w[one].broadcast_to([P, 64])),
                    (kn_w, gqa_k_norm_w[one].broadcast_to([P, 64])),
                    (wba, w_in[one, :, C_BA:C_BA + 16].rearrange("o (p c) n -> p (o c) n", c=KC)),
                ]
                late = [
                    (g_ffn, ffn_norm_w[one].rearrange("o (p c) -> p (o c)", c=KC)),
                    (dt_bias, gdn_dt_bias[one].rearrange("o d h -> o (d h)").broadcast_to([P, 8])),
                    (a_log, gdn_a_log[one].rearrange("o d h -> o (d h)").broadcast_to([P, 8])),
                    (n_gdn, gdn_norm_w[one].rearrange("o p -> p o")),
                    (n_diff, diff_norm_w[one].rearrange("o p -> p o")),
                    (lamv_flat, diff_lambda[one].rearrange("o k d -> o (k d)").broadcast_to([P, 256])),
                    (rw[:, :, 0:N_GROUPS], router_group_w[one].rearrange("o (p c) n -> p (o c) n", c=KC)),
                    (rw[:, :, N_GROUPS:], router_expert_w[one].rearrange("o (p c) n -> p (o c) n", c=KC)),
                    (rb[:, 0:N_GROUPS], router_group_b[one].broadcast_to([P, N_GROUPS])),
                    (rb[:, N_GROUPS:], router_expert_b[one].broadcast_to([P, N_EXPERTS])),
                ]
                for dst, src in early:
                    sp.dma_start(dst, src).then_inc(a_par, 16)
                for u in range(2):
                    load_unit(sp, l, u)
                for dst, src in late:
                    sp.dma_start(dst, src).then_inc(a_late, 16)
                for u in range(2, RING):
                    load_unit(sp, l, u)
                sp.wait_ge(a_par, 16 * len(early))

            @block.scalar
            def _(act):
                act.wait_ge(s_x, 16)
                norm_act(act, a_squares)
                act.wait_ge(a_par, 16 * 5)
                scaled_act(act, a_turned, g_attn, a_done, ps[0:4])

            @block.vector
            def _(v):
                v.wait_ge(s_x, 16)
                norm_dve(v, a_squares, root_asker(v, a_asked, a_root), a_xn)
                v.wait_ge(a_par, 16 * 5)
                scaled_dve(v, a_turned, g_attn, a_done, ps[0:4])
                v.wait_ge(a_convt, 1)
                v.tensor_copy(convw, ps[4][:, 0:60])

            @block.gpsimd
            def _(pool):
                pool.wait_ge(s_cst, 16)
                roots(pool, a_asked, a_root, [rstd])
                for name in expert_sems:
                    pool.sem_clear(names[name])

            @block.tensor
            def _(pe):
                pe.wait_ge(s_cst, 16)
                transpose_pe(pe, XN, a_xn, a_turned, ps[0:4])
                pe.wait_ge(a_par, 16 * 5)
                pe.transpose(ps[4][:, 0:60], convrows[0:60], ident[0:60, 0:60]).then_inc(a_convt, 1)

        b_proj, b_free, b_rope, b_turned, b_out = sem("b_proj"), sem("b_free"), sem("b_rope"), sem("b_turned"), sem("b_out")
        b_chain, b_sq, b_ba, b_dvc, b_asked, b_root = sem("b_chain"), sem("b_squares"), sem("b_ba"), sem("b_dv_copied"), sem("b_root_asked"), sem("b_root")
        items = [(u, t) for u in (U_DQ, U_DK, U_DV, U_CQ, U_CKV) for t in range(NT)]
        roped = [i for i, (u, t) in enumerate(items) if u != U_DV]
        width = {U_CKV: 256}
        used_at.update({u: (b_proj, NT * (n + 1)) for n, u in enumerate((U_DQ, U_DK, U_DV, U_CQ, U_CKV))})
        with nc.Block() as block:
            @block.sync
            def _(sp):
                for u in range(RING, RING + 5):
                    load_unit(sp, l, u)
                sp.wait_ge(a_late, 16 * 10)

            @block.tensor
            def _(pe):
                def heads(i):
                    n = roped.index(i)
                    u, t = items[i]
                    pe.wait_ge(b_rope, n + 1)
                    if n >= 2:
                        pe.wait_ge(b_out, n - 1)
                    for j in range(2 if u == U_CKV else HEADS):
                        ins = pe.transpose(ps[4 + n % 2][:, j * P:(j + 1) * P],
                                           rope_b[:, n % 2, j * P:(j + 1) * P], ident)
                    ins.then_inc(b_turned, 1)

                for i, (u, t) in enumerate(items):
                    if t == 0:
                        unit_landed(pe, u)
                    if i >= 4:
                        pe.wait_ge(b_free, i - 3)
                    n = width.get(u, 512)
                    for c in range(KC):
                        ins = pe.matmul(ps[i % 4][:, 0:n], HT[:, c, t * P:(t + 1) * P], unit8(u)[:, c, 0:n],
                                        start=(c == 0), stop=(c == KC - 1))
                    ins.then_inc(b_proj, 1)
                    if i == 0:
                        for tt in range(NT):
                            for c in range(KC):
                                ins2 = pe.matmul(ps[6][:, tt * 16:(tt + 1) * 16], HT[:, c, tt * P:(tt + 1) * P], wba[:, c],
                                                 start=(c == 0), stop=(c == KC - 1))
                        ins2.then_inc(b_ba, 1)
                    if i - 1 in roped:
                        heads(i - 1)
                heads(len(items) - 1)

            @block.scalar
            def _(act):
                def heads_out(i):
                    n = roped.index(i)
                    u, t = items[i]
                    dst = {U_DQ: dqT, U_DK: dkT, U_CQ: cqT, U_CKV: ckT}[u]
                    nh = 2 if u == U_CKV else HEADS
                    act.wait_ge(b_turned, n + 1)
                    act.activation(dst[:, :, t * P:(t + 1) * P],
                                   ps[4 + n % 2][:, 0:nh * P].rearrange("p (j q) -> p j q", j=nh), ACT.Copy).then_inc(b_out, 1)

                for i, (u, t) in enumerate(items):
                    if u in (U_CQ, U_CKV):
                        act.wait_ge(b_proj, i + 1)
                        n = 512 if u == U_CQ else 128
                        m = i - items.index((U_CQ, 0))
                        if m >= 2:
                            act.wait_ge(b_rope, roped.index(i) - 1)
                        act.activation(squares[:, m % 2, 0:n], ps[i % 4][:, 0:n], ACT.Square).then_inc(b_sq, 1)
                    if u == U_DV:
                        act.wait_ge(b_proj, i + 1)
                        act.activation(dv[:, t], ps[i % 4][:, :], ACT.Copy).then_inc(b_dvc, 1)
                    if i - 1 in roped and i >= 1:
                        heads_out(i - 1)
                heads_out(len(items) - 1)

            @block.vector
            def _(v):
                link = chain(v, b_chain)
                ask, got = root_asker(v, b_asked, b_root)
                n_sq = 0
                for i, (u, t) in enumerate(items):
                    src = ps[i % 4]
                    v.wait_ge(b_proj, i + 1)
                    if u == U_DV:
                        v.wait_ge(b_dvc, t + 1)
                        v.sem_inc(b_free, 1)
                        continue
                    n = roped.index(i)
                    if n >= 2:
                        v.wait_ge(b_turned, n - 1)
                    ra, rb_ = rope_a[:, n % 2], rope_b[:, n % 2]
                    if u in (U_DQ, U_DK):
                        cos = cst[:, K_COSD + t * 64:K_COSD + (t + 1) * 64]
                        sin = cst[:, K_SIND + t * 64:K_SIND + (t + 1) * 64]
                        s4 = src[:, :].rearrange("p (h a d) -> p h a d", a=2, d=32)
                        r4 = rb_.rearrange("p (h a d) -> p h a d", a=2, d=32)
                        for a in range(2):
                            v.tensor_tensor(r4[:, :, a], s4[:, :, 1 - a],
                                            bcast(sin[:, a * 32:(a + 1) * 32].unsqueeze(1), [P, 8, 32]), ALU.mult)
                        v.tensor_tensor(ra.rearrange("p (h d) -> p h d", d=64), src[:, :].rearrange("p (h d) -> p h d", d=64),
                                        bcast(cos.unsqueeze(1), [P, 8, 64]), ALU.mult).then_inc(b_free, 1)
                        v.wait_ge(b_free, i + 1)
                        v.tensor_tensor(rb_, rb_, ra, ALU.add).then_inc(b_rope, 1)
                    else:
                        nh = 8 if u == U_CQ else 2
                        w = qn_w if u == U_CQ else kn_w
                        cos = cst[:, K_COSG + t * 64:K_COSG + (t + 1) * 64]
                        sin = cst[:, K_SING + t * 64:K_SING + (t + 1) * 64]
                        n_sq += 1
                        qw = gqn[:, n % 2, 0:nh * 64]
                        v.wait_ge(b_sq, n_sq)
                        v.tensor_tensor(qw.rearrange("p (h d) -> p h d", d=64), src[:, 0:nh * 64].rearrange("p (h d) -> p h d", d=64),
                                        bcast(w.unsqueeze(1), [P, nh, 64]), ALU.mult)
                        if u == U_CKV:
                            v.tensor_copy(cv[:, t], src[:, 128:256])
                        link(v.tensor_reduce(hss[:, 0:nh], squares[:, (n_sq - 1) % 2, 0:nh * 64].rearrange("p (h d) -> p h d", d=64), AX.X, ALU.add))
                        v.sem_inc(b_free, 1)
                        ask(v.tensor_scalar(hrs[:, 0:nh], hss[:, 0:nh], 1.0 / 64, EPS, ALU.mult, ALU.add))
                        tmp = gqa_tmp[:, 0:nh * 64]
                        sin4 = sin.rearrange("p (g a d) -> p g a d", a=2, d=16)
                        for a in range(2):
                            for g in range(2):
                                ins = v.tensor_tensor(tmp.rearrange("p (h g a d) -> p h g a d", g=2, a=2, d=16)[:, :, g, a],
                                                qw.rearrange("p (h g a d) -> p h g a d", g=2, a=2, d=16)[:, :, g, 1 - a],
                                                bcast(sin4[:, g, a].unsqueeze(1), [P, nh, 16]), ALU.mult)
                        link(ins)
                        link(v.tensor_tensor(qw.rearrange("p (h d) -> p h d", d=64), qw.rearrange("p (h d) -> p h d", d=64),
                                             bcast(cos.unsqueeze(1), [P, nh, 64]), ALU.mult))
                        link(v.tensor_tensor(tmp, tmp, qw, ALU.add))
                        got()
                        if u == U_CQ:
                            v.tensor_tensor(rb_.rearrange("p (h d) -> p h d", d=64), tmp.rearrange("p (h d) -> p h d", d=64),
                                            bcast(hrs[:, 0:8].unsqueeze(2), [P, 8, 64]), ALU.mult).then_inc(b_rope, 1)
                        else:
                            for a in range(2):
                                ins = v.tensor_tensor(rb_[:, 0:256].rearrange("p (h a d) -> p h a d", a=2, d=64)[:, :, a],
                                                      tmp.rearrange("p (h d) -> p h d", d=64),
                                                      bcast(hrs[:, 0:2].unsqueeze(2), [P, 2, 64]), ALU.mult)
                            ins.then_inc(b_rope, 1)
                v.wait_ge(b_ba, 1)
                v.tensor_copy(bar, ps[6][:, 0:32].rearrange("p (t n) -> p t n", t=NT))

            @block.gpsimd
            def _(pool):
                roots(pool, b_asked, b_root, [hrs[:, 0:8], hrs[:, 0:8], hrs[:, 0:2], hrs[:, 0:2]])

        c_score, c_max, c_exp, c_prob = sem("c_scores"), sem("c_max"), sem("c_exp"), sem("c_probs")
        c_turned, c_pT, c_pv, c_y, c_chain, c_achain = (sem("c_" + n) for n in ("turned", "probsT", "pv", "y", "chain", "act_chain"))
        d_fill, d_empty, d_conv, d_silu, d_sq, d_norm, d_zero = (sem("d_" + n) for n in ("fill", "empty", "conv", "silu", "squares", "norm", "zero"))
        d_asked, d_root = sem("d_root_asked"), sem("d_root")
        g_dve, g_act = sem("g_dve"), sem("g_act")
        STEPS = 8
        first_fill = [s if s < 4 else 4 + 2 * (s - 4) for s in range(STEPS + 1)]
        pieces = [[("proj", 0, 0), ("proj", 0, 1)], [("proj", 1, 0), ("proj", 1, 1)], [("proj", 2, 0), ("tok", 0, 0), ("tok", 0, 1)],
                  [("tok", 1, 0), ("tok", 1, 1)], [("proj", 2, 1)], [], [("back", 0, 0), ("back", 0, 1)],
                  [("tok", 2, 0), ("tok", 2, 1), ("back", 1, 0), ("back", 1, 1)]]
        fills_at = {k: n for n, k in enumerate(k for step in pieces for k in step)}

        def filled(kind, g):
            return fills_at[kind, g, 1] + 1

        tok = (qtok, ktok, vtok)
        used_at.update({U_GQ + g: (d_fill, filled("proj", g)) for g in range(3)})
        with nc.Block() as block:
            @block.sync
            def _(sp):
                for u in range(RING + 5, RING + 8):
                    load_unit(sp, l, u)

            @block.tensor
            def _(pe):
                def scores(s):
                    if s >= 2:
                        pe.wait_ge(c_exp, s - 1)
                    for m in range(2):
                        half = slice(64 * m, 64 * m + 64)
                        q, k = (dqT[half, s], dkT[half, s]) if s < 4 else (cqT[half, s - 4], ckT[half, (s - 4) // 2])
                        for t in range(NT):
                            ins = pe.matmul(ps[2 * (s % 2) + m][:, t * SEQ:(t + 1) * SEQ], q[:, t * P:(t + 1) * P], k,
                                            start=True, stop=True)
                    ins.then_inc(c_score, 1)

                def turn(s, m, f):
                    pe.wait_ge(c_prob, s + 1)
                    if f:
                        pe.wait_ge(c_pT, f)
                    for t in range(NT):
                        for kt in range(NT):
                            ins = pe.transpose(ps[4][:, kt * SEQ + t * P:kt * SEQ + (t + 1) * P],
                                               probs[:, s % 2, m, t, kt * P:(kt + 1) * P], ident)
                    ins.then_inc(c_turned, 1)

                def weighted(s, m, f):
                    pe.wait_ge(c_pT, f + 1)
                    if s:
                        pe.wait_ge(c_y, s)
                    for t in range(NT):
                        for kt in range(NT):
                            if s < 4:
                                o, val = ps[5][:, t * P:(t + 1) * P], dv[:, kt, s * P:(s + 1) * P]
                            else:
                                kv = (s - 4) // 2
                                o, val = ps[5][:, (2 * t + m) * 64:(2 * t + m + 1) * 64], cv[:, kt, kv * 64:(kv + 1) * 64]
                            ins = pe.matmul(o, probsT[:, f % 2, kt, t * P:(t + 1) * P], val, start=(kt == 0), stop=(kt == NT - 1))
                    ins.then_inc(c_pv, 1)

                def fill(kind, g, w):
                    f = fills_at[kind, g, w]
                    bank = ps[6 + f % 2]
                    if f >= 2:
                        pe.wait_ge(d_empty, f - 1)
                    if kind == "proj":
                        if w == 0:
                            unit_landed(pe, U_GQ + g)
                        for h in (2 * w, 2 * w + 1):
                            for c in range(KC):
                                ins = pe.matmul(bank[:, (h % 2) * SEQ:(h % 2 + 1) * SEQ],
                                                unit8(U_GQ + g)[:, c, h * DH:(h + 1) * DH], HT[:, c],
                                                start=(c == 0), stop=(c == KC - 1))
                    elif kind == "tok":
                        pe.wait_ge(d_silu, g + 1)
                        for h in range(HEADS):
                            ins = pe.transpose(bank[:, h * DH:(h + 1) * DH], conv[:, g % 2, h, w * P:(w + 1) * P], ident)
                    else:
                        pe.wait_ge(d_norm, g + 1)
                        for h in range(HEADS):
                            ins = pe.transpose(bank[:, h * P:(h + 1) * P], tok[g][:, w, h], ident)
                    ins.then_inc(d_fill, 1)

                scores(0)
                scores(1)
                before = None
                for s in range(STEPS):
                    for piece in pieces[s]:
                        fill(*piece)
                    for m in range(1 if s < 4 else 2):
                        turn(s, m, first_fill[s] + m)
                        if m == 0 and s + 2 < STEPS:
                            scores(s + 2)
                        if before is not None:
                            weighted(*before)
                        before = (s, m, first_fill[s] + m)
                weighted(*before)

            @block.scalar
            def _(act):
                alink = chain(act, c_achain)
                act.activation(beta.rearrange("p d t h -> p t d h"), bar[:, :, 0:8].rearrange("p t (d h) -> p t d h", d=2),
                               ACT.Sigmoid)
                act.activation(aexp, a_log, ACT.Exp).then_inc(g_act, 1)
                act.wait_ge(g_dve, 1)
                act.activation(lexp, lsum, ACT.Exp)
                act.activation(sp_b, sp_b, ACT.Exp, scale=-1.0).then_inc(g_act, 1)
                act.wait_ge(g_dve, 2)
                act.activation(sp_b, sp_b, ACT.Ln).then_inc(g_act, 1)

                def exps(s):
                    act.wait_ge(c_max, s + 1)
                    if s >= 2:
                        act.wait_ge(c_turned, first_fill[s - 1])
                    for m in range(2):
                        for t in range(NT):
                            ins = act.activation(probs[:, s % 2, m, t], ps[2 * (s % 2) + m][:, t * SEQ:(t + 1) * SEQ], ACT.Exp,
                                                 bias=nmx[:, s % 2, 2 * m + t:2 * m + t + 1], scale=SCALE,
                                                 accum_out=rsum[:, s % 2, 2 * m + t:2 * m + t + 1])
                    ins.then_inc(c_exp, 1)

                def empty(kind, g, w):
                    f = fills_at[kind, g, w]
                    act.wait_ge(d_fill, f + 1)
                    bank = ps[6 + f % 2]
                    if kind == "proj":
                        if g == 2 and w == 0:
                            act.wait_ge(d_conv, 2)
                        dst, src = pad[:, g % 2, 2 * w:2 * w + 2, 2:2 + SEQ], bank[:, :].rearrange("p (h t) -> p h t", h=2)
                    elif kind == "tok":
                        dst, src = tok[g][:, w], bank[:, :].rearrange("p (h d) -> p h d", h=HEADS)
                    else:
                        if g == 0 and w == 0:
                            act.wait_ge(d_conv, 6)
                        dst, src = (QT, KT)[g][:, :, w * P:(w + 1) * P], bank[:, :].rearrange("p (h t) -> p h t", h=HEADS)
                    act.activation(dst, src, ACT.Copy).then_inc(d_empty, 1)

                def silu(g):
                    act.wait_ge(d_conv, 2 * g + 2)
                    act.activation(conv[:, g % 2], conv[:, g % 2], ACT.Silu).then_inc(d_silu, 1)

                def square(g):
                    act.wait_ge(d_empty, filled("tok", g))
                    act.activation(conv_flat[:, g % 2], tok[g].rearrange("p t h d -> p (t h d)"),
                                   ACT.Square).then_inc(d_sq, 1)

                silu_early, silu_late = {1: 0, 2: 1}, {5: 2}
                exps(0)
                exps(1)
                for s in range(STEPS):
                    for piece in pieces[s]:
                        empty(*piece)
                        if piece in (("tok", 0, 1), ("tok", 1, 1)):
                            square(piece[1])
                    if s in silu_early:
                        silu(silu_early[s])
                    for m in range(1 if s < 4 else 2):
                        f = first_fill[s] + m
                        act.wait_ge(c_turned, f + 1)
                        if f >= 2:
                            act.wait_ge(c_pv, f - 1)
                        act.activation(probsT[:, f % 2].rearrange("p k q -> p (k q)"), ps[4][:, :], ACT.Copy).then_inc(c_pT, 1)
                    if s + 2 < STEPS:
                        exps(s + 2)
                    if s in silu_late:
                        silu(silu_late[s])

            @block.vector
            def _(v):
                link = chain(v, c_chain)
                ask, got = root_asker(v, d_asked, d_root)
                for b in range(2):
                    v.memset(pad[:, b, :, 0:2], 0.0)
                    v.memset(pad[:, b, :, SEQ + 2:SEQ + 4], 0.0)
                link(v.tensor_tensor(lprod, lamv[:, :, 0], lamv[:, :, 1], ALU.mult))
                v.tensor_reduce(lsum, lprod, AX.X, ALU.add)
                link(v.tensor_tensor(sp_a.rearrange("p d t h -> p t d h"), bar[:, :, 8:16].rearrange("p t (d h) -> p t d h", d=2),
                                     bcast(dt_bias.rearrange("p (d h) -> p d h", d=2).unsqueeze(1), [P, NT, 2, HEADS]), ALU.add))
                v.scalar_tensor_tensor(sp_b, sp_a, -1.0, sp_a, ALU.mult, ALU.max).then_inc(g_dve, 1)

                def maxima(s):
                    v.wait_ge(c_score, s + 1)
                    for m in range(2):
                        ins = v.tensor_reduce(mx[:, s % 2, 2 * m:2 * m + 2],
                                              ps[2 * (s % 2) + m][:, :].rearrange("p (t k) -> p t k", t=NT), AX.X, ALU.max)
                    link(ins)
                    v.tensor_scalar(nmx[:, s % 2], mx[:, s % 2], -SCALE, None, ALU.mult).then_inc(c_max, 1)

                maxima(0)
                maxima(1)
                v.wait_ge(g_act, 2)
                link(v.tensor_scalar(sp_b, sp_b, 1.0, None, ALU.add))
                v.sem_inc(g_dve, 1)
                link(v.tensor_tensor(nlam, lexp[:, 1:2], lexp[:, 0:1], ALU.subtract))
                link(v.tensor_tensor(nlam, nlam, cst[:, bass.ds(l * 2 + K_LAM, 1)], ALU.subtract))
                v.wait_ge(g_act, 3)
                link(v.scalar_tensor_tensor(sp_a, sp_a, 0.0, sp_b, ALU.max, ALU.add))
                for t in range(NT):
                    ins = v.tensor_tensor(gg[:, :, t], sp_a[:, :, t], aexp.rearrange("p (d h) -> p d h", d=2), ALU.mult)
                link(ins)
                v.tensor_scalar(gg, gg, -1.0, None, ALU.mult)

                def convolve(g, w):
                    v.wait_ge(d_empty, fills_at["proj", g, w] + 1)
                    if g == 2:
                        v.wait_ge(d_fill, filled("tok", 0))
                    for k in range(TAPS):
                        for h in (2 * w, 2 * w + 1):
                            cw = convw[:, k * 12 + g * HEADS + h:k * 12 + g * HEADS + h + 1]
                            src = pad[:, g % 2, h, k:k + SEQ]
                            if k == 0:
                                ins = v.tensor_scalar(conv[:, g % 2, h], src, cw, None, ALU.mult)
                            else:
                                ins = v.scalar_tensor_tensor(conv[:, g % 2, h], src, cw, conv[:, g % 2, h], ALU.mult, ALU.add)
                        if k < TAPS - 1:
                            link(ins)
                    ins.then_inc(d_conv, 1)

                def l2norm(g):
                    v.wait_ge(d_sq, g + 1)
                    link(v.tensor_reduce(qss, conv_flat[:, g % 2].rearrange("p (t h d) -> p t h d", t=NT, h=HEADS), AX.X, ALU.add))
                    ask(v.tensor_scalar(qrs, qss, EPS, None, ALU.add))
                    got()
                    if g == 0:
                        link(v.tensor_scalar(qrs, qrs, DH ** -0.5, None, ALU.mult))
                    v.tensor_tensor(tok[g], tok[g], bcast(qrs.unsqueeze(3), [P, NT, HEADS, DH]), ALU.mult).then_inc(d_norm, 1)

                def weigh(s):
                    b = s % 2
                    v.wait_ge(c_exp, s + 1)
                    if s >= 2:
                        v.wait_ge(c_y, s - 1)
                    if s >= 4:
                        v.reciprocal(rinv[:, b], rsum[:, b]).then_inc(c_prob, 1)
                        return
                    link(v.reciprocal(rinv[:, b], rsum[:, b]))
                    link(v.tensor_scalar(rl[:, b], rinv[:, b, 2:4], nlam, None, ALU.mult))
                    for t in range(NT):
                        ins = v.tensor_scalar(probs[:, b, 1, t], probs[:, b, 1, t], rl[:, b, t:t + 1], None, ALU.mult)
                    link(ins)
                    for t in range(NT):
                        ins = v.scalar_tensor_tensor(probs[:, b, 0, t], probs[:, b, 0, t], rinv[:, b, t:t + 1], probs[:, b, 1, t],
                                                     ALU.mult, ALU.add)
                    ins.then_inc(c_prob, 1)

                work = {0: [(convolve, 0, 0), (convolve, 0, 1)], 1: [(convolve, 1, 0), (convolve, 1, 1)], 2: [(l2norm, 0)],
                        3: [(convolve, 2, 0)], 4: [(convolve, 2, 1)], 5: [(l2norm, 1)]}
                weigh(0)
                for s in range(STEPS):
                    b = s % 2
                    if s + 1 < STEPS:
                        weigh(s + 1)
                    if s + 2 < STEPS:
                        maxima(s + 2)
                    for f, *args in work.get(s, []):
                        f(*args)
                    v.wait_ge(c_pv, first_fill[s + 1])
                    if s < 4:
                        v.tensor_copy(yb[:, :, s * P:(s + 1) * P], ps[5][:, 0:SEQ].rearrange("p (t e) -> p t e", t=NT)).then_inc(c_y, 1)
                    else:
                        v.wait_ge(c_prob, s + 1)
                        for m in range(2):
                            h = 2 * (s - 4) + m
                            ins = v.tensor_tensor(yc[:, :, h * 64:(h + 1) * 64],
                                                  ps[5][:, 0:256].rearrange("p (t m e) -> p t m e", t=NT, m=2)[:, :, m],
                                                  bcast(rinv[:, b, 2 * m:2 * m + 2].unsqueeze(2), [P, NT, 64]), ALU.mult)
                        ins.then_inc(c_y, 1)

            @block.gpsimd
            def _(pool):
                roots(pool, d_asked, d_root, [qrs, qrs])

        e_gc, e_gcc, e_gr, e_kk, e_d, e_e, e_m = (sem("e_" + n) for n in ("gc", "gc_copied", "gc_rows", "kk", "diff", "exp", "masked"))
        e_lt, e_y, e_ym, e_z, e_upd, e_chain = (sem("e_" + n) for n in ("lt", "y", "ym", "z", "updated", "chain"))
        e_u, e_v, e_kd, e_s, e_sc, e_ks, e_r, e_o, e_oa, e_osq, e_small, e_int = (
            sem("e_" + n) for n in ("u", "v", "kd", "s", "s_copied", "ks", "r", "o", "oa", "osq", "small", "qk_masked"))
        e_asked, e_root = sem("e_root_asked"), sem("e_root")
        ybank = [ps[1], ps[2], ps[3], ps[4]]
        zbank, tbank = [ps[5], ps[6]], [ps[7], ps[0]]
        e_t, e_dt = sem("e_inverse_turned"), sem("e_dt")
        kkbank, qkbank = [ps[5], ps[6]], [ps[7], ps[0]]

        def heads3(bank):
            return bank[:, :].rearrange("p (h i) -> p h i", h=HEADS)

        def per_head(cols):
            return bcast(cols.unsqueeze(2), [P, HEADS, P])

        def columns(m, direction, n):
            if len(m.shape) == 2:
                return m.rearrange("p (b a s) -> p b a s", a=2, s=1 << n)[:, :, direction]
            return m.rearrange("p h (b a s) -> p h b a s", a=2, s=1 << n)[:, :, :, direction]

        def all_heads(m):
            return bcast(m.unsqueeze(1), [P, HEADS, P])

        with nc.Block() as block:
            @block.tensor
            def _(pe):
                def turn_inverse(k):
                    G = k % 4
                    pe.wait_ge(e_upd, k + 1)
                    if k >= 2:
                        pe.wait_ge(e_dt, k - 1)
                    for h in range(HEADS):
                        ins = pe.transpose(tbank[G % 2][:, h * P:(h + 1) * P], DI[:, G, h], ident)
                    ins.then_inc(e_t, 1)

                for d in range(2):
                    pe.matmul(ps[0][:, 8 * d:8 * d + 8], cum[d], gg[:, d].rearrange("p t h -> p (t h)"), start=True, stop=True)
                pe.matmul(ps[0][:, 16:32], ones, gg.rearrange("p d t h -> p (d t h)"), start=True, stop=True).then_inc(e_gc, 1)
                for G in range(4):
                    d, t = divmod(G, 2)
                    for h in range(HEADS):
                        ins = pe.matmul(ybank[G][:, h * P:(h + 1) * P], bcast(gg[:, d, t, h:h + 1], [P, P]), cum[d],
                                        start=True, stop=True)
                    ins.then_inc(e_gr, 1)
                for t in range(NT):
                    for h in range(HEADS):
                        k = KT[:, h, t * P:(t + 1) * P]
                        ins = pe.matmul(kkbank[t][:, h * P:(h + 1) * P], k, k, start=True, stop=True)
                    ins.then_inc(e_kk, 1)
                pe.wait_ge(e_gcc, 1)
                for t in range(NT):
                    for h in range(HEADS):
                        ins = pe.matmul(qkbank[t][:, h * P:(h + 1) * P], KT[:, h, t * P:(t + 1) * P], QT[:, h, t * P:(t + 1) * P],
                                        start=True, stop=True)
                    ins.then_inc(e_kk, 1)
                for G in range(4):
                    pe.wait_ge(e_lt, G + 1)
                    for h in range(HEADS):
                        ins = pe.transpose(ybank[G][:, h * P:(h + 1) * P], LT[:, G, h], ident)
                    ins.then_inc(e_y, 1)
                pe.wait_ge(e_int, 1)
                for G in range(4):
                    turn_inverse(G)
                for n in range(1, LEVELS):
                    for G in range(4):
                        k = 4 * n + G
                        pe.wait_ge(e_upd, k - 3)
                        for h in range(HEADS):
                            ins = pe.matmul(ybank[G][:, h * 64:(h + 1) * 64], LT[:, G, h], columns(DI[:, G, h], G // 2, n),
                                            start=True, stop=True)
                        ins.then_inc(e_y, 1)
                    for G in range(4):
                        k = 4 * n + G
                        pe.wait_ge(e_ym, k - 3)
                        pe.wait_ge(e_dt, k - 3)
                        pe.wait_ge(e_upd, k - 1)
                        for h in range(HEADS):
                            ins = pe.matmul(zbank[G % 2][:, h * 64:(h + 1) * 64], DT[:, G, h], YM[:, G, h], start=True, stop=True)
                        ins.then_inc(e_z, 1)
                        if G >= 1:
                            turn_inverse(k - 1)
                    turn_inverse(4 * n + 3)
                pe.wait_ge(e_dt, 4 * LEVELS)
                for d in range(2):
                    t = d
                    for h in range(HEADS):
                        ins = pe.matmul(ps[1 + d][:, h * P:(h + 1) * P], DT[:, 2 * d + t, h], vtok[:, t, h], start=True, stop=True)
                    ins.then_inc(e_u, 1)
                for d in range(2):
                    pe.wait_ge(e_v, d + 1)
                    pe.wait_ge(e_kd, d + 1)
                    for h in range(HEADS):
                        ins = pe.matmul(ps[3 + d][:, h * P:(h + 1) * P], kd[:, d, h], vn1[:, d, h], start=True, stop=True)
                    ins.then_inc(e_s, 1)
                for d in range(2):
                    t = 1 - d
                    pe.wait_ge(e_sc, d + 1)
                    for h in range(HEADS):
                        pe.matmul(ps[5 + d][:, h * P:(h + 1) * P], KT[:, h, t * P:(t + 1) * P], S1[:, d, h], start=True, stop=True)
                    for h in range(HEADS):
                        ins = pe.matmul(qkbank[d][:, h * P:(h + 1) * P], QT[:, h, t * P:(t + 1) * P], S1[:, d, h], start=True, stop=True)
                    ins.then_inc(e_ks, 1)
                for d in range(2):
                    t = 1 - d
                    pe.wait_ge(e_r, d + 1)
                    for h in range(HEADS):
                        ins = pe.matmul(ps[1 + d][:, h * P:(h + 1) * P], DT[:, 2 * d + t, h], R2[:, d, h], start=True, stop=True)
                    ins.then_inc(e_u, 1)
                pe.wait_ge(e_v, 4)
                for t in range(NT):
                    first, second = t, 1 - t
                    for h in range(HEADS):
                        pe.matmul(ps[3 + t][:, h * P:(h + 1) * P], INT[:, 2 * first + t, h], vn1[:, first, h], start=True, stop=False)
                        ins = pe.matmul(ps[3 + t][:, h * P:(h + 1) * P], INT[:, 2 * second + t, h], vn2[:, second, h],
                                        start=False, stop=True)
                    ins.then_inc(e_o, 1)

            @block.scalar
            def _(act):
                act.wait_ge(e_gcc, 1)
                act.activation(egc, gc, ACT.Exp)
                act.activation(kdec, kdec, ACT.Exp).then_inc(e_small, 1)
                for G in range(4):
                    act.wait_ge(e_d, G + 1)
                    act.activation(E[:, G], E[:, G], ACT.Exp).then_inc(e_e, 1)
                for k in range(4 * LEVELS):
                    act.wait_ge(e_t, k + 1)
                    act.activation(DT[:, k % 4], heads3(tbank[k % 2]), ACT.Copy).then_inc(e_dt, 1)
                for d in range(2):
                    act.wait_ge(e_s, d + 1)
                    act.activation(S1[:, d], heads3(ps[3 + d]), ACT.Copy).then_inc(e_sc, 1)
                act.wait_ge(e_oa, 2)
                act.activation(ysq.rearrange("p t n -> p (t n)"), oa.rearrange("p t h e -> p (t h e)"), ACT.Square).then_inc(e_osq, 1)

            @block.gpsimd
            def _(pool):
                pool.wait_ge(e_small, 1)
                for d in range(2):
                    pool.tensor_tensor(kd[:, d], ktok[:, d], per_head(kdec[:, 12 * d:12 * d + 4]),
                                       ALU.mult).then_inc(e_kd, 1)
                for G in range(4):
                    d, t = divmod(G, 2)
                    pool.wait_ge(e_e, G + 1)
                    pool.tensor_tensor(INT[:, G], E[:, G], all_heads(cum[d]), ALU.mult).then_inc(e_m, 1)
                roots(pool, e_asked, e_root, [yrs[:, 0:8]])

            @block.vector
            def _(v):
                link = chain(v, e_chain)
                ask, got = root_asker(v, e_asked, e_root)
                v.wait_ge(e_gc, 1)
                v.tensor_copy(gc, ps[0][:, 0:16])
                link(v.tensor_copy(gtot, ps[0][:, 16:32]))
                v.tensor_tensor(kdec, gtot, gc, ALU.subtract).then_inc(e_gcc, 1)
                for G in range(4):
                    v.wait_ge(e_gr, G + 1)
                    for h in range(HEADS):
                        ins = v.tensor_scalar(E[:, G, h], ybank[G][:, h * P:(h + 1) * P], gc[:, 4 * G + h:4 * G + h + 1], 0.0,
                                              ALU.subtract, ALU.min)
                    ins.then_inc(e_d, 1)
                v.wait_ge(e_kk, 2)
                for G in range(4):
                    d, t = divmod(G, 2)
                    v.wait_ge(e_e, G + 1)
                    for h in range(HEADS):
                        ins = v.scalar_tensor_tensor(LT[:, G, h], kkbank[t][:, h * P:(h + 1) * P], beta[:, d, t, h:h + 1], E[:, G, h],
                                                     ALU.mult, ALU.mult)
                    ins.then_inc(e_lt, 1)
                v.wait_ge(e_kk, 4)
                for G in range(4):
                    v.wait_ge(e_m, G + 1)
                    ins = v.tensor_tensor(INT[:, G], heads3(qkbank[G % 2]), INT[:, G], ALU.mult)
                ins.then_inc(e_int, 1)
                for G in range(4):
                    d, t = divmod(G, 2)
                    v.wait_ge(e_y, G + 1)
                    link(v.tensor_tensor(E[:, G], heads3(ybank[G]), all_heads(level0(d)), ALU.mult))
                    v.tensor_tensor(DI[:, G], all_heads(ident), E[:, G], ALU.subtract).then_inc(e_upd, 1)
                for n in range(1, LEVELS):
                    for G in range(4):
                        k = 4 * n + G
                        v.wait_ge(e_y, k + 1)
                        if n > 1:
                            v.wait_ge(e_z, k - 7)
                        v.tensor_tensor(YM[:, G], ybank[G][:, 0:256].rearrange("p (h i) -> p h i", h=HEADS),
                                        bcast(level(G // 2, n).unsqueeze(1), [P, HEADS, 64]), ALU.mult).then_inc(e_ym, 1)
                    for G in range(4):
                        k = 4 * n + G
                        v.wait_ge(e_z, k - 3)
                        v.wait_ge(e_t, k - 3)
                        d = columns(DI[:, G], G // 2, n)
                        v.tensor_tensor(d, d, zbank[G % 2][:, 0:256].rearrange("p (h b s) -> p h b s", h=HEADS, s=1 << n),
                                        ALU.subtract).then_inc(e_upd, 1)
                for d in range(2):
                    v.wait_ge(e_u, d + 1)
                    v.tensor_tensor(vn1[:, d], heads3(ps[1 + d]), per_head(beta[:, d, d]), ALU.mult).then_inc(e_v, 1)
                v.wait_ge(e_small, 1)
                for d in range(2):
                    t = 1 - d
                    G = 2 * d + t
                    v.wait_ge(e_ks, d + 1)
                    link(v.tensor_tensor(R2[:, d], heads3(ps[5 + d]), per_head(egc[:, 4 * G:4 * G + 4]), ALU.mult))
                    v.tensor_tensor(R2[:, d], vtok[:, t], R2[:, d], ALU.subtract).then_inc(e_r, 1)
                    v.tensor_tensor(qs[:, d], heads3(qkbank[d]), per_head(egc[:, 4 * G:4 * G + 4]), ALU.mult)
                for d in range(2):
                    v.wait_ge(e_u, d + 3)
                    v.tensor_tensor(vn2[:, d], heads3(ps[1 + d]), per_head(beta[:, d, 1 - d]), ALU.mult).then_inc(e_v, 1)
                for t in range(NT):
                    v.wait_ge(e_o, t + 1)
                    v.wait_ge(e_v, 4)
                    v.tensor_tensor(oa[:, t], heads3(ps[3 + t]), qs[:, 1 - t], ALU.add).then_inc(e_oa, 1)
                v.wait_ge(e_osq, 1)
                link(v.tensor_reduce(yss[:, 0:8], ysq.rearrange("p t (h e) -> p (t h) e", h=HEADS), AX.X, ALU.add))
                ask(v.tensor_scalar(yrs[:, 0:8], yss[:, 0:8], 1.0 / DH, EPS, ALU.mult, ALU.add))
                got()
                v.tensor_tensor(oa.rearrange("p t h e -> p (t h) e"), oa.rearrange("p t h e -> p (t h) e"),
                                bcast(yrs[:, 0:8].unsqueeze(2), [P, 8, DH]), ALU.mult)

        f_sq, f_yn, f_z, f_zs, f_ya, f_t, f_y, f_p, f_sig, f_m, f_chain = (
            sem("f_" + n) for n in ("squares", "y_normed", "z", "z_silu", "ya", "turned", "yT", "products", "gates", "merged", "chain"))
        f_asked, f_root = sem("f_root_asked"), sem("f_root")
        used_at[U_Z] = (f_z, NT)
        for k in range(3):
            used_at.update({U_GATE0[k]: (f_p, 4 * k + 2), U_BRANCH[k]: (f_p, 4 * k + 4), U_GATE1[k]: (f_p, 4 * k + 4)})
        merges = [(k, n, t) for k in range(3) for n in range(2) for t in range(NT)]
        with nc.Block() as block:
            @block.sync
            def _(sp):
                for u in range(RING + 8, N_FIXED):
                    load_unit(sp, l, u)
                for n in range(2, RING):
                    sp.wait_ge(*used_at[last_unit(n)])
                    load_expert(sp, l, n // 3, n)

            @block.tensor
            def _(pe):
                def turn(src, banks):
                    for h in range(HEADS):
                        for t in range(NT):
                            ins = pe.transpose(banks[h // 2][:, (h % 2) * SEQ + t * P:(h % 2) * SEQ + (t + 1) * P],
                                               src[:, t, h * P:(h + 1) * P], ident)
                    ins.then_inc(f_t, 1)

                unit_landed(pe, U_Z)
                for t in range(NT):
                    for c in range(KC):
                        ins = pe.matmul(ps[t][:, :], HT[:, c, t * P:(t + 1) * P], unit8(U_Z)[:, c], start=(c == 0), stop=(c == KC - 1))
                    ins.then_inc(f_z, 1)
                turn(yc, ps[2:4])
                pe.wait_ge(f_yn, 1)
                turn(yb, ps[4:6])
                pe.wait_ge(f_ya, 1)
                turn(oa.rearrange("p t h e -> p t (h e)"), ps[6:8])
                pe.wait_ge(f_y, 3)
                for i, (k, n, t) in enumerate(merges):
                    pair = 2 * (i % 3)
                    gate = (U_GATE0, U_GATE1)[n][k]
                    if i >= 3:
                        pe.wait_ge(f_m, i - 2)
                    unit_landed(pe, U_BRANCH[k])
                    unit_landed(pe, gate)
                    w = slot(U_BRANCH[k]).rearrange("p (c n) -> p c n", c=HEADS)
                    for c in range(HEADS):
                        pe.matmul(ps[pair][:, :], yT[ORDER[k]][:, c, t * P:(t + 1) * P], w[:, c, n * 512:(n + 1) * 512],
                                  start=(c == 0), stop=(c == HEADS - 1))
                    for c in range(KC):
                        ins = pe.matmul(ps[pair + 1][:, :], HT[:, c, t * P:(t + 1) * P], unit8(gate)[:, c],
                                        start=(c == 0), stop=(c == KC - 1))
                    ins.then_inc(f_p, 1)

            @block.scalar
            def _(act):
                act.activation(ysq.rearrange("p t n -> p (t n)"), yb.rearrange("p t n -> p (t n)"), ACT.Square).then_inc(f_sq, 1)
                for t in range(NT):
                    act.wait_ge(f_z, t + 1)
                    act.activation(zs[:, t], ps[t][:, :], ACT.Silu).then_inc(f_zs, 1)
                for n, (b, gain) in enumerate(((2, 1.0), (1, ndl), (0, n_gdn))):
                    act.wait_ge(f_t, n + 1)
                    for j in range(2):
                        ins = act.activation(yT[b][:, 2 * j:2 * j + 2].rearrange("p h t -> p (h t)"), ps[2 + 2 * n + j][:, :],
                                             ACT.Copy, scale=gain)
                    ins.then_inc(f_y, 1)
                for i in range(len(merges)):
                    act.wait_ge(f_p, i + 1)
                    if i >= 3:
                        act.wait_ge(f_m, i - 2)
                    act.activation(sig[:, i % 3], ps[2 * (i % 3) + 1][:, :], ACT.Sigmoid).then_inc(f_sig, 1)

            @block.vector
            def _(v):
                link = chain(v, f_chain)
                ask, got = root_asker(v, f_asked, f_root)
                v.wait_ge(f_sq, 1)
                link(v.tensor_reduce(yss[:, 0:8], ysq.rearrange("p t (h e) -> p (t h) e", h=HEADS), AX.X, ALU.add))
                ask(v.tensor_scalar(yrs[:, 0:8], yss[:, 0:8], 1.0 / DH, EPS, ALU.mult, ALU.add))
                v.tensor_tensor(ndl, n_diff, cst[:, bass.ds(l * 2 + (K_LAM + 1), 1)], ALU.mult)
                got()
                v.tensor_tensor(yb.rearrange("p t (h e) -> p (t h) e", h=HEADS), yb.rearrange("p t (h e) -> p (t h) e", h=HEADS),
                                bcast(yrs[:, 0:8].unsqueeze(2), [P, 8, DH]), ALU.mult).then_inc(f_yn, 1)
                v.wait_ge(f_zs, 2)
                v.tensor_tensor(oa.rearrange("p t h e -> p (t h e)"), oa.rearrange("p t h e -> p (t h e)"),
                                zs.rearrange("p t n -> p (t n)"), ALU.mult).then_inc(f_ya, 1)
                for i, (k, n, t) in enumerate(merges):
                    v.wait_ge(f_sig, i + 1)
                    bank = ps[2 * (i % 3)]
                    dst = merged[:, t, n * 512:(n + 1) * 512]
                    if k == 0:
                        v.tensor_tensor(dst, bank[:, :], sig[:, i % 3], ALU.mult).then_inc(f_m, 1)
                    else:
                        link(v.tensor_tensor(part[:, i % 2], bank[:, :], sig[:, i % 3], ALU.mult))
                        v.tensor_tensor(dst, dst, part[:, i % 2], ALU.add).then_inc(f_m, 1)

            @block.gpsimd
            def _(pool):
                roots(pool, f_asked, f_root, [yrs[:, 0:8]])

        h_t, h_tc, h_o, h_x, h_sq, h_xn, h_turned, h_done, h_chain = (
            sem("h_" + n) for n in ("turned", "turned_copied", "out", "residual", "squares", "xn", "turned2", "hT", "chain"))
        h_asked, h_root = sem("h_root_asked"), sem("h_root")
        used_at.update({U_OUT + n: (h_o, NT * (n + 1)) for n in range(2)})
        h_r, h_gm, h_ge, h_e1, h_ev, h_a, h_pos, h_mgood = (sem("h_" + n) for n in ("router", "group_max", "group_exp", "pair", "pair_exp", "assigned", "pos", "merged_ready"))
        with nc.Block() as block:
            @block.sync
            def _(sp):
                for n in range(RING, RING + 3):
                    if n == RING + 2:
                        sp.wait_ge(h_t, 4)
                    load_expert(sp, l, n // 3, n)
                for n in range(2):
                    sp.wait_ge(*used_at[last_unit(n)])
                    load_expert(sp, l, 0, n)

            @block.tensor
            def _(pe):
                for c in range(KC):
                    for t in range(NT):
                        ins = pe.transpose(ps[c // 2][:, (c % 2) * SEQ + t * P:(c % 2) * SEQ + (t + 1) * P],
                                           merged[:, t].rearrange("p (f c) -> p c f", c=KC)[:, c], ident)
                    if c % 2:
                        ins.then_inc(h_t, 1)
                pe.wait_ge(h_tc, 4)
                for n in range(2):
                    unit_landed(pe, U_OUT + n)
                    for t in range(NT):
                        for c in range(KC):
                            ins = pe.matmul(ps[4 + 2 * n + t][:, :], HT[:, c, t * P:(t + 1) * P], unit8(U_OUT + n)[:, c],
                                            start=(c == 0), stop=(c == KC - 1))
                        ins.then_inc(h_o, 1)
                for n in range(2):
                    for t in range(NT):
                        pe.wait_ge(h_x, 2 * n + t + 1)
                        pe.matmul(ps[2 * t + n][:, :], ident, X[:, t, n * 512:(n + 1) * 512], start=True, stop=True)
                transpose_pe(pe, XN, h_xn, h_turned, ps[4:8])
                pe.wait_ge(h_done, 4)
                for t in range(NT):
                    for c in range(KC):
                        ins = pe.matmul(ps[4][:, t * 36:(t + 1) * 36], HT[:, c, t * P:(t + 1) * P], rw[:, c], start=(c == 0), stop=(c == KC - 1))
                ins.then_inc(h_r, 1)
                pe.wait_ge(h_a, 1)
                pe.matmul(ps[5][:, 0:32], strict[0], assigned[:, 0], start=True, stop=True)
                pe.matmul(ps[5][:, 32:64], strict[0], assigned[:, 1], start=True, stop=False)
                pe.matmul(ps[5][:, 32:64], ones, assigned[:, 0], start=False, stop=True)
                pe.matmul(ps[5][:, 64:96], ones, assigned[:, 0], start=True, stop=False)
                pe.matmul(ps[5][:, 64:96], ones, assigned[:, 1], start=False, stop=True).then_inc(h_pos, 1)

            @block.scalar
            def _(act):
                scaled_act(act, h_t, None, h_tc, ps[0:4])
                act.wait_ge(h_x, 4)
                norm_act(act, h_sq)
                scaled_act(act, h_turned, g_ffn, h_done, ps[4:8])
                act.wait_ge(h_gm, 1)
                for t in range(NT):
                    ins = act.activation(gexp[:, t], logit[:, t, 0:4], ACT.Exp, bias=ngm[:, t:t + 1], accum_out=gsum[:, t:t + 1])
                ins.then_inc(h_ge, 1)
                act.wait_ge(h_e1, 1)
                act.activation(e1, e1, ACT.Exp).then_inc(h_ev, 1)

            @block.vector
            def _(v):
                link = chain(v, h_chain)
                v.memset(gpad, -3e38)
                scaled_dve(v, h_t, None, h_tc, ps[0:4])
                for n in range(2):
                    for t in range(NT):
                        v.wait_ge(h_o, 2 * n + t + 1)
                        dst = X[:, t, n * 512:(n + 1) * 512]
                        v.tensor_tensor(dst, dst, ps[4 + 2 * n + t][:, :], ALU.add).then_inc(h_x, 1)
                norm_dve(v, h_sq, root_asker(v, h_asked, h_root), h_xn)
                scaled_dve(v, h_turned, g_ffn, h_done, ps[4:8])
                v.wait_ge(h_r, 1)
                link(v.tensor_tensor(logit, ps[4][:, 0:72].rearrange("p (t n) -> p t n", t=NT), bcast(rb.unsqueeze(1), [P, NT, 36]), ALU.add))
                link(v.tensor_copy(gpad[:, :, 0:4], logit[:, :, 0:4]))
                for t in range(NT):
                    ins = v.max(gmax8[:, t], gpad[:, t])
                link(ins)
                v.tensor_scalar(ngm, gmax8[:, :, 0], -1.0, None, ALU.mult).then_inc(h_gm, 1)
                for t in range(NT):
                    ins = v.max_index(idx3[:, t], gmax8[:, t], gpad[:, t])
                link(ins)
                link(v.tensor_copy(idxf, idx3))
                for t in range(NT):
                    ins = v.tensor_scalar(goh[:, t], cst[:, K_IOTA:K_IOTA + 8], idxf[:, t, 0:1], None, ALU.is_equal)
                link(ins)
                link(v.tensor_scalar(goh, goh, -1.0, 1e30, ALU.add, ALU.mult))
                for t in range(NT):
                    ins = v.tensor_tensor(emask[:, t].rearrange("p (g e) -> p g e", g=N_GROUPS),
                                          logit[:, t, 4:36].rearrange("p (g e) -> p g e", g=N_GROUPS),
                                          bcast(goh[:, t, 0:4].unsqueeze(2), [P, N_GROUPS, PER_GROUP]), ALU.add)
                link(ins)
                for t in range(NT):
                    ins = v.max(etop[:, t], emask[:, t])
                link(ins)
                v.tensor_tensor(e1, etop[:, :, 1], etop[:, :, 0], ALU.subtract).then_inc(h_e1, 1)
                for t in range(NT):
                    ins = v.max_index(idx3[:, t], etop[:, t], emask[:, t])
                link(ins)
                link(v.tensor_copy(idxf, idx3))
                for t in range(NT):
                    v.tensor_scalar(hot0[:, t], cst[:, K_IOTA:K_IOTA + N_EXPERTS], idxf[:, t, 0:1], None, ALU.is_equal)
                    ins = v.tensor_scalar(hot1[:, t], cst[:, K_IOTA:K_IOTA + N_EXPERTS], idxf[:, t, 1:2], None, ALU.is_equal)
                link(ins)
                v.tensor_tensor(assigned, hot0, hot1, ALU.add).then_inc(h_a, 1)
                v.wait_ge(h_ge, 1)
                v.wait_ge(h_ev, 1)
                v.tensor_scalar(esum, e1, 1.0, None, ALU.add)
                link(v.reciprocal(gprob, gsum))
                link(v.reciprocal(esum, esum))
                link(v.tensor_tensor(w01[:, :, 0], gprob, esum, ALU.mult))
                link(v.tensor_tensor(w01[:, :, 1], w01[:, :, 0], e1, ALU.mult))
                for t in range(NT):
                    ins = v.tensor_scalar(hotw[:, t], hot0[:, t], w01[:, t, 0:1], None, ALU.mult)
                link(ins)
                for t in range(NT):
                    ins = v.scalar_tensor_tensor(weight[:, t], hot1[:, t], w01[:, t, 1:2], hotw[:, t], ALU.mult, ALU.add)
                link(ins)
                v.wait_ge(h_pos, 1)
                link(v.scalar_tensor_tensor(posn, ps[5][:, 0:64].rearrange("p (t e) -> p t e", t=NT), 1.0, assigned, ALU.add, ALU.mult))
                v.tensor_scalar(posn, posn, -1.0, None, ALU.add)
                link(v.tensor_copy(cnt[:, :], ps[5][:, 64:96]))
                link(v.tensor_tensor(over, bcast(cnt[:, :].unsqueeze(2), [P, N_EXPERTS, 8]),
                                     bcast(cst[:, K_THR:K_THR + 8].unsqueeze(1), [P, N_EXPERTS, 8]), ALU.is_gt))
                link(v.tensor_reduce(nbf[:, :], over, AX.X, ALU.add))
                link(v.tensor_scalar(nbf[:, :], nbf[:, :], 1.0, None, ALU.add))
                v.tensor_copy(nbi[:, :], nbf[:, :])

            @block.gpsimd
            def _(pool):
                roots(pool, h_asked, h_root, [rstd])

        bank_a, bank_b, bank_c, bank_d = ps[4:8]
        wg, wu, wd = [[expert_slot(3 * k + n) for k in range(SETS)] for n in range(3)]

        def jobs(eng, body):
            J = eng.alloc_register("jobs")
            eng.reg_mov(J, 1)

            def of_expert(i, k):
                n = eng.value_load(nbi[0:1, bass.ds(i * SETS + k, 1)], min_val=1, max_val=ROUNDS)
                with eng.Fori(0, n) as r:
                    body(eng.snap(J), i, k, r)
                    eng.reg_add(J, J, 1)

            with eng.Fori(0, N_EXPERTS // SETS) as i:
                for k in range(SETS):
                    of_expert(i, k)
            for k in range(N_EXPERTS % SETS):
                of_expert(N_EXPERTS // SETS, k)
            eng.free_register(J)

        with nc.Block() as block:
            @block.gpsimd
            def _(pool):
                for name in names:
                    if name not in expert_sems:
                        pool.sem_clear(names[name])

            @block.sync
            def _(sp):
                ended = sp.alloc_register("jobs_ended")
                sp.reg_mov(ended, 0)

                def refill(i, k):
                    n = sp.value_load(nbi[0:1, bass.ds(i * SETS + k, 1)], min_val=1, max_val=ROUNDS)
                    sp.reg_add(ended, ended, n)
                    sp.wait_ge(m_gu, sp.snap(ended))
                    for n in range(2):
                        load_expert(sp, l, (i + 1) * SETS + k, 3 * k + n)
                    sp.wait_ge(m_d1, sp.snap(ended))
                    load_expert(sp, l, (i + 1) * SETS + k, 3 * k + 2)

                with sp.Fori(0, N_EXPERTS // SETS - 1) as i:
                    for k in range(SETS):
                        refill(i, k)
                for k in range(N_EXPERTS % SETS):
                    refill(N_EXPERTS // SETS - 1, k)
                sp.free_register(ended)

            @block.tensor
            def _(pe):
                def gather(J):
                    pe.wait_ge(m_sel, J)
                    for t in range(NT):
                        for g in range(4):
                            ins = pe.matmul(bank_a[32 * g:32 * g + 32, 0:256], sel[:, t],
                                            XN[:, t].rearrange("p (f c) -> p c f", c=KC)[:, 2 * g:2 * g + 2],
                                            start=(t == 0), stop=(t == NT - 1))
                    ins.then_inc(m_gathered, 1)

                def turn(J):
                    pe.wait_ge(m_rows, J)
                    for h in range(2):
                        ins = pe.transpose(bank_a[:, 256 + h * P:256 + (h + 1) * P], rows[:, h * P:(h + 1) * P], ident)
                    ins.then_inc(m_turned, 1)

                def scatter(J):
                    pe.wait_ge(m_selwT, J)
                    for n, s in ((0, m_y0), (1, m_y1)):
                        pe.wait_ge(s, J)
                        for t in range(NT):
                            pe.matmul(ps[2 * t + n][:, :], selwT[:, t], ymoe[:, n * 512:(n + 1) * 512], start=False, stop=True,
                                      skip_group_check=True)

                def job(J, i, k, r):
                    pe.wait_ge(m_xg, J)
                    landing = i * 16 + 16 if isinstance(i, int) else pe.snap(i * 16 + 16)
                    pe.wait_ge(m_land[3 * k], landing)
                    pe.wait_ge(m_land[3 * k + 1], landing)
                    for kk in range(4):
                        for g in range(4):
                            c = 4 * (g % 2) + kk
                            w = (wg if g < 2 else wu)[k].rearrange("p (c n) -> p c n", c=KC)
                            ins = pe.matmul(bank_b[32 * g:32 * g + 32, :], xg[:, c], w[:, c], start=(kk == 0), stop=(kk == 3))
                    ins.then_inc(m_gu, 1)
                    pe.wait_ge(m_y1, J)
                    gather(pe.snap(J + 1))
                    pe.wait_ge(m_p, J)
                    pe.wait_ge(m_selwT, J)
                    for c in range(4):
                        ins = pe.matmul(bank_c[:, c * 64:(c + 1) * 64], gu.rearrange("p (f c) -> p c f", c=4)[:, c],
                                        cst[:, K_FOLD:K_FOLD + 64], start=True, stop=True)
                    ins.then_inc(m_fold, 1)
                    turn(pe.snap(J + 1))
                    scatter(J)
                    pe.wait_ge(m_hid, J)
                    pe.wait_ge(m_land[3 * k + 2], landing)
                    w = wd[k].rearrange("p (c n) -> p c n", c=4)
                    for n, bank, s in ((0, bank_d, m_d0), (1, bank_a, m_d1)):
                        for g in range(4):
                            ins = pe.matmul(bank[32 * g:32 * g + 32, :], hid[:, g], w[:, g, n * 512:(n + 1) * 512], start=True, stop=True)
                        ins.then_inc(s, 1)
                    for t in range(NT):
                        ins = pe.transpose(bank_c[:, 256 + t * P:256 + (t + 1) * P], selw[:, t].rearrange("p g s -> p (g s)"), ident)
                    ins.then_inc(m_tw, 1)

                gather(1)
                turn(1)
                pe.wait_ge(m_jobs, 1)
                for n in range(2):
                    ins = pe.transpose(bank_c[0:1, 256 + n * P:256 + (n + 1) * P], jf[:, n:n + 1], ident)
                ins.then_inc(m_jobs_turned, 1)
                jobs(pe, job)
                pe.wait_ge(m_end, 1)
                scatter_last = [(m, n) for n in range(2) for m in range(NT)]
                for t, n in scatter_last:
                    ins = pe.matmul(ps[2 * t + n][:, :], selwT[:, t], ymoe[:, n * 512:(n + 1) * 512], start=False, stop=True,
                                    skip_group_check=True)
                ins.then_inc(m_scattered, 1)

            @block.scalar
            def _(act):
                def job(J, i, k, r):
                    act.wait_ge(m_gu, J)
                    act.activation(gu, bank_b[:, :], ACT.Copy).then_inc(m_p, 1)
                    act.wait_ge(m_fold, J)
                    act.activation(sg, bank_c[:, 0:256].rearrange("p (c x s) -> p c x s", c=4, x=2)[:, :, 0], ACT.Silu).then_inc(m_sg, 1)
                    act.wait_ge(m_d0, J)
                    act.activation(ymoe[:, 0:512], bank_d[:, :], ACT.Copy).then_inc(m_y0, 1)
                jobs(act, job)

            @block.vector
            def _(v):
                def select(e, r):
                    for t in range(NT):
                        ins = v.tensor_scalar(sel[:, t], cst[:, bass.ds(r * CAP + K_IOTA, CAP)], posn[:, t, bass.ds(e, 1)], None, ALU.is_equal)
                    ins.then_inc(m_sel, 1)

                def gained(J):
                    v.wait_ge(m_gathered, J)
                    v.tensor_copy(rows, bank_a[:, 0:256]).then_inc(m_rows, 1)
                    v.wait_ge(m_turned, J)
                    v.tensor_tensor(xg.rearrange("p (g h) s -> p h g s", h=2), bank_a[:, 256:512].rearrange("p (h g s) -> p h g s", h=2, g=4),
                                    bcast(g_ffn.rearrange("p (g h) -> p h g", h=2).unsqueeze(3), [P, 2, 4, CAP]),
                                    ALU.mult).then_inc(m_xg, 1)

                v.memset(ymoe[:, 0:512], 0.0).then_inc(m_y0, 1)
                v.memset(ymoe[:, 512:1024], 0.0).then_inc(m_y1, 1)
                v.memset(selwT, 0.0).then_inc(m_selwT, 1)
                select(0, 0)
                index = cst[:, K_INDEX:K_INDEX + 1]
                link = chain(v, m_chain)
                link(v.tensor_tensor_scan(jend, cst[:, K_ONES:K_ONES + N_EXPERTS], nbf, 0.0, ALU.mult, ALU.add))
                v.tensor_scalar(jcmp[:, 0], jend, index, None, ALU.is_le)
                link(v.tensor_tensor(jstart, jend, nbf, ALU.subtract))
                gained(1)
                link(v.scalar_tensor_tensor(jcmp[:, 1], jstart, index, jstart, ALU.is_le, ALU.mult))
                link(v.tensor_reduce(jf[:, 0:1], jcmp[:, 0], AX.X, ALU.add))
                v.tensor_scalar(jf[:, 0:1], jf[:, 0:1], float(N_EXPERTS - 1), None, ALU.min)
                link(v.tensor_reduce(jf[:, 1:2], jcmp[:, 1], AX.X, ALU.max))
                link(v.tensor_tensor(jf[:, 1:2], index, jf[:, 1:2], ALU.subtract))
                v.tensor_scalar(jf[:, 1:2], jf[:, 1:2], float(ROUNDS - 1), None, ALU.min).then_inc(m_jobs, 1)
                v.wait_ge(m_jobs_turned, 1)
                link(v.tensor_copy(jobtab[0:1], bank_c[0:1, 256:512].rearrange("p (a j) -> p a j", a=2)[:, :, 0:JOBS]))

                def job(J, i, k, r):
                    e = i * SETS + k
                    for t in range(NT):
                        v.tensor_scalar(selw[:, t], bcast(cst[:, bass.ds(r * CAP + K_IOTA, CAP)].unsqueeze(1), [P, 4, CAP]),
                                        posn[:, t, bass.ds(e, 1)], weight[:, t, bass.ds(e, 1)], ALU.is_equal, ALU.mult)
                    e_next = v.value_load(jobtab[0:1, 0, bass.ds(J, 1)], min_val=0, max_val=N_EXPERTS - 1)
                    r_next = v.value_load(jobtab[0:1, 1, bass.ds(J, 1)], min_val=0, max_val=ROUNDS - 1)
                    select(e_next, r_next)
                    gained(v.snap(J + 1))
                    v.wait_ge(m_sg, J)
                    v.tensor_tensor(hid, bank_c[:, 0:256].rearrange("p (c x s) -> p c x s", c=4, x=2)[:, :, 1], sg, ALU.mult).then_inc(m_hid, 1)
                    v.wait_ge(m_d1, J)
                    v.tensor_copy(ymoe[:, 512:1024], bank_a[:, :]).then_inc(m_y1, 1)
                    v.wait_ge(m_tw, J)
                    v.tensor_copy(selwT.rearrange("p t q -> p (t q)"), bank_c[:, 256:512]).then_inc(m_selwT, 1)
                    v.wait_ge(m_y0, v.snap(J + 1))
                jobs(v, job)
                v.drain().then_inc(m_end, 1)
                v.wait_ge(m_scattered, 1)
                for t in range(NT):
                    for n in range(2):
                        v.tensor_copy(X[:, t, n * 512:(n + 1) * 512], ps[2 * t + n][:, :])


    z_sq, z_asked, z_root, z_w, z_out, z_y = (top.enter_context(nc.semaphore("z_" + n)) for n in ("squares", "root_asked", "root", "gain", "stored", "y"))
    with nc.Block() as block:
        @block.sync
        def _(sp):
            sp.dma_start(fw, final_norm_w.rearrange("(o d) -> o d", o=1).broadcast_to([P, D_MODEL])).then_inc(z_w, 16)
            for t in range(NT):
                sp.wait_ge(z_y, t + 1)
                sp.dma_start(out[0, t * P:(t + 1) * P, :], fin[:, t]).then_inc(z_out, 16)
            sp.wait_ge(z_out, 16 * NT)

        @block.gpsimd
        def _(pool):
            roots(pool, z_asked, z_root, [rstd])

        @block.scalar
        def _(act):
            norm_act(act, z_sq)

        @block.vector
        def _(v):
            ask, got = root_asker(v, z_asked, z_root)
            v.wait_ge(z_sq, NT)
            ask(v.tensor_scalar(rstd, ss, 1.0 / D_MODEL, EPS, ALU.mult, ALU.add))
            got()
            v.wait_ge(z_w, 16)
            for t in range(NT):
                v.scalar_tensor_tensor(fin[:, t], X[:, t], rstd[:, t:t + 1], fw, ALU.mult, ALU.mult).then_inc(z_y, 1)
    top.close()


_INS = ['x', 'attn_norm_w', 'w_in', 'gdn_conv_w', 'gdn_a_log', 'gdn_dt_bias', 'gdn_norm_w', 'diff_lambda', 'diff_norm_w',
        'gqa_q_norm_w', 'gqa_k_norm_w', 'w_branch_a', 'w_branch_b', 'w_branch_c', 'w_out', 'ffn_norm_w', 'router_group_w',
        'router_group_b', 'router_expert_w', 'router_expert_b', 'expert_w_gate', 'expert_w_up', 'expert_w_down',
        'final_norm_w']
_OUTS = [((1, SEQ, D_MODEL), 'float32')]


def kernel(**inputs):
    import numpy as _np
    import concourse.bacc as _bacc
    from concourse import mybir as _mybir
    from concourse.bass_utils import run_bass_kernel_spmd as _run

    nc = _bacc.Bacc("TRN2", target_bir_lowering=False, num_devices=1)
    arrays, args = {}, []
    for name in _INS:
        a = _np.ascontiguousarray(inputs[name])
        arrays[f"in_{name}_dram"] = a
        args.append(nc.dram_tensor(f"in_{name}_dram", a.shape, _mybir.dt.from_np(a.dtype), kind="ExternalInput").ap())
    c = shape_constants()
    arrays["consts_dram"] = c
    args.append(nc.dram_tensor("consts_dram", c.shape, _mybir.dt.from_np(c.dtype), kind="ExternalInput").ap())
    for i, (shape, dtype) in enumerate(_OUTS):
        dt = _mybir.dt.from_np(_np.dtype(dtype))
        args.append(nc.dram_tensor(f"out_{i}_dram", shape, dt, kind="ExternalOutput").ap())
    encoder_trunk(nc, *args)
    r = _run(nc, [arrays], core_ids=[0])
    got = tuple(r.results[0][f"out_{i}_dram"] for i in range(len(_OUTS)))
    return got[0]
```

```python
import concourse.bass as bass
from concourse import mybir
from contextlib import ExitStack
import math

F32 = mybir.dt.float32
F32R = mybir.dt.float32r
I32 = mybir.dt.int32
ALU = mybir.AluOpType
ACT = mybir.ActivationFunctionType
AX = mybir.AxisListType

P = 128
D_MODEL = 1024
SEQ = 256
NT = SEQ // P
KC = D_MODEL // P
EPS = 1e-6
HEADS = 4
DH = 128
TAPS = 5
N_EXPERTS = 32
N_GROUPS = 4
PER_GROUP = 8
FF = 512
CAP = 32
ROUNDS = SEQ // CAP
SETS = 3
JOBS = 48
LEVELS = 7
SCALE = 64 ** -0.5

C_Q, C_Z, C_BA, C_DQ, C_DK, C_DV, C_CQ, C_CKV, C_GATE = 0, 1536, 2048, 2064, 2576, 3088, 3600, 4112, 4368

RING = 6
U_CQ, U_CKV, U_DQ, U_DK, U_DV, U_GQ, U_GK, U_GV, U_Z = range(9)
ORDER = (2, 1, 0)
U_GATE0, U_BRANCH, U_GATE1 = (9, 12, 15), (10, 13, 16), (11, 14, 17)
U_OUT = 18
N_FIXED = 20

K_IDENT, K_ONES, K_UF, K_UB, K_SF, K_SB = (128 * n for n in range(6))
K_LEVEL0 = 768
K_LEVEL = K_LEVEL0 + 2 * 128
K_COSD = K_LEVEL + 2 * LEVELS * 64
K_SIND, K_COSG, K_SING = K_COSD + 128, K_COSD + 256, K_COSD + 384
K_IOTA = K_COSD + 512
K_LAM = K_IOTA + SEQ
K_THR = K_LAM + 4
K_FOLD = K_THR + 8
K_HALF = K_FOLD + 64
K_INDEX = K_HALF + 16
K_ALL = K_INDEX + 1


def shape_constants():
    import numpy as np
    c = np.zeros((P, K_ALL), np.float32)
    r, j = np.arange(P)[:, None], np.arange(P)[None, :]
    c[:, K_IDENT:K_IDENT + P] = r == j
    c[:, K_ONES:K_ONES + P] = 1
    c[:, K_UF:K_UF + P] = r <= j
    c[:, K_UB:K_UB + P] = r >= j
    c[:, K_SF:K_SF + P] = r < j
    c[:, K_SB:K_SB + P] = r > j
    for n in range(LEVELS):
        s = 1 << n
        m = (r // (2 * s) == j // (2 * s)) & (r % (2 * s) >= s) & (j % (2 * s) < s)
        for d, mask in enumerate((m, m.T)):
            cols = (np.arange(P) >> n & 1) == d
            c[:, K_LEVEL + (d * LEVELS + n) * 64:K_LEVEL + (d * LEVELS + n + 1) * 64] = mask[:, cols]
            if n == 0:
                c[:, K_LEVEL0 + d * P:K_LEVEL0 + (d + 1) * P] = mask

    def rope(pos, dim):
        inv = np.float32(1.0) / np.power(np.float32(10000.0), np.arange(0, dim, 2, dtype=np.float32) / np.float32(dim))
        ang = pos.astype(np.float32)[:, None] * inv[None, :].astype(np.float32)
        cos, sin = np.cos(ang), np.sin(ang)
        return np.concatenate([cos, cos], 1), np.concatenate([-sin, sin], 1)

    pos = np.arange(SEQ)
    cd, sd = rope(pos, 64)
    cr, sr = rope(pos // 64, 32)
    cc, sc = rope(pos % 64, 32)
    for at, t in ((K_COSD, cd), (K_SIND, sd), (K_COSG, np.concatenate([cr, cc], 1)), (K_SING, np.concatenate([sr, sc], 1))):
        c[:, at:at + 128] = t.reshape(NT, P, 64).transpose(1, 0, 2).reshape(P, 128)
    c[:, K_IOTA:K_IOTA + SEQ] = np.arange(SEQ)
    for l in range(2):
        init = 0.8 - 0.6 * math.exp(-0.3 * l)
        c[:, K_LAM + 2 * l] = init
        c[:, K_LAM + 2 * l + 1] = 1.0 - init
    c[:, K_THR:K_THR + ROUNDS] = CAP * np.arange(ROUNDS)
    c[:, K_THR] = -1
    m = np.arange(64)[None, :]
    c[:, K_FOLD:K_FOLD + 64] = (r % 32 == m % 32) & ((r >= 64) == (m >= 32))
    c[:, K_HALF:K_HALF + 16] = -0.5
    c[:, K_INDEX] = np.arange(P)
    return c


def encoder_trunk(nc, x, attn_norm_w, w_in, gdn_conv_w, gdn_a_log, gdn_dt_bias, gdn_norm_w, diff_lambda, diff_norm_w,
                  gqa_q_norm_w, gqa_k_norm_w, w_branch_a, w_branch_b, w_branch_c, w_out, ffn_norm_w, router_group_w,
                  router_group_b, router_expert_w, router_expert_b, expert_w_gate, expert_w_up, expert_w_down,
                  final_norm_w, consts, out):
    depth = w_in.shape[0]
    top = ExitStack()

    start_of = {}

    def sb(name, cols, dt=F32):
        start_of[name] = (nc.sbuf_base + 31) // 32 * 32
        return top.enter_context(nc.sbuf_tensor(name, [P, cols], dt))

    def rounded(name, tensor, at, *dims):
        t = nc.alloc_sbuf_tensor_at(name, [P, math.prod(dims)], F32R, offset=start_of[tensor] + 4 * at)
        return view(t, 0, *dims)

    ring = sb("ring", RING * 4096)
    x_sb = sb("x_sb", NT * D_MODEL)
    hT = sb("hT", KC * SEQ)
    xn = sb("xn", NT * D_MODEL)
    cst = sb("cst", K_ALL)
    arena = sb("arena", 16160)
    par = sb("par", 1064)
    small = sb("small", 768)
    nbi = sb("nbi", N_EXPERTS, I32)
    ps = [top.enter_context(nc.psum_tensor(f"ps{i}", [P, 512], F32)) for i in range(8)]

    def view(t, at, *dims):
        n = math.prod(dims)
        v = t[:, at:at + n]
        if len(dims) == 1:
            return v
        names = "abcd"[:len(dims)]
        return v.rearrange(f"p ({' '.join(names)}) -> p {' '.join(names)}", **dict(zip(names, dims)))

    ident = cst[:, K_IDENT:K_IDENT + P]
    ones = cst[:, K_ONES:K_ONES + P]
    cum = [cst[:, K_UF:K_UF + P], cst[:, K_UB:K_UB + P]]
    strict = [cst[:, K_SF:K_SF + P], cst[:, K_SB:K_SB + P]]

    def level0(direction):
        return cst[:, K_LEVEL0 + direction * P:K_LEVEL0 + (direction + 1) * P]

    def level(direction, n):
        return cst[:, K_LEVEL + (direction * LEVELS + n) * 64:K_LEVEL + (direction * LEVELS + n + 1) * 64]

    X = view(x_sb, 0, NT, D_MODEL)
    HT = view(hT, 0, KC, SEQ)
    XN = view(xn, 0, NT, D_MODEL)

    p_at = [0]

    def param(*dims):
        v = view(par, p_at[0], *dims)
        p_at[0] += math.prod(dims)
        return v

    g_attn, g_ffn = param(KC), param(KC)
    convw = param(TAPS * 12)
    dt_bias, a_log = param(8), param(8)
    n_gdn, n_diff = param(1), param(1)
    lamv_flat = param(256)
    lamv = lamv_flat.rearrange("p (a b d) -> p a b d", a=2, b=2)
    qn_w, kn_w = param(64), param(64)
    rw = param(KC, N_GROUPS + N_EXPERTS)
    rb = param(N_GROUPS + N_EXPERTS)
    wba = param(KC, 16)
    convrows = param(128)
    assert p_at[0] <= 1064

    s_at = [0]

    def tiny(*dims):
        v = view(small, s_at[0], *dims)
        s_at[0] += math.prod(dims)
        return v

    ss, rstd = tiny(NT), tiny(NT)
    beta, gg = tiny(2, NT, HEADS), tiny(2, NT, HEADS)
    sp_a, sp_b = tiny(2, NT, HEADS), tiny(2, NT, HEADS)
    aexp = tiny(8)
    bar = tiny(NT, 16)
    gc, gtot, egc, kdec = tiny(16), tiny(16), tiny(16), tiny(16)
    lprod, lsum, lexp = tiny(2, 64), tiny(2), tiny(2)
    nlam, ndl = tiny(1), tiny(1)
    hss, hrs = tiny(16), tiny(16)
    qss, qrs = tiny(NT, HEADS), tiny(NT, HEADS)
    mx, nmx, rsum, rinv = tiny(2, 4), tiny(2, 4), tiny(2, 4), tiny(2, 4)
    rl = tiny(2, 2)
    yss, yrs = tiny(16), tiny(16)
    logit = tiny(NT, 36)
    gpad, gmax8 = tiny(NT, 8), tiny(NT, 8)
    gexp, gsum, gprob, ngm = tiny(NT, 4), tiny(NT), tiny(NT), tiny(NT)
    goh = tiny(NT, 8)
    emask, etop = tiny(NT, N_EXPERTS), tiny(NT, 8)
    e1, esum, w01 = tiny(NT), tiny(NT), tiny(NT, 2)
    idxf = tiny(NT, 8)
    assert s_at[0] <= 768, s_at[0]
    idx = top.enter_context(nc.sbuf_tensor("idx", [P, NT * 8], mybir.dt.uint32))
    idx3 = idx[:, :].rearrange("p (t k) -> p t k", t=NT)
    hot = view(arena, 2880, 6, NT, N_EXPERTS)
    assigned, weight, posn, hot0, hot1, hotw = (hot[:, n] for n in range(6))
    nbf = view(arena, 3296, N_EXPERTS)
    over = view(arena, 3328, N_EXPERTS, 8)
    jend, jstart = view(arena, 3584, N_EXPERTS), view(arena, 3616, N_EXPERTS)
    jf = view(arena, 3648, 2)
    jcmp = view(arena, 3652, 2, N_EXPERTS)
    jobtab = top.enter_context(nc.sbuf_tensor("jobtab", [P, 2 * JOBS], I32))[:, :].rearrange("p (a j) -> p a j", a=2)

    dqT, dkT = view(arena, 0, HEADS, SEQ), view(arena, 1024, HEADS, SEQ)
    dv = view(arena, 2048, NT, 512)
    cqT = view(arena, 3072, HEADS, SEQ)
    ckT = view(arena, 4096, 2, SEQ)
    cv = view(arena, 4608, NT, 128)
    squares, gqa_tmp = view(arena, 6912, 2, 512), view(arena, 7936, 512)
    rope_a, rope_b = view(arena, 4864, 2, 512), view(arena, 5888, 2, 512)
    probs = view(arena, 6912, 2, 2, NT, SEQ)
    probsT = view(arena, 5888, 2, 2, SEQ)
    gqn = view(arena, 4864, 2, 512)
    pad = view(arena, 8960, 2, HEADS, SEQ + 4)
    conv = view(arena, 11040, 2, HEADS, SEQ)
    conv_flat = view(arena, 11040, 2, HEADS * SEQ)
    qtok = view(arena, 13088, NT, HEADS, DH)
    ktok = view(arena, 14112, NT, HEADS, DH)
    vtok = view(arena, 15136, NT, HEADS, DH)
    QT, KT = view(arena, 8960, HEADS, SEQ), view(arena, 9984, HEADS, SEQ)
    yb, yc = view(xn, 0, NT, 512), view(xn, 1024, NT, 512)
    LT = view(arena, 0, 4, HEADS, P)
    INT = view(arena, 2048, 4, HEADS, P)
    DI = view(arena, 4096, 4, HEADS, P)
    DT = view(arena, 6144, 4, HEADS, P)
    E = view(arena, 11040, 4, HEADS, P)
    YM = view(arena, 11040, 4, HEADS, 64)
    kd = view(arena, 13088, 2, HEADS, DH)
    vn1, S1 = view(arena, 0, 2, HEADS, DH), view(arena, 1024, 2, HEADS, DH)
    R2 = view(arena, 4096, 2, HEADS, DH)
    vn2, qs = view(arena, 5120, 2, HEADS, DH), view(arena, 11040, 2, HEADS, DH)
    oa = view(arena, 12064, NT, HEADS, DH)
    zs = view(arena, 3072, NT, 512)
    sig = view(arena, 4096, 4, 512)
    HT_hi, HT_lo = rounded("hT_high", "arena", 6656, KC, SEQ), rounded("hT_low", "hT", 0, KC, SEQ)
    w_hi = rounded("w_high", "arena", 8704, 4, 512)
    mergedT_hi, mergedT_lo = rounded("merged_high", "hT", 0, KC, SEQ), rounded("merged_low", "arena", 0, KC, SEQ)
    o_w_hi = rounded("o_w_high", "arena", 2048, 3, 512)
    b_HT_hi, b_HT_lo = rounded("b_hT_high", "arena", 8960, KC, SEQ), rounded("b_hT_low", "arena", 11008, KC, SEQ)
    b_w_hi = rounded("b_w_high", "arena", 13056, 4, 512)
    w_lo = [rounded(f"w_low{n}", "ring", n * 4096, 4096) for n in range(RING)]
    yT_hi = [rounded(f"yT_high{n}", "arena", 1024 * n, HEADS, SEQ) for n in range(3)]
    yT_lo = [rounded(f"yT_low{n}", "arena", at, HEADS, SEQ) for n, at in enumerate((3072, 11040, 15136))]
    merged = view(arena, 13088, NT, D_MODEL)
    ysq, ysq_a = view(arena, 11040, 1024), view(arena, 15136, 1024)
    sel = view(arena, 0, NT, CAP)
    selw = view(arena, 64, NT, 4, CAP)
    selwT = view(arena, 320, NT, P)
    xg = view(arena, 576, KC, CAP)
    gu = view(arena, 832, FF)
    sg = view(arena, 1344, 4, CAP)
    hid = view(arena, 1472, 4, CAP)
    ymoe = view(arena, 1600, D_MODEL)
    rows = view(arena, 2624, 256)
    junk = view(arena, 0, NT, D_MODEL)
    fin = view(arena, 0, NT, D_MODEL)
    fw = view(arena, 2048, D_MODEL)

    def slot(u):
        return ring[:, (u % RING) * 4096:(u % RING + 1) * 4096]

    def expert_slot(n):
        return slot(n) if n < RING else view(arena, 3872 + (n - RING) * 4096, 4096)

    def unit8(u):
        return slot(u).rearrange("p (c n) -> p c n", c=8)

    def bcast(ap, shape):
        return ap.broadcast_to(shape)

    names = {}

    def sem(name):
        names[name] = top.enter_context(nc.semaphore(name))
        return names[name]

    landed = [sem(f"unit_landed{n}") for n in range(RING)]
    used_at = {}
    (m_sel, m_gathered, m_rows, m_turned, m_xg, m_tw, m_selwT, m_gu, m_p, m_fold, m_sg, m_hid,
     m_d0, m_d1, m_y0, m_y1, m_end, m_scattered, m_chain, m_jobs, m_jobs_turned) = (
        sem("m_" + n) for n in ("selected", "gathered", "rows_copied", "rows_turned", "xg", "selw_turned", "selwT", "gate_up", "gate_up_copied", "folded",
                                "silu", "hidden", "down0", "down1", "y0", "y1", "end", "scattered", "chain", "jobs", "jobs_turned"))
    m_land = [sem(f"expert_landed{n}") for n in range(3 * SETS)]
    expert_sems = [name for name in names if name.startswith(("m_", "expert_landed"))]

    def unit_landed(eng, u):
        eng.wait_ge(landed[u % RING], 16 * (u // RING + 1))

    def load_unit(sp, l, u):
        if u >= RING:
            sp.wait_ge(*used_at[u - RING])
        cols = {U_DQ: C_DQ, U_DK: C_DK, U_DV: C_DV, U_CQ: C_CQ, U_GQ: C_Q, U_GK: C_Q + 512, U_GV: C_Q + 1024, U_Z: C_Z}
        for k, b in enumerate(ORDER):
            cols[U_GATE0[k]] = C_GATE + b * D_MODEL
            cols[U_GATE1[k]] = C_GATE + b * D_MODEL + 512
        if u in U_BRANCH:
            w = (w_branch_a, w_branch_b, w_branch_c)[ORDER[U_BRANCH.index(u)]]
            src = w[bass.ds(l, 1)].rearrange("o (c p) n -> p (o c) n", p=P)
            dst = slot(u).rearrange("p (c n) -> p c n", c=4)
        elif u == U_CKV:
            src = w_in[bass.ds(l, 1), :, C_CKV:C_CKV + 256].rearrange("o (p c) n -> p (o c) n", c=KC)
            dst = unit8(u)[:, :, 0:256]
        elif u >= U_OUT:
            n = u - U_OUT
            src = w_out[bass.ds(l, 1), :, n * 512:(n + 1) * 512].rearrange("o (p c) n -> p (o c) n", c=KC)
            dst = unit8(u)
        else:
            src = w_in[bass.ds(l, 1), :, cols[u]:cols[u] + 512].rearrange("o (p c) n -> p (o c) n", c=KC)
            dst = unit8(u)
        sp.dma_start(dst, src).then_inc(landed[u % RING], 16)

    def last_unit(n):
        return max(u for u in range(N_FIXED) if u % RING == n)

    def load_expert(sp, l, e, n):
        if n % 3 < 2:
            w = (expert_w_gate, expert_w_up)[n % 3].rearrange("l e (p c) f -> (l e) p c f", c=KC)
            dst = expert_slot(n).rearrange("p (o c f) -> p o c f", o=1, c=KC)
        else:
            w = expert_w_down.rearrange("l e (p c) d -> (l e) p c d", c=4)
            dst = expert_slot(n).rearrange("p (o c d) -> p o c d", o=1, c=4)
        src = w[bass.ds(l * N_EXPERTS + e, 1)].rearrange("o p c f -> p o c f")
        sp.dma_start(dst, src).then_inc(m_land[n], 16)

    def chain(eng, s):
        count = [0]

        def link(ins):
            count[0] += 1
            ins.then_inc(s, 1)
            eng.wait_ge(s, count[0])
        return link

    def root_asker(v, asked, given):
        count = [0]

        def ask(ins):
            count[0] += 1
            ins.then_inc(asked, 1)

        def got():
            v.wait_ge(given, count[0])
        return ask, got

    def roots(pool, asked, given, args):
        for n, a in enumerate(args):
            pool.wait_ge(asked, n + 1)
            half = cst[:, K_HALF:K_HALF + math.prod(a.shape[1:])]
            if len(a.shape) == 3:
                half = half.rearrange("p (t h) -> p t h", t=a.shape[1])
            pool.tensor_tensor(a, a, half, ALU.pow).then_inc(given, 1)

    def norm_act(act, done):
        for t in range(NT):
            act.activation(junk[:, t], X[:, t], ACT.Square, accum_out=ss[:, t:t + 1]).then_inc(done, 1)

    def norm_dve(v, squares, root, xn_ready):
        ask, got = root
        v.wait_ge(squares, NT)
        ask(v.tensor_scalar(rstd, ss, 1.0 / D_MODEL, EPS, ALU.mult, ALU.add))
        got()
        for t in range(NT):
            v.tensor_scalar(XN[:, t], X[:, t], rstd[:, t:t + 1], None, ALU.mult).then_inc(xn_ready, 1)

    def transpose_pe(pe, src, ready, turned, banks):
        pe.wait_ge(ready, NT)
        for c in range(KC):
            for t in range(NT):
                ins = pe.transpose(banks[c // 2][:, (c % 2) * SEQ + t * P:(c % 2) * SEQ + (t + 1) * P],
                                   src[:, t].rearrange("p (f c) -> p c f", c=KC)[:, c], ident)
            if c % 2:
                ins.then_inc(turned, 1)

    def scaled_act(act, turned, gain, done, banks):
        for j in (0, 2):
            act.wait_ge(turned, j + 1)
            for c in (2 * j, 2 * j + 1):
                ins = act.activation(HT[:, c], banks[j][:, (c % 2) * SEQ:(c % 2 + 1) * SEQ], ACT.Copy,
                                     scale=1.0 if gain is None else gain[:, c:c + 1])
            ins.then_inc(done, 1)

    def scaled_dve(v, turned, gain, done, banks):
        for j in (1, 3):
            v.wait_ge(turned, j + 1)
            for c in (2 * j, 2 * j + 1):
                src = banks[j][:, (c % 2) * SEQ:(c % 2 + 1) * SEQ]
                if gain is None:
                    ins = v.tensor_copy(HT[:, c], src)
                else:
                    ins = v.tensor_scalar(HT[:, c], src, gain[:, c:c + 1], None, ALU.mult)
            ins.then_inc(done, 1)

    s_x, s_cst = (top.enter_context(nc.semaphore(n)) for n in ("x_landed", "constants_landed"))
    with nc.Block() as block:
        @block.sync
        def _(sp):
            sp.dma_start(X, x.rearrange("b (t p) d -> p (b t) d", p=P)).then_inc(s_x, 16)
            sp.dma_start(cst[:, :], consts).then_inc(s_cst, 16)

    with nc.Fori(0, depth) as l:
        a_squares, a_asked, a_root, a_xn, a_turned, a_done = sem("a_squares"), sem("a_root_asked"), sem("a_root"), sem("a_xn"), sem("a_turned"), sem("a_done")
        a_par, a_late, a_convt = sem("a_params"), sem("a_late_params"), sem("a_convT")
        with nc.Block() as block:
            @block.sync
            def _(sp):
                one = bass.ds(l, 1)
                early = [
                    (g_attn, attn_norm_w[one].rearrange("o (p c) -> p (o c)", c=KC)),
                    (convrows[0:60], gdn_conv_w[one].rearrange("o k (c p) -> (o k c) p", p=P)),
                    (qn_w, gqa_q_norm_w[one].broadcast_to([P, 64])),
                    (kn_w, gqa_k_norm_w[one].broadcast_to([P, 64])),
                    (wba, w_in[one, :, C_BA:C_BA + 16].rearrange("o (p c) n -> p (o c) n", c=KC)),
                ]
                late = [
                    (g_ffn, ffn_norm_w[one].rearrange("o (p c) -> p (o c)", c=KC)),
                    (dt_bias, gdn_dt_bias[one].rearrange("o d h -> o (d h)").broadcast_to([P, 8])),
                    (a_log, gdn_a_log[one].rearrange("o d h -> o (d h)").broadcast_to([P, 8])),
                    (n_gdn, gdn_norm_w[one].rearrange("o p -> p o")),
                    (n_diff, diff_norm_w[one].rearrange("o p -> p o")),
                    (lamv_flat, diff_lambda[one].rearrange("o k d -> o (k d)").broadcast_to([P, 256])),
                    (rw[:, :, 0:N_GROUPS], router_group_w[one].rearrange("o (p c) n -> p (o c) n", c=KC)),
                    (rw[:, :, N_GROUPS:], router_expert_w[one].rearrange("o (p c) n -> p (o c) n", c=KC)),
                    (rb[:, 0:N_GROUPS], router_group_b[one].broadcast_to([P, N_GROUPS])),
                    (rb[:, N_GROUPS:], router_expert_b[one].broadcast_to([P, N_EXPERTS])),
                ]
                for dst, src in early:
                    sp.dma_start(dst, src).then_inc(a_par, 16)
                for u in range(2):
                    load_unit(sp, l, u)
                for dst, src in late:
                    sp.dma_start(dst, src).then_inc(a_late, 16)
                for u in range(2, RING):
                    load_unit(sp, l, u)
                sp.wait_ge(a_par, 16 * len(early))

            @block.scalar
            def _(act):
                act.wait_ge(s_x, 16)
                norm_act(act, a_squares)
                act.wait_ge(a_par, 16 * 5)
                scaled_act(act, a_turned, g_attn, a_done, ps[0:4])

            @block.vector
            def _(v):
                v.wait_ge(s_x, 16)
                norm_dve(v, a_squares, root_asker(v, a_asked, a_root), a_xn)
                v.wait_ge(a_par, 16 * 5)
                scaled_dve(v, a_turned, g_attn, a_done, ps[0:4])
                v.wait_ge(a_convt, 1)
                v.tensor_copy(convw, ps[4][:, 0:60])

            @block.gpsimd
            def _(pool):
                pool.wait_ge(s_cst, 16)
                roots(pool, a_asked, a_root, [rstd])
                for name in expert_sems:
                    pool.sem_clear(names[name])

            @block.tensor
            def _(pe):
                pe.wait_ge(s_cst, 16)
                transpose_pe(pe, XN, a_xn, a_turned, ps[0:4])
                pe.wait_ge(a_par, 16 * 5)
                pe.transpose(ps[4][:, 0:60], convrows[0:60], ident[0:60, 0:60]).then_inc(a_convt, 1)

        b_hh, b_hl, b_hi, b_lo, b_used = (sem("b_" + n) for n in ("hT_high", "hT_low", "w_high", "w_low", "w_used"))
        b_free, b_rope, b_turned, b_out = sem("b_free"), sem("b_rope"), sem("b_turned"), sem("b_out")
        b_chain, b_sq, b_ba, b_asked, b_root = sem("b_chain"), sem("b_squares"), sem("b_ba"), sem("b_root_asked"), sem("b_root")
        streamed = (U_CQ, U_CKV, U_DQ, U_DK, U_DV)
        items = [(u, t) for u in streamed for t in range(NT)]
        roped = 8
        chunks = [(u, j, 256 if u == U_CKV else 512) for u in streamed for j in range(KC)]
        used_at.update({u: (b_used, KC * (n + 1)) for n, u in enumerate(streamed)})

        def product_done(i):
            return b_used, KC * (i // NT + 1)

        with nc.Block() as block:
            @block.sync
            def _(sp):
                for u in range(RING, RING + 5):
                    load_unit(sp, l, u)
                sp.wait_ge(a_late, 16 * 10)

            @block.tensor
            def _(pe):
                def heads(i):
                    pe.wait_ge(b_rope, i + 1)
                    if i >= 2:
                        pe.wait_ge(b_out, i - 1)
                    for j in range(2 if items[i][0] == U_CKV else HEADS):
                        ins = pe.transpose(ps[4 + i % 2][:, j * P:(j + 1) * P], rope_b[:, i % 2, j * P:(j + 1) * P], ident)
                    ins.then_inc(b_turned, 1)

                for q, (u, c, cols) in enumerate(chunks):
                    n = q // KC
                    if c == 0 and n >= 2:
                        pe.wait_ge(b_free, 2 * n - 2)
                    if q < KC:
                        pe.wait_ge(b_hl, c // 2 + 1)
                    pe.wait_ge(b_lo, q + 1)
                    w, w_low = b_w_hi[:, q % 4, 0:cols], w_lo[u % RING][:, c * 512:c * 512 + cols]
                    for t in range(NT):
                        bank, tok = ps[(2 * n + t) % 4][:, 0:cols], slice(t * P, (t + 1) * P)
                        pe.matmul(bank, b_HT_hi[:, c, tok], w, start=(c == 0), stop=False)
                        pe.matmul(bank, b_HT_hi[:, c, tok], w_low, start=False, stop=False)
                        ins = pe.matmul(bank, b_HT_lo[:, c, tok], w, start=False, stop=(c == KC - 1))
                    ins.then_inc(b_used, 1)
                    if q == KC - 1:
                        for t in range(NT):
                            for cc in range(KC):
                                ins = pe.matmul(ps[6][:, t * 16:(t + 1) * 16], HT[:, cc, t * P:(t + 1) * P], wba[:, cc],
                                                start=(cc == 0), stop=(cc == KC - 1))
                        ins.then_inc(b_ba, 1)
                    if c == KC - 1 and n >= 1:
                        for t in range(NT):
                            heads(2 * (n - 1) + t)

            @block.scalar
            def _(act):
                def squares_of(i):
                    act.wait_ge(*product_done(i))
                    if i >= 2:
                        act.wait_ge(b_rope, i - 1)
                    n = 512 if items[i][0] == U_CQ else 128
                    act.activation(squares[:, i % 2, 0:n], ps[i % 4][:, 0:n], ACT.Square).then_inc(b_sq, 1)

                def heads_out(i):
                    u, t = items[i]
                    dst = {U_DQ: dqT, U_DK: dkT, U_CQ: cqT, U_CKV: ckT}[u]
                    nh = 2 if u == U_CKV else HEADS
                    act.wait_ge(b_turned, i + 1)
                    act.activation(dst[:, :, t * P:(t + 1) * P],
                                   ps[4 + i % 2][:, 0:nh * P].rearrange("p (j q) -> p j q", j=nh), ACT.Copy).then_inc(b_out, 1)

                for q, (u, c, cols) in enumerate(chunks):
                    n = q // KC
                    if q < 4:
                        act.activation(b_HT_hi[:, 2 * q:2 * q + 2], HT[:, 2 * q:2 * q + 2], ACT.Copy).then_inc(b_hh, 1)
                    if c == 0:
                        unit_landed(act, u)
                    if q >= 4:
                        act.wait_ge(b_used, q - 3)
                    act.activation(b_w_hi[:, q % 4, 0:cols], unit8(u)[:, c, 0:cols], ACT.Copy).then_inc(b_hi, 1)
                    if c == 3:
                        for t in range(NT):
                            if n in (1, 2):
                                squares_of(2 * (n - 1) + t)
                        for t in range(NT):
                            if n >= 2:
                                heads_out(2 * (n - 2) + t)
                for t in range(NT):
                    heads_out(roped - 2 + t)
                for t in range(NT):
                    act.wait_ge(*product_done(roped + t))
                    act.activation(dv[:, t], ps[(roped + t) % 4][:, :], ACT.Copy)

            @block.vector
            def _(v):
                link = chain(v, b_chain)
                ask, got = root_asker(v, b_asked, b_root)

                def rope(i):
                    u, t = items[i]
                    src = ps[i % 4]
                    v.wait_ge(*product_done(i))
                    if i >= 2:
                        v.wait_ge(b_turned, i - 1)
                    ra, rb_ = rope_a[:, i % 2], rope_b[:, i % 2]
                    if u in (U_DQ, U_DK):
                        cos = cst[:, K_COSD + t * 64:K_COSD + (t + 1) * 64]
                        sin = cst[:, K_SIND + t * 64:K_SIND + (t + 1) * 64]
                        s4 = src[:, :].rearrange("p (h a d) -> p h a d", a=2, d=32)
                        r4 = rb_.rearrange("p (h a d) -> p h a d", a=2, d=32)
                        for a in range(2):
                            v.tensor_tensor(r4[:, :, a], s4[:, :, 1 - a],
                                            bcast(sin[:, a * 32:(a + 1) * 32].unsqueeze(1), [P, 8, 32]), ALU.mult)
                        v.tensor_tensor(ra.rearrange("p (h d) -> p h d", d=64), src[:, :].rearrange("p (h d) -> p h d", d=64),
                                        bcast(cos.unsqueeze(1), [P, 8, 64]), ALU.mult).then_inc(b_free, 1)
                        v.wait_ge(b_free, i + 1)
                        v.tensor_tensor(rb_, rb_, ra, ALU.add).then_inc(b_rope, 1)
                    else:
                        nh = 8 if u == U_CQ else 2
                        w = qn_w if u == U_CQ else kn_w
                        cos = cst[:, K_COSG + t * 64:K_COSG + (t + 1) * 64]
                        sin = cst[:, K_SING + t * 64:K_SING + (t + 1) * 64]
                        qw = gqn[:, i % 2, 0:nh * 64]
                        v.wait_ge(b_sq, i + 1)
                        v.tensor_tensor(qw.rearrange("p (h d) -> p h d", d=64), src[:, 0:nh * 64].rearrange("p (h d) -> p h d", d=64),
                                        bcast(w.unsqueeze(1), [P, nh, 64]), ALU.mult)
                        if u == U_CKV:
                            v.tensor_copy(cv[:, t], src[:, 128:256])
                        link(v.tensor_reduce(hss[:, 0:nh], squares[:, i % 2, 0:nh * 64].rearrange("p (h d) -> p h d", d=64), AX.X, ALU.add))
                        v.sem_inc(b_free, 1)
                        ask(v.tensor_scalar(hrs[:, 0:nh], hss[:, 0:nh], 1.0 / 64, EPS, ALU.mult, ALU.add))
                        tmp = gqa_tmp[:, 0:nh * 64]
                        sin4 = sin.rearrange("p (g a d) -> p g a d", a=2, d=16)
                        for a in range(2):
                            for g in range(2):
                                ins = v.tensor_tensor(tmp.rearrange("p (h g a d) -> p h g a d", g=2, a=2, d=16)[:, :, g, a],
                                                qw.rearrange("p (h g a d) -> p h g a d", g=2, a=2, d=16)[:, :, g, 1 - a],
                                                bcast(sin4[:, g, a].unsqueeze(1), [P, nh, 16]), ALU.mult)
                        link(ins)
                        link(v.tensor_tensor(qw.rearrange("p (h d) -> p h d", d=64), qw.rearrange("p (h d) -> p h d", d=64),
                                             bcast(cos.unsqueeze(1), [P, nh, 64]), ALU.mult))
                        link(v.tensor_tensor(tmp, tmp, qw, ALU.add))
                        got()
                        if u == U_CQ:
                            v.tensor_tensor(rb_.rearrange("p (h d) -> p h d", d=64), tmp.rearrange("p (h d) -> p h d", d=64),
                                            bcast(hrs[:, 0:8].unsqueeze(2), [P, 8, 64]), ALU.mult).then_inc(b_rope, 1)
                        else:
                            for a in range(2):
                                ins = v.tensor_tensor(rb_[:, 0:256].rearrange("p (h a d) -> p h a d", a=2, d=64)[:, :, a],
                                                      tmp.rearrange("p (h d) -> p h d", d=64),
                                                      bcast(hrs[:, 0:2].unsqueeze(2), [P, 2, 64]), ALU.mult)
                            ins.then_inc(b_rope, 1)
                for q, (u, c, cols) in enumerate(chunks):
                    n = q // KC
                    if q < 4:
                        v.wait_ge(b_hh, q + 1)
                        v.tensor_tensor(b_HT_lo[:, 2 * q:2 * q + 2], HT[:, 2 * q:2 * q + 2], b_HT_hi[:, 2 * q:2 * q + 2].bitcast(F32),
                                        ALU.subtract).then_inc(b_hl, 1)
                    v.wait_ge(b_hi, q + 1)
                    v.tensor_tensor(w_lo[u % RING][:, c * 512:c * 512 + cols], unit8(u)[:, c, 0:cols], b_w_hi[:, q % 4, 0:cols].bitcast(F32),
                                    ALU.subtract).then_inc(b_lo, 1)
                    if n >= 1 and c in (3, 6):
                        rope(2 * (n - 1) + c // 6)
                v.wait_ge(b_ba, 1)
                v.tensor_copy(bar, ps[6][:, 0:32].rearrange("p (t n) -> p t n", t=NT))

            @block.gpsimd
            def _(pool):
                roots(pool, b_asked, b_root, [hrs[:, 0:8], hrs[:, 0:8], hrs[:, 0:2], hrs[:, 0:2]])

        c_score, c_max, c_exp, c_prob = sem("c_scores"), sem("c_max"), sem("c_exp"), sem("c_probs")
        c_turned, c_pT, c_pv, c_y, c_chain = (sem("c_" + n) for n in ("turned", "probsT", "pv", "y", "chain"))
        d_fill, d_empty, d_conv, d_silu, d_sq, d_norm = (sem("d_" + n) for n in ("fill", "empty", "conv", "silu", "squares", "norm"))
        d_asked, d_root = sem("d_root_asked"), sem("d_root")
        g_dve, g_act = sem("g_dve"), sem("g_act")
        STEPS = 8
        first_fill = [s if s < 4 else 4 + 2 * (s - 4) for s in range(STEPS + 1)]
        pieces = [[("proj", 0, 0), ("proj", 0, 1)], [("proj", 1, 0), ("proj", 1, 1)], [("proj", 2, 0), ("tok", 0, 0), ("tok", 0, 1)],
                  [("tok", 1, 0), ("tok", 1, 1)], [("proj", 2, 1)], [], [("back", 0, 0), ("back", 0, 1)],
                  [("tok", 2, 0), ("tok", 2, 1), ("back", 1, 0), ("back", 1, 1)]]
        fills_at = {k: n for n, k in enumerate(k for step in pieces for k in step)}

        def filled(kind, g):
            return fills_at[kind, g, 1] + 1

        tok = (qtok, ktok, vtok)
        used_at.update({U_GQ + g: (d_fill, filled("proj", g)) for g in range(3)})
        with nc.Block() as block:
            @block.sync
            def _(sp):
                for u in range(RING + 5, RING + 8):
                    load_unit(sp, l, u)

            @block.tensor
            def _(pe):
                def scores(s):
                    if s >= 2:
                        pe.wait_ge(c_exp, s - 1)
                    for m in range(2):
                        half = slice(64 * m, 64 * m + 64)
                        q, k = (dqT[half, s], dkT[half, s]) if s < 4 else (cqT[half, s - 4], ckT[half, (s - 4) // 2])
                        for t in range(NT):
                            ins = pe.matmul(ps[2 * (s % 2) + m][:, t * SEQ:(t + 1) * SEQ], q[:, t * P:(t + 1) * P], k,
                                            start=True, stop=True)
                    ins.then_inc(c_score, 1)

                def turn(s, m, f):
                    pe.wait_ge(c_prob, s + 1)
                    if f:
                        pe.wait_ge(c_pT, f)
                    for t in range(NT):
                        for kt in range(NT):
                            ins = pe.transpose(ps[4][:, kt * SEQ + t * P:kt * SEQ + (t + 1) * P],
                                               probs[:, s % 2, m, t, kt * P:(kt + 1) * P], ident)
                    ins.then_inc(c_turned, 1)

                def weighted(s, m, f):
                    pe.wait_ge(c_pT, f + 1)
                    if s:
                        pe.wait_ge(c_y, s)
                    for t in range(NT):
                        for kt in range(NT):
                            if s < 4:
                                o, val = ps[5][:, t * P:(t + 1) * P], dv[:, kt, s * P:(s + 1) * P]
                            else:
                                kv = (s - 4) // 2
                                o, val = ps[5][:, (2 * t + m) * 64:(2 * t + m + 1) * 64], cv[:, kt, kv * 64:(kv + 1) * 64]
                            ins = pe.matmul(o, probsT[:, f % 2, kt, t * P:(t + 1) * P], val, start=(kt == 0), stop=(kt == NT - 1))
                    ins.then_inc(c_pv, 1)

                def fill(kind, g, w):
                    f = fills_at[kind, g, w]
                    bank = ps[6 + f % 2]
                    if f >= 2:
                        pe.wait_ge(d_empty, f - 1)
                    if kind == "proj":
                        if w == 0:
                            unit_landed(pe, U_GQ + g)
                        for h in (2 * w, 2 * w + 1):
                            for c in range(KC):
                                ins = pe.matmul(bank[:, (h % 2) * SEQ:(h % 2 + 1) * SEQ],
                                                unit8(U_GQ + g)[:, c, h * DH:(h + 1) * DH], HT[:, c],
                                                start=(c == 0), stop=(c == KC - 1))
                    elif kind == "tok":
                        pe.wait_ge(d_silu, g + 1)
                        for h in range(HEADS):
                            ins = pe.transpose(bank[:, h * DH:(h + 1) * DH], conv[:, g % 2, h, w * P:(w + 1) * P], ident)
                    else:
                        pe.wait_ge(d_norm, g + 1)
                        for h in range(HEADS):
                            ins = pe.transpose(bank[:, h * P:(h + 1) * P], tok[g][:, w, h], ident)
                    ins.then_inc(d_fill, 1)

                scores(0)
                scores(1)
                before = None
                for s in range(STEPS):
                    for piece in pieces[s]:
                        fill(*piece)
                    for m in range(1 if s < 4 else 2):
                        turn(s, m, first_fill[s] + m)
                        if m == 0 and s + 2 < STEPS:
                            scores(s + 2)
                        if before is not None:
                            weighted(*before)
                        before = (s, m, first_fill[s] + m)
                weighted(*before)

            @block.scalar
            def _(act):
                act.activation(beta.rearrange("p d t h -> p t d h"), bar[:, :, 0:8].rearrange("p t (d h) -> p t d h", d=2),
                               ACT.Sigmoid)
                act.activation(aexp, a_log, ACT.Exp).then_inc(g_act, 1)
                act.wait_ge(g_dve, 1)
                act.activation(lexp, lsum, ACT.Exp)
                act.activation(sp_b, sp_b, ACT.Exp, scale=-1.0).then_inc(g_act, 1)
                act.wait_ge(g_dve, 2)
                act.activation(sp_b, sp_b, ACT.Ln).then_inc(g_act, 1)

                def exps(s):
                    act.wait_ge(c_max, s + 1)
                    if s >= 2:
                        act.wait_ge(c_turned, first_fill[s - 1])
                    for m in range(2):
                        for t in range(NT):
                            ins = act.activation(probs[:, s % 2, m, t], ps[2 * (s % 2) + m][:, t * SEQ:(t + 1) * SEQ], ACT.Exp,
                                                 bias=nmx[:, s % 2, 2 * m + t:2 * m + t + 1], scale=SCALE,
                                                 accum_out=rsum[:, s % 2, 2 * m + t:2 * m + t + 1])
                    ins.then_inc(c_exp, 1)

                def empty(kind, g, w):
                    f = fills_at[kind, g, w]
                    act.wait_ge(d_fill, f + 1)
                    bank = ps[6 + f % 2]
                    if kind == "proj":
                        if g == 2 and w == 0:
                            act.wait_ge(d_conv, 2)
                        dst, src = pad[:, g % 2, 2 * w:2 * w + 2, 2:2 + SEQ], bank[:, :].rearrange("p (h t) -> p h t", h=2)
                    elif kind == "tok":
                        dst, src = tok[g][:, w], bank[:, :].rearrange("p (h d) -> p h d", h=HEADS)
                    else:
                        if g == 0 and w == 0:
                            act.wait_ge(d_conv, 6)
                        dst, src = (QT, KT)[g][:, :, w * P:(w + 1) * P], bank[:, :].rearrange("p (h t) -> p h t", h=HEADS)
                    act.activation(dst, src, ACT.Copy).then_inc(d_empty, 1)

                def silu(g):
                    act.wait_ge(d_conv, 2 * g + 2)
                    act.activation(conv[:, g % 2], conv[:, g % 2], ACT.Silu).then_inc(d_silu, 1)

                def square(g):
                    act.wait_ge(d_empty, filled("tok", g))
                    act.activation(conv_flat[:, g % 2], tok[g].rearrange("p t h d -> p (t h d)"),
                                   ACT.Square).then_inc(d_sq, 1)

                silu_early, silu_late = {1: 0, 2: 1}, {5: 2}
                exps(0)
                exps(1)
                for s in range(STEPS):
                    for piece in pieces[s]:
                        empty(*piece)
                        if piece in (("tok", 0, 1), ("tok", 1, 1)):
                            square(piece[1])
                    if s in silu_early:
                        silu(silu_early[s])
                    for m in range(1 if s < 4 else 2):
                        f = first_fill[s] + m
                        act.wait_ge(c_turned, f + 1)
                        if f >= 2:
                            act.wait_ge(c_pv, f - 1)
                        act.activation(probsT[:, f % 2].rearrange("p k q -> p (k q)"), ps[4][:, :], ACT.Copy).then_inc(c_pT, 1)
                    if s + 2 < STEPS:
                        exps(s + 2)
                    if s in silu_late:
                        silu(silu_late[s])

            @block.vector
            def _(v):
                link = chain(v, c_chain)
                ask, got = root_asker(v, d_asked, d_root)
                for b in range(2):
                    v.memset(pad[:, b, :, 0:2], 0.0)
                    v.memset(pad[:, b, :, SEQ + 2:SEQ + 4], 0.0)
                link(v.tensor_tensor(lprod, lamv[:, :, 0], lamv[:, :, 1], ALU.mult))
                v.tensor_reduce(lsum, lprod, AX.X, ALU.add)
                link(v.tensor_tensor(sp_a.rearrange("p d t h -> p t d h"), bar[:, :, 8:16].rearrange("p t (d h) -> p t d h", d=2),
                                     bcast(dt_bias.rearrange("p (d h) -> p d h", d=2).unsqueeze(1), [P, NT, 2, HEADS]), ALU.add))
                v.scalar_tensor_tensor(sp_b, sp_a, -1.0, sp_a, ALU.mult, ALU.max).then_inc(g_dve, 1)

                def maxima(s):
                    v.wait_ge(c_score, s + 1)
                    for m in range(2):
                        ins = v.tensor_reduce(mx[:, s % 2, 2 * m:2 * m + 2],
                                              ps[2 * (s % 2) + m][:, :].rearrange("p (t k) -> p t k", t=NT), AX.X, ALU.max)
                    link(ins)
                    v.tensor_scalar(nmx[:, s % 2], mx[:, s % 2], -SCALE, None, ALU.mult).then_inc(c_max, 1)

                maxima(0)
                maxima(1)
                v.wait_ge(g_act, 2)
                link(v.tensor_scalar(sp_b, sp_b, 1.0, None, ALU.add))
                v.sem_inc(g_dve, 1)
                link(v.tensor_tensor(nlam, lexp[:, 1:2], lexp[:, 0:1], ALU.subtract))
                link(v.tensor_tensor(nlam, nlam, cst[:, bass.ds(l * 2 + K_LAM, 1)], ALU.subtract))
                v.wait_ge(g_act, 3)
                link(v.scalar_tensor_tensor(sp_a, sp_a, 0.0, sp_b, ALU.max, ALU.add))
                for t in range(NT):
                    ins = v.tensor_tensor(gg[:, :, t], sp_a[:, :, t], aexp.rearrange("p (d h) -> p d h", d=2), ALU.mult)
                link(ins)
                v.tensor_scalar(gg, gg, -1.0, None, ALU.mult)

                def convolve(g, w):
                    v.wait_ge(d_empty, fills_at["proj", g, w] + 1)
                    if g == 2:
                        v.wait_ge(d_fill, filled("tok", 0))
                    for k in range(TAPS):
                        for h in (2 * w, 2 * w + 1):
                            cw = convw[:, k * 12 + g * HEADS + h:k * 12 + g * HEADS + h + 1]
                            src = pad[:, g % 2, h, k:k + SEQ]
                            if k == 0:
                                ins = v.tensor_scalar(conv[:, g % 2, h], src, cw, None, ALU.mult)
                            else:
                                ins = v.scalar_tensor_tensor(conv[:, g % 2, h], src, cw, conv[:, g % 2, h], ALU.mult, ALU.add)
                        if k < TAPS - 1:
                            link(ins)
                    ins.then_inc(d_conv, 1)

                def l2norm(g):
                    v.wait_ge(d_sq, g + 1)
                    link(v.tensor_reduce(qss, conv_flat[:, g % 2].rearrange("p (t h d) -> p t h d", t=NT, h=HEADS), AX.X, ALU.add))
                    ask(v.tensor_scalar(qrs, qss, EPS, None, ALU.add))
                    got()
                    if g == 0:
                        link(v.tensor_scalar(qrs, qrs, DH ** -0.5, None, ALU.mult))
                    v.tensor_tensor(tok[g], tok[g], bcast(qrs.unsqueeze(3), [P, NT, HEADS, DH]), ALU.mult).then_inc(d_norm, 1)

                def weigh(s):
                    b = s % 2
                    v.wait_ge(c_exp, s + 1)
                    if s >= 2:
                        v.wait_ge(c_y, s - 1)
                    if s >= 4:
                        v.reciprocal(rinv[:, b], rsum[:, b]).then_inc(c_prob, 1)
                        return
                    link(v.reciprocal(rinv[:, b], rsum[:, b]))
                    link(v.tensor_scalar(rl[:, b], rinv[:, b, 2:4], nlam, None, ALU.mult))
                    for t in range(NT):
                        ins = v.tensor_scalar(probs[:, b, 1, t], probs[:, b, 1, t], rl[:, b, t:t + 1], None, ALU.mult)
                    link(ins)
                    for t in range(NT):
                        ins = v.scalar_tensor_tensor(probs[:, b, 0, t], probs[:, b, 0, t], rinv[:, b, t:t + 1], probs[:, b, 1, t],
                                                     ALU.mult, ALU.add)
                    ins.then_inc(c_prob, 1)

                work = {0: [(convolve, 0, 0), (convolve, 0, 1)], 1: [(convolve, 1, 0), (convolve, 1, 1)], 2: [(l2norm, 0)],
                        3: [(convolve, 2, 0)], 4: [(convolve, 2, 1)], 5: [(l2norm, 1)]}
                weigh(0)
                for s in range(STEPS):
                    b = s % 2
                    if s + 1 < STEPS:
                        weigh(s + 1)
                    if s + 2 < STEPS:
                        maxima(s + 2)
                    for f, *args in work.get(s, []):
                        f(*args)
                    v.wait_ge(c_pv, first_fill[s + 1])
                    if s < 4:
                        v.tensor_copy(yb[:, :, s * P:(s + 1) * P], ps[5][:, 0:SEQ].rearrange("p (t e) -> p t e", t=NT)).then_inc(c_y, 1)
                    else:
                        v.wait_ge(c_prob, s + 1)
                        for m in range(2):
                            h = 2 * (s - 4) + m
                            ins = v.tensor_tensor(yc[:, :, h * 64:(h + 1) * 64],
                                                  ps[5][:, 0:256].rearrange("p (t m e) -> p t m e", t=NT, m=2)[:, :, m],
                                                  bcast(rinv[:, b, 2 * m:2 * m + 2].unsqueeze(2), [P, NT, 64]), ALU.mult)
                        ins.then_inc(c_y, 1)

            @block.gpsimd
            def _(pool):
                roots(pool, d_asked, d_root, [qrs, qrs])

        e_gc, e_gcc, e_gr, e_kk, e_d, e_e, e_m = (sem("e_" + n) for n in ("gc", "gc_copied", "gc_rows", "kk", "diff", "exp", "masked"))
        e_lt, e_y, e_ym, e_z, e_upd, e_chain = (sem("e_" + n) for n in ("lt", "y", "ym", "z", "updated", "chain"))
        e_u, e_v, e_kd, e_s, e_sc, e_ks, e_r, e_o, e_small, e_int = (
            sem("e_" + n) for n in ("u", "v", "kd", "s", "s_copied", "ks", "r", "o", "small", "qk_masked"))
        ybank = [ps[1], ps[2], ps[3], ps[4]]
        zbank, tbank = [ps[5], ps[6]], [ps[7], ps[0]]
        e_t, e_dt = sem("e_inverse_turned"), sem("e_dt")
        kkbank, qkbank = [ps[5], ps[6]], [ps[7], ps[0]]

        def heads3(bank):
            return bank[:, :].rearrange("p (h i) -> p h i", h=HEADS)

        def per_head(cols):
            return bcast(cols.unsqueeze(2), [P, HEADS, P])

        def columns(m, direction, n):
            if len(m.shape) == 2:
                return m.rearrange("p (b a s) -> p b a s", a=2, s=1 << n)[:, :, direction]
            return m.rearrange("p h (b a s) -> p h b a s", a=2, s=1 << n)[:, :, :, direction]

        def all_heads(m):
            return bcast(m.unsqueeze(1), [P, HEADS, P])

        with nc.Block() as block:
            @block.tensor
            def _(pe):
                def turn_inverse(k):
                    G = k % 4
                    pe.wait_ge(e_upd, k + 1)
                    if k >= 2:
                        pe.wait_ge(e_dt, k - 1)
                    for h in range(HEADS):
                        ins = pe.transpose(tbank[G % 2][:, h * P:(h + 1) * P], DI[:, G, h], ident)
                    ins.then_inc(e_t, 1)

                for d in range(2):
                    pe.matmul(ps[0][:, 8 * d:8 * d + 8], cum[d], gg[:, d].rearrange("p t h -> p (t h)"), start=True, stop=True)
                pe.matmul(ps[0][:, 16:32], ones, gg.rearrange("p d t h -> p (d t h)"), start=True, stop=True).then_inc(e_gc, 1)
                for G in range(4):
                    d, t = divmod(G, 2)
                    for h in range(HEADS):
                        ins = pe.matmul(ybank[G][:, h * P:(h + 1) * P], bcast(gg[:, d, t, h:h + 1], [P, P]), cum[d],
                                        start=True, stop=True)
                    ins.then_inc(e_gr, 1)
                for t in range(NT):
                    for h in range(HEADS):
                        k = KT[:, h, t * P:(t + 1) * P]
                        ins = pe.matmul(kkbank[t][:, h * P:(h + 1) * P], k, k, start=True, stop=True)
                    ins.then_inc(e_kk, 1)
                pe.wait_ge(e_gcc, 1)
                for t in range(NT):
                    for h in range(HEADS):
                        ins = pe.matmul(qkbank[t][:, h * P:(h + 1) * P], KT[:, h, t * P:(t + 1) * P], QT[:, h, t * P:(t + 1) * P],
                                        start=True, stop=True)
                    ins.then_inc(e_kk, 1)
                for G in range(4):
                    pe.wait_ge(e_lt, G + 1)
                    for h in range(HEADS):
                        ins = pe.transpose(ybank[G][:, h * P:(h + 1) * P], LT[:, G, h], ident)
                    ins.then_inc(e_y, 1)
                for n in range(1, LEVELS):
                    for G in range(4):
                        k = 4 * n + G
                        pe.wait_ge(e_upd, k - 3)
                        for h in range(HEADS):
                            ins = pe.matmul(ybank[G][:, h * 64:(h + 1) * 64], LT[:, G, h], columns(DI[:, G, h], G // 2, n),
                                            start=True, stop=True)
                        ins.then_inc(e_y, 1)
                    if n == 1:
                        pe.wait_ge(e_int, 1)
                        for G in range(4):
                            turn_inverse(G)
                    for G in range(4):
                        k = 4 * n + G
                        pe.wait_ge(e_ym, k - 3)
                        pe.wait_ge(e_dt, k - 3)
                        pe.wait_ge(e_upd, k - 1)
                        for h in range(HEADS):
                            ins = pe.matmul(zbank[G % 2][:, h * 64:(h + 1) * 64], DT[:, G, h], YM[:, G, h], start=True, stop=True)
                        ins.then_inc(e_z, 1)
                        if G >= 1:
                            turn_inverse(k - 1)
                    turn_inverse(4 * n + 3)
                pe.wait_ge(e_dt, 4 * LEVELS)
                for d in range(2):
                    t = d
                    for h in range(HEADS):
                        ins = pe.matmul(ps[1 + d][:, h * P:(h + 1) * P], DT[:, 2 * d + t, h], vtok[:, t, h], start=True, stop=True)
                    ins.then_inc(e_u, 1)
                for d in range(2):
                    pe.wait_ge(e_v, d + 1)
                    pe.wait_ge(e_kd, d + 1)
                    for h in range(HEADS):
                        ins = pe.matmul(ps[3 + d][:, h * P:(h + 1) * P], kd[:, d, h], vn1[:, d, h], start=True, stop=True)
                    ins.then_inc(e_s, 1)
                for d in range(2):
                    t = 1 - d
                    pe.wait_ge(e_sc, d + 1)
                    for h in range(HEADS):
                        pe.matmul(ps[5 + d][:, h * P:(h + 1) * P], KT[:, h, t * P:(t + 1) * P], S1[:, d, h], start=True, stop=True)
                    for h in range(HEADS):
                        ins = pe.matmul(qkbank[d][:, h * P:(h + 1) * P], QT[:, h, t * P:(t + 1) * P], S1[:, d, h], start=True, stop=True)
                    ins.then_inc(e_ks, 1)
                for d in range(2):
                    t = 1 - d
                    pe.wait_ge(e_r, d + 1)
                    for h in range(HEADS):
                        ins = pe.matmul(ps[1 + d][:, h * P:(h + 1) * P], DT[:, 2 * d + t, h], R2[:, d, h], start=True, stop=True)
                    ins.then_inc(e_u, 1)
                pe.wait_ge(e_v, 4)
                for t in range(NT):
                    first, second = t, 1 - t
                    for h in range(HEADS):
                        pe.matmul(ps[3 + t][:, h * P:(h + 1) * P], INT[:, 2 * first + t, h], vn1[:, first, h], start=True, stop=False)
                        ins = pe.matmul(ps[3 + t][:, h * P:(h + 1) * P], INT[:, 2 * second + t, h], vn2[:, second, h],
                                        start=False, stop=True)
                    ins.then_inc(e_o, 1)

            @block.scalar
            def _(act):
                act.wait_ge(e_gcc, 1)
                act.activation(egc, gc, ACT.Exp)
                act.activation(kdec, kdec, ACT.Exp).then_inc(e_small, 1)
                for G in range(4):
                    act.wait_ge(e_d, G + 1)
                    act.activation(E[:, G], E[:, G], ACT.Exp).then_inc(e_e, 1)
                for k in range(4 * LEVELS):
                    act.wait_ge(e_t, k + 1)
                    act.activation(DT[:, k % 4], heads3(tbank[k % 2]), ACT.Copy).then_inc(e_dt, 1)
                for d in range(2):
                    act.wait_ge(e_s, d + 1)
                    act.activation(S1[:, d], heads3(ps[3 + d]), ACT.Copy).then_inc(e_sc, 1)

            @block.gpsimd
            def _(pool):
                pool.wait_ge(e_small, 1)
                for d in range(2):
                    pool.tensor_tensor(kd[:, d], ktok[:, d], per_head(kdec[:, 12 * d:12 * d + 4]),
                                       ALU.mult).then_inc(e_kd, 1)
                for G in range(4):
                    d, t = divmod(G, 2)
                    pool.wait_ge(e_e, G + 1)
                    pool.tensor_tensor(INT[:, G], E[:, G], all_heads(cum[d]), ALU.mult).then_inc(e_m, 1)

            @block.vector
            def _(v):
                link = chain(v, e_chain)
                v.wait_ge(e_gc, 1)
                v.tensor_copy(gc, ps[0][:, 0:16])
                link(v.tensor_copy(gtot, ps[0][:, 16:32]))
                v.tensor_tensor(kdec, gtot, gc, ALU.subtract).then_inc(e_gcc, 1)
                for G in range(4):
                    v.wait_ge(e_gr, G + 1)
                    for h in range(HEADS):
                        ins = v.tensor_scalar(E[:, G, h], ybank[G][:, h * P:(h + 1) * P], gc[:, 4 * G + h:4 * G + h + 1], 0.0,
                                              ALU.subtract, ALU.min)
                    ins.then_inc(e_d, 1)
                v.wait_ge(e_kk, 2)
                for G in range(4):
                    d, t = divmod(G, 2)
                    v.wait_ge(e_e, G + 1)
                    for h in range(HEADS):
                        ins = v.scalar_tensor_tensor(LT[:, G, h], kkbank[t][:, h * P:(h + 1) * P], beta[:, d, t, h:h + 1], E[:, G, h],
                                                     ALU.mult, ALU.mult)
                    ins.then_inc(e_lt, 1)
                for G in range(4):
                    d, t = divmod(G, 2)
                    v.wait_ge(e_y, G + 1)
                    v.wait_ge(e_m, G + 1)
                    link(v.tensor_tensor(E[:, G], heads3(ybank[G]), all_heads(level0(d)), ALU.mult))
                    v.tensor_tensor(DI[:, G], all_heads(ident), E[:, G], ALU.subtract).then_inc(e_upd, 1)
                v.wait_ge(e_kk, 4)
                for G in range(4):
                    ins = v.tensor_tensor(INT[:, G], heads3(qkbank[G % 2]), INT[:, G], ALU.mult)
                ins.then_inc(e_int, 1)
                for n in range(1, LEVELS):
                    for G in range(4):
                        k = 4 * n + G
                        v.wait_ge(e_y, k + 1)
                        if n > 1:
                            v.wait_ge(e_z, k - 7)
                        v.tensor_tensor(YM[:, G], ybank[G][:, 0:256].rearrange("p (h i) -> p h i", h=HEADS),
                                        bcast(level(G // 2, n).unsqueeze(1), [P, HEADS, 64]), ALU.mult).then_inc(e_ym, 1)
                    for G in range(4):
                        k = 4 * n + G
                        v.wait_ge(e_z, k - 3)
                        v.wait_ge(e_t, k - 3)
                        d = columns(DI[:, G], G // 2, n)
                        v.tensor_tensor(d, d, zbank[G % 2][:, 0:256].rearrange("p (h b s) -> p h b s", h=HEADS, s=1 << n),
                                        ALU.subtract).then_inc(e_upd, 1)
                for d in range(2):
                    v.wait_ge(e_u, d + 1)
                    v.tensor_tensor(vn1[:, d], heads3(ps[1 + d]), per_head(beta[:, d, d]), ALU.mult).then_inc(e_v, 1)
                v.wait_ge(e_small, 1)
                for d in range(2):
                    t = 1 - d
                    G = 2 * d + t
                    v.wait_ge(e_ks, d + 1)
                    link(v.tensor_tensor(R2[:, d], heads3(ps[5 + d]), per_head(egc[:, 4 * G:4 * G + 4]), ALU.mult))
                    v.tensor_tensor(R2[:, d], vtok[:, t], R2[:, d], ALU.subtract).then_inc(e_r, 1)
                    v.tensor_tensor(qs[:, d], heads3(qkbank[d]), per_head(egc[:, 4 * G:4 * G + 4]), ALU.mult)
                for d in range(2):
                    v.wait_ge(e_u, d + 3)
                    v.tensor_tensor(vn2[:, d], heads3(ps[1 + d]), per_head(beta[:, d, 1 - d]), ALU.mult).then_inc(e_v, 1)
                for t in range(NT):
                    v.wait_ge(e_o, t + 1)
                    v.wait_ge(e_v, 4)
                    v.tensor_tensor(oa[:, t], heads3(ps[3 + t]), qs[:, 1 - t], ALU.add)

        f_hh, f_hl, f_hi, f_lo, f_used = (sem("f_" + n) for n in ("hT_high", "hT_low", "w_high", "w_low", "w_used"))
        f_sq, f_yn, f_on, f_zs, f_ya, f_t, f_yh, f_yl, f_sig, f_m, f_chain = (
            sem("f_" + n) for n in ("squares", "y_normed", "o_normed", "z_silu", "ya", "turned", "yT_high", "yT_low", "gates", "merged", "chain"))
        f_asked, f_root = sem("f_root_asked"), sem("f_root")
        streamed = [U_Z] + [u for k in range(3) for u in (U_GATE0[k], U_BRANCH[k], U_GATE1[k])]
        chunks = [(u, j) for u in streamed for j in range(8)]
        ended = {u: 8 * n + 7 for n, u in enumerate(streamed)}
        used_at.update({u: (f_used, q + 1) for u, q in ended.items()})
        gains = {2: 1.0, 1: ndl, 0: n_gdn}
        yT_banks = {2: ps[2:4], 1: ps[6:8], 0: ps[6:8]}

        def chunk(u, j, low=False):
            at = (j % 4) * 1024 + j // 4 * 512 if u in U_BRANCH else j * 512
            return (w_lo[u % RING] if low else slot(u))[:, at:at + 512]

        with nc.Block() as block:
            @block.sync
            def _(sp):
                for u in range(RING + 8, N_FIXED):
                    load_unit(sp, l, u)
                for n in range(2, RING):
                    sp.wait_ge(*used_at[last_unit(n)])
                    load_expert(sp, l, n // 3, n)

            @block.tensor
            def _(pe):
                def turn(src, banks):
                    for h in range(HEADS):
                        for t in range(NT):
                            ins = pe.transpose(banks[h // 2][:, (h % 2) * SEQ + t * P:(h % 2) * SEQ + (t + 1) * P],
                                               src[:, t, h * P:(h + 1) * P], ident)
                    ins.then_inc(f_t, 1)

                def product(u):
                    for j in range(8):
                        q = ended[u] - 7 + j
                        if u in U_BRANCH:
                            b = ORDER[U_BRANCH.index(u)]
                            hi, lo, c, first, last = yT_hi[b], yT_lo[b], j % 4, j % 4 == 0, j % 4 == 3
                            banks = ps[2 * (j // 4):2 * (j // 4) + 2]
                            if j == 4 and u != U_BRANCH[0]:
                                pe.wait_ge(f_m, 4 * U_BRANCH.index(u))
                        else:
                            hi, lo, c, first, last = HT_hi, HT_lo, j, j == 0, j == 7
                            banks = ps[0:2] if u == U_Z else ps[4:6] if u in U_GATE0 else ps[6:8]
                        if u == U_Z:
                            pe.wait_ge(f_hl, j // 2 + 1)
                        pe.wait_ge(f_lo, q + 1)
                        for t in range(NT):
                            tok = slice(t * P, (t + 1) * P)
                            w, w_low = w_hi[:, q % 4], chunk(u, j, low=True)
                            pe.matmul(banks[t][:, :], hi[:, c, tok], w, start=first, stop=False)
                            pe.matmul(banks[t][:, :], hi[:, c, tok], w_low, start=False, stop=False)
                            ins = pe.matmul(banks[t][:, :], lo[:, c, tok], w, start=False, stop=last)
                        ins.then_inc(f_used, 1)

                turn(yc, yT_banks[2])
                product(U_Z)
                pe.wait_ge(f_yn, 1)
                turn(yb, yT_banks[1])
                for k in range(3):
                    if k:
                        pe.wait_ge(f_sig, 4 * k - 2)
                    product(U_GATE0[k])
                    if k == 0:
                        pe.wait_ge(f_ya, 1)
                        pe.wait_ge(f_yl, 2)
                        turn(oa.rearrange("p t h e -> p t (h e)"), yT_banks[0])
                        pe.wait_ge(f_zs, 2)
                    else:
                        pe.wait_ge(f_m, 4 * k - 2)
                    pe.wait_ge(f_yl, k + 1)
                    product(U_BRANCH[k])
                    if k == 0:
                        pe.wait_ge(f_yl, 3)
                    else:
                        pe.wait_ge(f_sig, 4 * k)
                    product(U_GATE1[k])

            @block.scalar
            def _(act):
                def high(y):
                    n = ORDER.index(y)
                    act.wait_ge(f_t, n + 1)
                    for j in range(2):
                        ins = act.activation(yT_hi[y][:, 2 * j:2 * j + 2].rearrange("p h t -> p (h t)"), yT_banks[y][j][:, :],
                                             ACT.Copy, scale=gains[y])
                    ins.then_inc(f_yh, 1)

                def gates(k, n):
                    act.wait_ge(f_used, ended[(U_GATE0, U_GATE1)[n][k]] + 1)
                    for t in range(NT):
                        i = 4 * k + 2 * n + t
                        if i >= 4:
                            act.wait_ge(f_m, i - 3)
                        act.activation(sig[:, i % 4], ps[4 + 2 * n + t][:, :], ACT.Sigmoid).then_inc(f_sig, 1)

                def silu_z():
                    act.wait_ge(f_used, ended[U_Z] + 1)
                    for t in range(NT):
                        act.activation(zs[:, t], ps[t][:, :], ACT.Silu).then_inc(f_zs, 1)

                def squares():
                    act.activation(ysq, yb.rearrange("p t n -> p (t n)"), ACT.Square).then_inc(f_sq, 1)
                    act.activation(ysq_a, oa.rearrange("p t h e -> p (t h e)"), ACT.Square).then_inc(f_sq, 1)

                follows = {3: [(squares,), (high, 2)], ended[U_Z] + 3: [(silu_z,)], ended[U_Z] + 4: [(high, 1)], ended[U_GATE0[0]] + 4: [(high, 0)]}
                for k in range(3):
                    for n in range(2):
                        follows.setdefault(ended[(U_GATE0, U_GATE1)[n][k]] + 3, []).append((gates, k, n))
                for q, (u, j) in enumerate(chunks):
                    if q < 4:
                        act.activation(HT_hi[:, 2 * q:2 * q + 2], HT[:, 2 * q:2 * q + 2], ACT.Copy).then_inc(f_hh, 1)
                    if j == 0:
                        unit_landed(act, u)
                    if q >= 4:
                        act.wait_ge(f_used, q - 3)
                    act.activation(w_hi[:, q % 4], chunk(u, j), ACT.Copy).then_inc(f_hi, 1)
                    for f, *args in follows.get(q, []):
                        f(*args)
                gates(2, 1)

            @block.vector
            def _(v):
                link = chain(v, f_chain)
                ask, got = root_asker(v, f_asked, f_root)

                def low(y):
                    n = ORDER.index(y)
                    v.wait_ge(f_yh, n + 1)
                    for j in range(2):
                        part = slice(2 * j, 2 * j + 2)
                        ins = v.scalar_tensor_tensor(yT_lo[y][:, part].rearrange("p h t -> p (h t)"), yT_banks[y][j][:, :], gains[y],
                                                     yT_hi[y][:, part].rearrange("p h t -> p (h t)"), ALU.mult, ALU.subtract)
                    ins.then_inc(f_yl, 1)

                def norm_root():
                    v.wait_ge(f_sq, 2)
                    v.tensor_reduce(yss[:, 0:8], ysq.rearrange("p (g e) -> p g e", e=DH), AX.X, ALU.add)
                    link(v.tensor_reduce(yss[:, 8:16], ysq_a.rearrange("p (g e) -> p g e", e=DH), AX.X, ALU.add))
                    ask(v.tensor_scalar(yrs, yss, 1.0 / DH, EPS, ALU.mult, ALU.add))
                    v.tensor_tensor(ndl, n_diff, cst[:, bass.ds(l * 2 + (K_LAM + 1), 1)], ALU.mult)

                def norm_b():
                    got()
                    v.tensor_tensor(yb.rearrange("p t (h e) -> p (t h) e", h=HEADS), yb.rearrange("p t (h e) -> p (t h) e", h=HEADS),
                                    bcast(yrs[:, 0:8].unsqueeze(2), [P, 8, DH]), ALU.mult).then_inc(f_yn, 1)
                    v.tensor_tensor(oa.rearrange("p t h e -> p (t h) e"), oa.rearrange("p t h e -> p (t h) e"),
                                    bcast(yrs[:, 8:16].unsqueeze(2), [P, 8, DH]), ALU.mult).then_inc(f_on, 1)

                def gated_a():
                    v.wait_ge(f_zs, 2)
                    v.wait_ge(f_on, 1)
                    v.tensor_tensor(oa.rearrange("p t h e -> p (t h e)"), oa.rearrange("p t h e -> p (t h e)"),
                                    zs.rearrange("p t n -> p (t n)"), ALU.mult).then_inc(f_ya, 1)

                def merge(k, n):
                    v.wait_ge(f_used, ended[U_BRANCH[k]] + 1 - (4 if n == 0 else 0))
                    for t in range(NT):
                        i = 4 * k + 2 * n + t
                        v.wait_ge(f_sig, i + 1)
                        dst = merged[:, t, n * 512:(n + 1) * 512]
                        if k == 0:
                            v.tensor_tensor(dst, ps[2 * n + t][:, :], sig[:, i % 4], ALU.mult).then_inc(f_m, 1)
                        else:
                            link(v.tensor_tensor(sig[:, i % 4], ps[2 * n + t][:, :], sig[:, i % 4], ALU.mult))
                            v.tensor_tensor(dst, dst, sig[:, i % 4], ALU.add).then_inc(f_m, 1)

                follows = {4: [(norm_root,)], 6: [(norm_b,)], 7: [(low, 2)], ended[U_Z] + 4: [(gated_a,)], ended[U_Z] + 5: [(low, 1)],
                           ended[U_GATE0[0]] + 5: [(low, 0)]}
                for k in range(3):
                    follows.setdefault(ended[U_BRANCH[k]] - 1, []).append((merge, k, 0))
                    follows.setdefault(ended[U_GATE1[k]] + 4, []).append((merge, k, 1))
                for q, (u, j) in enumerate(chunks):
                    if q < 4:
                        v.wait_ge(f_hh, q + 1)
                        v.tensor_tensor(HT_lo[:, 2 * q:2 * q + 2], HT[:, 2 * q:2 * q + 2], HT_hi[:, 2 * q:2 * q + 2].bitcast(F32),
                                        ALU.subtract).then_inc(f_hl, 1)
                    v.wait_ge(f_hi, q + 1)
                    w = chunk(u, j)
                    v.tensor_tensor(chunk(u, j, low=True), w, w_hi[:, q % 4].bitcast(F32), ALU.subtract).then_inc(f_lo, 1)
                    for f, *args in follows.get(q, []):
                        f(*args)
                merge(2, 1)

            @block.gpsimd
            def _(pool):
                roots(pool, f_asked, f_root, [yrs])

        h_t, h_mh, h_ml, h_hi, h_lo, h_used, h_x, h_sq, h_xn, h_turned, h_done, h_chain = (
            sem("h_" + n) for n in ("turned", "merged_high", "merged_low", "w_high", "w_low", "w_used", "residual", "squares", "xn", "turned2", "hT", "chain"))
        h_asked, h_root = sem("h_root_asked"), sem("h_root")
        used_at.update({U_OUT + n: (h_used, KC * (n + 1)) for n in range(2)})
        chunks = [(U_OUT + n, c) for n in range(2) for c in range(KC)]
        h_r, h_gm, h_ge, h_e1, h_ev, h_a, h_pos = (sem("h_" + n) for n in ("router", "group_max", "group_exp", "pair", "pair_exp", "assigned", "pos"))
        with nc.Block() as block:
            @block.sync
            def _(sp):
                for n in range(RING, RING + 3):
                    if n == RING + 2:
                        sp.wait_ge(h_t, 4)
                    load_expert(sp, l, n // 3, n)
                for n in range(2):
                    sp.wait_ge(*used_at[last_unit(n)])
                    load_expert(sp, l, 0, n)

            @block.tensor
            def _(pe):
                for c in range(KC):
                    for t in range(NT):
                        ins = pe.transpose(ps[c // 2][:, (c % 2) * SEQ + t * P:(c % 2) * SEQ + (t + 1) * P],
                                           merged[:, t].rearrange("p (f c) -> p c f", c=KC)[:, c], ident)
                    if c % 2:
                        ins.then_inc(h_t, 1)
                for q, (u, c) in enumerate(chunks):
                    pe.wait_ge(h_ml, c // 2 + 1)
                    pe.wait_ge(h_lo, q + 1)
                    w, w_low = o_w_hi[:, q % 3], w_lo[u % RING][:, c * 512:(c + 1) * 512]
                    for t in range(NT):
                        bank, tok = ps[4 + 2 * (u - U_OUT) + t][:, :], slice(t * P, (t + 1) * P)
                        pe.matmul(bank, mergedT_hi[:, c, tok], w, start=(c == 0), stop=False)
                        pe.matmul(bank, mergedT_hi[:, c, tok], w_low, start=False, stop=False)
                        ins = pe.matmul(bank, mergedT_lo[:, c, tok], w, start=False, stop=(c == KC - 1))
                    ins.then_inc(h_used, 1)
                for n in range(2):
                    for t in range(NT):
                        pe.wait_ge(h_x, 2 * n + t + 1)
                        pe.matmul(ps[2 * t + n][:, :], ident, X[:, t, n * 512:(n + 1) * 512], start=True, stop=True)
                transpose_pe(pe, XN, h_xn, h_turned, ps[4:8])
                pe.wait_ge(h_done, 4)
                for t in range(NT):
                    for c in range(KC):
                        ins = pe.matmul(ps[4][:, t * 36:(t + 1) * 36], HT[:, c, t * P:(t + 1) * P], rw[:, c], start=(c == 0), stop=(c == KC - 1))
                ins.then_inc(h_r, 1)
                pe.wait_ge(h_a, 1)
                pe.matmul(ps[5][:, 0:32], strict[0], assigned[:, 0], start=True, stop=True)
                pe.matmul(ps[5][:, 32:64], strict[0], assigned[:, 1], start=True, stop=False)
                pe.matmul(ps[5][:, 32:64], ones, assigned[:, 0], start=False, stop=True)
                pe.matmul(ps[5][:, 64:96], ones, assigned[:, 0], start=True, stop=False)
                pe.matmul(ps[5][:, 64:96], ones, assigned[:, 1], start=False, stop=True).then_inc(h_pos, 1)

            @block.scalar
            def _(act):
                for q, (u, c) in enumerate(chunks):
                    if q < 4:
                        act.wait_ge(h_t, q + 1)
                        act.activation(mergedT_hi[:, 2 * q:2 * q + 2].rearrange("p c t -> p (c t)"), ps[q][:, :], ACT.Copy).then_inc(h_mh, 1)
                    if c == 0:
                        unit_landed(act, u)
                    if q >= 3:
                        act.wait_ge(h_used, q - 2)
                    act.activation(o_w_hi[:, q % 3], unit8(u)[:, c], ACT.Copy).then_inc(h_hi, 1)
                act.wait_ge(h_x, 4)
                norm_act(act, h_sq)
                scaled_act(act, h_turned, g_ffn, h_done, ps[4:8])
                act.wait_ge(h_gm, 1)
                for t in range(NT):
                    ins = act.activation(gexp[:, t], logit[:, t, 0:4], ACT.Exp, bias=ngm[:, t:t + 1], accum_out=gsum[:, t:t + 1])
                ins.then_inc(h_ge, 1)
                act.wait_ge(h_e1, 1)
                act.activation(e1, e1, ACT.Exp).then_inc(h_ev, 1)

            @block.vector
            def _(v):
                link = chain(v, h_chain)
                v.memset(gpad, -3e38)
                for q, (u, c) in enumerate(chunks):
                    if q < 4:
                        v.wait_ge(h_mh, q + 1)
                        v.tensor_tensor(mergedT_lo[:, 2 * q:2 * q + 2].rearrange("p c t -> p (c t)"), ps[q][:, :],
                                        mergedT_hi[:, 2 * q:2 * q + 2].rearrange("p c t -> p (c t)").bitcast(F32), ALU.subtract).then_inc(h_ml, 1)
                    v.wait_ge(h_hi, q + 1)
                    v.tensor_tensor(w_lo[u % RING][:, c * 512:(c + 1) * 512], unit8(u)[:, c], o_w_hi[:, q % 3].bitcast(F32),
                                    ALU.subtract).then_inc(h_lo, 1)
                for n in range(2):
                    v.wait_ge(h_used, KC * (n + 1))
                    for t in range(NT):
                        dst = X[:, t, n * 512:(n + 1) * 512]
                        v.tensor_tensor(dst, dst, ps[4 + 2 * n + t][:, :], ALU.add).then_inc(h_x, 1)
                norm_dve(v, h_sq, root_asker(v, h_asked, h_root), h_xn)
                scaled_dve(v, h_turned, g_ffn, h_done, ps[4:8])
                v.wait_ge(h_r, 1)
                link(v.tensor_tensor(logit, ps[4][:, 0:72].rearrange("p (t n) -> p t n", t=NT), bcast(rb.unsqueeze(1), [P, NT, 36]), ALU.add))
                link(v.tensor_copy(gpad[:, :, 0:4], logit[:, :, 0:4]))
                for t in range(NT):
                    ins = v.max(gmax8[:, t], gpad[:, t])
                link(ins)
                v.tensor_scalar(ngm, gmax8[:, :, 0], -1.0, None, ALU.mult).then_inc(h_gm, 1)
                for t in range(NT):
                    ins = v.max_index(idx3[:, t], gmax8[:, t], gpad[:, t])
                link(ins)
                link(v.tensor_copy(idxf, idx3))
                for t in range(NT):
                    ins = v.tensor_scalar(goh[:, t], cst[:, K_IOTA:K_IOTA + 8], idxf[:, t, 0:1], None, ALU.is_equal)
                link(ins)
                link(v.tensor_scalar(goh, goh, -1.0, 1e30, ALU.add, ALU.mult))
                for t in range(NT):
                    ins = v.tensor_tensor(emask[:, t].rearrange("p (g e) -> p g e", g=N_GROUPS),
                                          logit[:, t, 4:36].rearrange("p (g e) -> p g e", g=N_GROUPS),
                                          bcast(goh[:, t, 0:4].unsqueeze(2), [P, N_GROUPS, PER_GROUP]), ALU.add)
                link(ins)
                for t in range(NT):
                    ins = v.max(etop[:, t], emask[:, t])
                link(ins)
                v.tensor_tensor(e1, etop[:, :, 1], etop[:, :, 0], ALU.subtract).then_inc(h_e1, 1)
                for t in range(NT):
                    ins = v.max_index(idx3[:, t], etop[:, t], emask[:, t])
                link(ins)
                link(v.tensor_copy(idxf, idx3))
                for t in range(NT):
                    v.tensor_scalar(hot0[:, t], cst[:, K_IOTA:K_IOTA + N_EXPERTS], idxf[:, t, 0:1], None, ALU.is_equal)
                    ins = v.tensor_scalar(hot1[:, t], cst[:, K_IOTA:K_IOTA + N_EXPERTS], idxf[:, t, 1:2], None, ALU.is_equal)
                link(ins)
                v.tensor_tensor(assigned, hot0, hot1, ALU.add).then_inc(h_a, 1)
                v.wait_ge(h_ge, 1)
                v.wait_ge(h_ev, 1)
                v.tensor_scalar(esum, e1, 1.0, None, ALU.add)
                link(v.reciprocal(gprob, gsum))
                link(v.reciprocal(esum, esum))
                link(v.tensor_tensor(w01[:, :, 0], gprob, esum, ALU.mult))
                link(v.tensor_tensor(w01[:, :, 1], w01[:, :, 0], e1, ALU.mult))
                for t in range(NT):
                    ins = v.tensor_scalar(hotw[:, t], hot0[:, t], w01[:, t, 0:1], None, ALU.mult)
                link(ins)
                for t in range(NT):
                    ins = v.scalar_tensor_tensor(weight[:, t], hot1[:, t], w01[:, t, 1:2], hotw[:, t], ALU.mult, ALU.add)
                link(ins)
                v.wait_ge(h_pos, 1)
                link(v.scalar_tensor_tensor(posn, ps[5][:, 0:64].rearrange("p (t e) -> p t e", t=NT), 1.0, assigned, ALU.add, ALU.mult))
                v.tensor_scalar(posn, posn, -1.0, None, ALU.add)
                link(v.tensor_tensor(over, bcast(ps[5][:, 64:96].unsqueeze(2), [P, N_EXPERTS, 8]),
                                     bcast(cst[:, K_THR:K_THR + 8].unsqueeze(1), [P, N_EXPERTS, 8]), ALU.is_gt))
                link(v.tensor_reduce(nbf[:, :], over, AX.X, ALU.add))
                v.tensor_copy(nbi[:, :], nbf[:, :])

            @block.gpsimd
            def _(pool):
                roots(pool, h_asked, h_root, [rstd])

        bank_a, bank_b, bank_c, bank_d = ps[4:8]
        wg, wu, wd = [[expert_slot(3 * k + n) for k in range(SETS)] for n in range(3)]

        def jobs(eng, body):
            J = eng.alloc_register("jobs")
            eng.reg_mov(J, 1)

            def of_expert(i, k):
                n = eng.value_load(nbi[0:1, bass.ds(i * SETS + k, 1)], min_val=1, max_val=ROUNDS)
                with eng.Fori(0, n) as r:
                    body(eng.snap(J), i, k, r)
                    eng.reg_add(J, J, 1)

            with eng.Fori(0, N_EXPERTS // SETS) as i:
                for k in range(SETS):
                    of_expert(i, k)
            for k in range(N_EXPERTS % SETS):
                of_expert(N_EXPERTS // SETS, k)
            eng.free_register(J)

        with nc.Block() as block:
            @block.gpsimd
            def _(pool):
                pool.memset(ymoe[:, 0:512], 0.0).then_inc(m_y0, 1)
                pool.memset(ymoe[:, 512:1024], 0.0).then_inc(m_y1, 1)
                pool.memset(selwT, 0.0).then_inc(m_selwT, 1)
                for name in names:
                    if name not in expert_sems:
                        pool.sem_clear(names[name])

            @block.sync
            def _(sp):
                ended = sp.alloc_register("jobs_ended")
                sp.reg_mov(ended, 0)

                def refill(i, k):
                    n = sp.value_load(nbi[0:1, bass.ds(i * SETS + k, 1)], min_val=1, max_val=ROUNDS)
                    sp.reg_add(ended, ended, n)
                    sp.wait_ge(m_gu, sp.snap(ended))
                    for n in range(2):
                        load_expert(sp, l, (i + 1) * SETS + k, 3 * k + n)
                    sp.wait_ge(m_d1, sp.snap(ended))
                    load_expert(sp, l, (i + 1) * SETS + k, 3 * k + 2)

                with sp.Fori(0, N_EXPERTS // SETS - 1) as i:
                    for k in range(SETS):
                        refill(i, k)
                for k in range(N_EXPERTS % SETS):
                    refill(N_EXPERTS // SETS - 1, k)
                sp.free_register(ended)

            @block.tensor
            def _(pe):
                def gather(J):
                    pe.wait_ge(m_sel, J)
                    for t in range(NT):
                        for g in range(4):
                            ins = pe.matmul(bank_a[32 * g:32 * g + 32, 0:256], sel[:, t],
                                            XN[:, t].rearrange("p (f c) -> p c f", c=KC)[:, 2 * g:2 * g + 2],
                                            start=(t == 0), stop=(t == NT - 1))
                    ins.then_inc(m_gathered, 1)

                def turn(J):
                    pe.wait_ge(m_rows, J)
                    for h in range(2):
                        ins = pe.transpose(bank_a[:, 256 + h * P:256 + (h + 1) * P], rows[:, h * P:(h + 1) * P], ident)
                    ins.then_inc(m_turned, 1)

                def scatter(J):
                    pe.wait_ge(m_selwT, J)
                    for n, s in ((0, m_y0), (1, m_y1)):
                        pe.wait_ge(s, J)
                        for t in range(NT):
                            pe.matmul(ps[2 * t + n][:, :], selwT[:, t], ymoe[:, n * 512:(n + 1) * 512], start=False, stop=True,
                                      skip_group_check=True)

                def job(J, i, k, r):
                    pe.wait_ge(m_xg, J)
                    landing = i * 16 + 16 if isinstance(i, int) else pe.snap(i * 16 + 16)
                    pe.wait_ge(m_land[3 * k], landing)
                    pe.wait_ge(m_land[3 * k + 1], landing)
                    for kk in range(4):
                        for g in range(4):
                            c = 4 * (g % 2) + kk
                            w = (wg if g < 2 else wu)[k].rearrange("p (c n) -> p c n", c=KC)
                            ins = pe.matmul(bank_b[32 * g:32 * g + 32, :], xg[:, c], w[:, c], start=(kk == 0), stop=(kk == 3))
                    ins.then_inc(m_gu, 1)
                    pe.wait_ge(m_y1, J)
                    gather(pe.snap(J + 1))
                    pe.wait_ge(m_p, J)
                    pe.wait_ge(m_selwT, J)
                    for c in range(4):
                        ins = pe.matmul(bank_c[:, c * 64:(c + 1) * 64], gu.rearrange("p (f c) -> p c f", c=4)[:, c],
                                        cst[:, K_FOLD:K_FOLD + 64], start=True, stop=True)
                    ins.then_inc(m_fold, 1)
                    turn(pe.snap(J + 1))
                    scatter(J)
                    pe.wait_ge(m_hid, J)
                    pe.wait_ge(m_land[3 * k + 2], landing)
                    w = wd[k].rearrange("p (c n) -> p c n", c=4)
                    for n, bank, s in ((0, bank_d, m_d0), (1, bank_a, m_d1)):
                        for g in range(4):
                            ins = pe.matmul(bank[32 * g:32 * g + 32, :], hid[:, g], w[:, g, n * 512:(n + 1) * 512], start=True, stop=True)
                        ins.then_inc(s, 1)
                    for t in range(NT):
                        ins = pe.transpose(bank_c[:, 256 + t * P:256 + (t + 1) * P], selw[:, t].rearrange("p g s -> p (g s)"), ident)
                    ins.then_inc(m_tw, 1)

                gather(1)
                pe.wait_ge(m_jobs, 1)
                for n in range(2):
                    ins = pe.transpose(bank_c[0:1, 256 + n * P:256 + (n + 1) * P], jf[:, n:n + 1], ident)
                ins.then_inc(m_jobs_turned, 1)
                turn(1)
                jobs(pe, job)
                pe.wait_ge(m_end, 1)
                scatter_last = [(m, n) for n in range(2) for m in range(NT)]
                for t, n in scatter_last:
                    ins = pe.matmul(ps[2 * t + n][:, :], selwT[:, t], ymoe[:, n * 512:(n + 1) * 512], start=False, stop=True,
                                    skip_group_check=True)
                ins.then_inc(m_scattered, 1)

            @block.scalar
            def _(act):
                def job(J, i, k, r):
                    act.wait_ge(m_gu, J)
                    act.activation(gu, bank_b[:, :], ACT.Copy).then_inc(m_p, 1)
                    act.wait_ge(m_fold, J)
                    act.activation(sg, bank_c[:, 0:256].rearrange("p (c x s) -> p c x s", c=4, x=2)[:, :, 0], ACT.Silu).then_inc(m_sg, 1)
                    act.wait_ge(m_d0, J)
                    act.activation(ymoe[:, 0:512], bank_d[:, :], ACT.Copy).then_inc(m_y0, 1)
                jobs(act, job)
                act.wait_ge(m_scattered, 1)
                for t in range(NT):
                    act.activation(X[:, t, 0:512], ps[2 * t][:, :], ACT.Copy)

            @block.vector
            def _(v):
                def select(e, r):
                    for t in range(NT):
                        ins = v.tensor_scalar(sel[:, t], cst[:, bass.ds(r * CAP + K_IOTA, CAP)], posn[:, t, bass.ds(e, 1)], None, ALU.is_equal)
                    ins.then_inc(m_sel, 1)

                def gained(J):
                    v.wait_ge(m_gathered, J)
                    v.tensor_copy(rows, bank_a[:, 0:256]).then_inc(m_rows, 1)
                    v.wait_ge(m_turned, J)
                    v.tensor_tensor(xg.rearrange("p (g h) s -> p h g s", h=2), bank_a[:, 256:512].rearrange("p (h g s) -> p h g s", h=2, g=4),
                                    bcast(g_ffn.rearrange("p (g h) -> p h g", h=2).unsqueeze(3), [P, 2, 4, CAP]),
                                    ALU.mult).then_inc(m_xg, 1)

                select(0, 0)
                index = cst[:, K_INDEX:K_INDEX + 1]
                link = chain(v, m_chain)
                link(v.tensor_tensor_scan(jend, cst[:, K_ONES:K_ONES + N_EXPERTS], nbf, 0.0, ALU.mult, ALU.add))
                v.tensor_scalar(jcmp[:, 0], jend, index, None, ALU.is_le)
                link(v.tensor_tensor(jstart, jend, nbf, ALU.subtract))
                link(v.scalar_tensor_tensor(jcmp[:, 1], jstart, index, jstart, ALU.is_le, ALU.mult))
                link(v.tensor_reduce(jf[:, 0:1], jcmp[:, 0], AX.X, ALU.add))
                v.tensor_scalar(jf[:, 0:1], jf[:, 0:1], float(N_EXPERTS - 1), None, ALU.min)
                link(v.tensor_reduce(jf[:, 1:2], jcmp[:, 1], AX.X, ALU.max))
                link(v.tensor_tensor(jf[:, 1:2], index, jf[:, 1:2], ALU.subtract))
                v.tensor_scalar(jf[:, 1:2], jf[:, 1:2], float(ROUNDS - 1), None, ALU.min).then_inc(m_jobs, 1)
                gained(1)
                v.wait_ge(m_jobs_turned, 1)
                link(v.tensor_copy(jobtab[0:1], bank_c[0:1, 256:512].rearrange("p (a j) -> p a j", a=2)[:, :, 0:JOBS]))

                def job(J, i, k, r):
                    e = i * SETS + k
                    for t in range(NT):
                        v.tensor_scalar(selw[:, t], bcast(cst[:, bass.ds(r * CAP + K_IOTA, CAP)].unsqueeze(1), [P, 4, CAP]),
                                        posn[:, t, bass.ds(e, 1)], weight[:, t, bass.ds(e, 1)], ALU.is_equal, ALU.mult)
                    e_next = v.value_load(jobtab[0:1, 0, bass.ds(J, 1)], min_val=0, max_val=N_EXPERTS - 1)
                    r_next = v.value_load(jobtab[0:1, 1, bass.ds(J, 1)], min_val=0, max_val=ROUNDS - 1)
                    select(e_next, r_next)
                    gained(v.snap(J + 1))
                    v.wait_ge(m_sg, J)
                    v.tensor_tensor(hid, bank_c[:, 0:256].rearrange("p (c x s) -> p c x s", c=4, x=2)[:, :, 1], sg, ALU.mult).then_inc(m_hid, 1)
                    v.wait_ge(m_d1, J)
                    v.tensor_copy(ymoe[:, 512:1024], bank_a[:, :]).then_inc(m_y1, 1)
                    v.wait_ge(m_tw, J)
                    v.tensor_copy(selwT.rearrange("p t q -> p (t q)"), bank_c[:, 256:512]).then_inc(m_selwT, 1)
                    v.wait_ge(m_y0, v.snap(J + 1))
                jobs(v, job)
                v.drain().then_inc(m_end, 1)
                v.wait_ge(m_scattered, 1)
                for t in range(NT):
                    v.tensor_copy(X[:, t, 512:1024], ps[2 * t + 1][:, :])


    z_sq, z_asked, z_root, z_w, z_out, z_y = (top.enter_context(nc.semaphore("z_" + n)) for n in ("squares", "root_asked", "root", "gain", "stored", "y"))
    with nc.Block() as block:
        @block.sync
        def _(sp):
            sp.dma_start(fw, final_norm_w.rearrange("(o d) -> o d", o=1).broadcast_to([P, D_MODEL])).then_inc(z_w, 16)
            for t in range(NT):
                sp.wait_ge(z_y, t + 1)
                sp.dma_start(out[0, t * P:(t + 1) * P, :], fin[:, t]).then_inc(z_out, 16)
            sp.wait_ge(z_out, 16 * NT)

        @block.gpsimd
        def _(pool):
            roots(pool, z_asked, z_root, [rstd])

        @block.scalar
        def _(act):
            norm_act(act, z_sq)

        @block.vector
        def _(v):
            ask, got = root_asker(v, z_asked, z_root)
            v.wait_ge(z_sq, NT)
            ask(v.tensor_scalar(rstd, ss, 1.0 / D_MODEL, EPS, ALU.mult, ALU.add))
            got()
            v.wait_ge(z_w, 16)
            for t in range(NT):
                v.scalar_tensor_tensor(fin[:, t], X[:, t], rstd[:, t:t + 1], fw, ALU.mult, ALU.mult).then_inc(z_y, 1)
    top.close()


_INS = ['x', 'attn_norm_w', 'w_in', 'gdn_conv_w', 'gdn_a_log', 'gdn_dt_bias', 'gdn_norm_w', 'diff_lambda', 'diff_norm_w',
        'gqa_q_norm_w', 'gqa_k_norm_w', 'w_branch_a', 'w_branch_b', 'w_branch_c', 'w_out', 'ffn_norm_w', 'router_group_w',
        'router_group_b', 'router_expert_w', 'router_expert_b', 'expert_w_gate', 'expert_w_up', 'expert_w_down',
        'final_norm_w']
_OUTS = [((1, SEQ, D_MODEL), 'float32')]


def kernel(**inputs):
    import numpy as _np
    import concourse.bacc as _bacc
    from concourse import mybir as _mybir
    from concourse.bass_utils import run_bass_kernel_spmd as _run

    nc = _bacc.Bacc("TRN2", target_bir_lowering=False, num_devices=1)
    arrays, args = {}, []
    for name in _INS:
        a = _np.ascontiguousarray(inputs[name])
        arrays[f"in_{name}_dram"] = a
        args.append(nc.dram_tensor(f"in_{name}_dram", a.shape, _mybir.dt.from_np(a.dtype), kind="ExternalInput").ap())
    c = shape_constants()
    arrays["consts_dram"] = c
    args.append(nc.dram_tensor("consts_dram", c.shape, _mybir.dt.from_np(c.dtype), kind="ExternalInput").ap())
    for i, (shape, dtype) in enumerate(_OUTS):
        dt = _mybir.dt.from_np(_np.dtype(dtype))
        args.append(nc.dram_tensor(f"out_{i}_dram", shape, dt, kind="ExternalOutput").ap())
    encoder_trunk(nc, *args)
    r = _run(nc, [arrays], core_ids=[0])
    got = tuple(r.results[0][f"out_{i}_dram"] for i in range(len(_OUTS)))
    return got[0]
```
